# Optimizing a Trainium2 kernel written in Bass

```python
import jax
import jax.numpy as jnp
from jax import lax
import numpy as np

D_MODEL = 1024
BATCH = 1
SEQ = 512
DEPTH = 2

CTX_LEN = 256
GRID_W = 64
HEAD_DIM = 64
D_MIX = D_MODEL
GROUP_W = D_MIX // 4
Q_BLOCK = 128
ROPE_THETA = 10000.0
NORM_EPS = 1e-6
D_FF = 2816

MLA_HEADS = 4
MLA_Q_RANK = 256
MLA_KV_RANK = 128
MLA_NOPE = 64
MLA_ROPE = 32
MLA_V = 64
RWKV_HEADS = 4
RWKV_N = 64
RWKV_W_LORA = 32
RWKV_A_LORA = 32
RWKV_G_LORA = 64
RWKV_LNX_EPS = 64e-5
NA_HEADS = 4
NA_WIN_R = 8
NA_WIN_C = 16
GQA_Q_HEADS = 4
GQA_KV_HEADS = 2

MLA_COLS = MLA_Q_RANK + MLA_KV_RANK + MLA_ROPE
RWKV_COLS = 3 * GROUP_W + 2 * RWKV_W_LORA + 2 * RWKV_A_LORA + RWKV_G_LORA
NA_COLS = 3 * GROUP_W
GQA_COLS = (GQA_Q_HEADS + 2 * GQA_KV_HEADS) * HEAD_DIM
N_IN_COLS = MLA_COLS + RWKV_COLS + NA_COLS + GQA_COLS
MIX_SPLITS = [MLA_COLS, MLA_COLS + RWKV_COLS, MLA_COLS + RWKV_COLS + NA_COLS]
RWKV_SPLITS = [GROUP_W, 2 * GROUP_W, 3 * GROUP_W,
               3 * GROUP_W + RWKV_W_LORA, 3 * GROUP_W + 2 * RWKV_W_LORA,
               3 * GROUP_W + 2 * RWKV_W_LORA + RWKV_A_LORA,
               3 * GROUP_W + 2 * RWKV_W_LORA + 2 * RWKV_A_LORA]

kernel_name = 'hybrid_parallel_group_diffusion_trunk'

def rms_norm(x, gain):
    xf = x.astype(jnp.float32)
    y = xf * lax.rsqrt(jnp.mean(xf * xf, axis=-1, keepdims=True) + NORM_EPS)
    return (y * gain.astype(jnp.float32)).astype(x.dtype)

def modulate(x, shift, scale):
    return x * (1 + scale) + shift

def swiglu(h, w_gu, w_down):
    gate, up = jnp.split(h @ w_gu, 2, axis=-1)
    return (jax.nn.silu(gate) * up) @ w_down

def rope_axis(x, pos):
    half = x.shape[-1] // 2
    inv_freq = ROPE_THETA ** (-jnp.arange(half, dtype=jnp.float32) / half)
    ang = pos.astype(jnp.float32)[:, None] * inv_freq[None, :]
    cos = jnp.cos(ang)[:, None, :].astype(x.dtype)
    sin = jnp.sin(ang)[:, None, :].astype(x.dtype)
    x1, x2 = x[..., :half], x[..., half:]
    return jnp.concatenate([x1 * cos - x2 * sin, x1 * sin + x2 * cos], axis=-1)

def rope_2d(x, row, col):
    a = x.shape[-1] // 2
    return jnp.concatenate([rope_axis(x[..., :a], row), rope_axis(x[..., a:], col)], axis=-1)

def blocked_attention(q, k, v, scale):
    B, S, H, dq = q.shape
    Hk, dv = k.shape[2], v.shape[-1]
    G = H // Hk
    nb = S // Q_BLOCK
    qb = q.reshape(B, nb, Q_BLOCK, Hk, G, dq).transpose(1, 0, 2, 3, 4, 5)

    def one_block(q_blk):
        s = jnp.einsum('bqkgd,btkd->bkgqt', q_blk, k, preferred_element_type=jnp.float32) * scale
        p = jax.nn.softmax(s, axis=-1).astype(v.dtype)
        return jnp.einsum('bkgqt,btkd->bqkgd', p, v)

    o = lax.map(one_block, qb)
    return o.transpose(1, 0, 2, 3, 4, 5).reshape(B, S, H, dv)

def neighbourhood_attention(q, k, v, k_ctx, v_ctx, rpb, scale):
    B, S, H, dh = q.shape
    rows = S // GRID_W
    win_r = min(NA_WIN_R, rows)
    n_nb = win_r * NA_WIN_C
    qg = q.reshape(B, rows, GRID_W, H, dh).transpose(1, 0, 2, 3, 4)
    kg = k.reshape(B, rows, GRID_W, H, dh)
    vg = v.reshape(B, rows, GRID_W, H, dh)
    cols = jnp.arange(GRID_W)
    c0 = jnp.clip(cols - NA_WIN_C // 2, 0, GRID_W - NA_WIN_C)
    col_idx = c0[:, None] + jnp.arange(NA_WIN_C)[None, :]
    dc_idx = col_idx - cols[:, None] + NA_WIN_C - 1

    def one_row(args):
        r, q_row = args
        r0 = jnp.clip(r - win_r // 2, 0, rows - win_r)
        k_nb = lax.dynamic_slice_in_dim(kg, r0, win_r, axis=1)[:, :, col_idx]
        v_nb = lax.dynamic_slice_in_dim(vg, r0, win_r, axis=1)[:, :, col_idx]
        dr_idx = r0 + jnp.arange(win_r) - r + NA_WIN_R - 1
        bias = rpb[:, dr_idx[:, None, None], dc_idx[None, :, :]].transpose(0, 2, 1, 3)
        s_nb = jnp.einsum('bchd,bicjhd->bhcij', q_row, k_nb,
                          preferred_element_type=jnp.float32) * scale + bias.astype(jnp.float32)
        s_ctx = jnp.einsum('bchd,blhd->bhcl', q_row, k_ctx, preferred_element_type=jnp.float32) * scale
        p = jax.nn.softmax(jnp.concatenate([s_nb.reshape(B, H, GRID_W, n_nb), s_ctx], axis=-1),
                           axis=-1).astype(v.dtype)
        p_nb = p[..., :n_nb].reshape(B, H, GRID_W, win_r, NA_WIN_C)
        return (jnp.einsum('bhcij,bicjhd->bchd', p_nb, v_nb)
                + jnp.einsum('bhcl,blhd->bchd', p[..., n_nb:], v_ctx))

    o = lax.map(one_row, (jnp.arange(rows), qg))
    return o.transpose(1, 0, 2, 3, 4).reshape(B, S, H, dh)

def mla_mixer(u, uc, row, col, q_norm, kv_norm, w_uq, w_ukv, qn, kn, with_ctx_out):
    def project(t, pos):
        B, T, _ = t.shape
        q_c, kv_c, k_r = jnp.split(t, [MLA_Q_RANK, MLA_Q_RANK + MLA_KV_RANK], axis=-1)
        q = (rms_norm(q_c, q_norm) @ w_uq).reshape(B, T, MLA_HEADS, MLA_NOPE + MLA_ROPE)
        kv = (rms_norm(kv_c, kv_norm) @ w_ukv).reshape(B, T, MLA_HEADS, MLA_NOPE + MLA_V)
        k_rope = jnp.broadcast_to(k_r[:, :, None, :], (B, T, MLA_HEADS, MLA_ROPE))
        k = jnp.concatenate([kv[..., :MLA_NOPE], k_rope], axis=-1)
        v = kv[..., MLA_NOPE:]
        q, k = rms_norm(q, qn), rms_norm(k, kn)
        if pos is not None:
            q = jnp.concatenate([q[..., :MLA_NOPE], rope_2d(q[..., MLA_NOPE:], *pos)], axis=-1)
            k = jnp.concatenate([k[..., :MLA_NOPE], rope_2d(k[..., MLA_NOPE:], *pos)], axis=-1)
        return q, k, v

    B, S, _ = u.shape
    scale = (MLA_NOPE + MLA_ROPE) ** -0.5
    q, k, v = project(u, (row, col))
    qc, kc, vc = project(uc, None)
    o = blocked_attention(q, jnp.concatenate([kc, k], axis=1), jnp.concatenate([vc, v], axis=1), scale)
    o_ctx = blocked_attention(qc, kc, vc, scale).reshape(B, -1, GROUP_W) if with_ctx_out else None
    return o.reshape(B, S, GROUP_W), o_ctx

def token_shift(t, mu):
    prev = jnp.pad(t, ((0, 0), (1, 0), (0, 0)))[:, :-1]
    nxt = jnp.pad(t, ((0, 0), (0, 1), (0, 0)))[:, 1:]
    return t + mu[0] * (prev - t) + mu[1] * (nxt - t)

def rwkv_features(t, shift, w0, w2, a0, a2, g2, k_k, k_a):
    B, T, _ = t.shape
    t = token_shift(t, shift).astype(jnp.float32)
    r, k, v, wd_f, wd_b, ad_f, ad_b, gd = jnp.split(t, RWKV_SPLITS, axis=-1)
    heads = lambda z: z.reshape(B, T, RWKV_HEADS, RWKV_N)
    kk = heads(k * k_k)
    kk = kk * lax.rsqrt(jnp.sum(kk * kk, axis=-1, keepdims=True) + 1e-12)
    g = jax.nn.sigmoid(gd) @ g2
    dirs = []
    for d, (wd, ad) in enumerate(((wd_f, ad_f), (wd_b, ad_b))):
        w_log = -jax.nn.softplus(-(w0[d] + jnp.tanh(wd) @ w2[d])) - 0.5
        decay = jnp.exp(-jnp.exp(w_log))
        a = jax.nn.sigmoid(a0[d] + ad @ a2[d])
        kd = k * (1 + (a - 1) * k_a)
        dirs.append((heads(decay), heads(kd), heads(a)))
    return heads(r), heads(v), kk, g, dirs

def wkv_scan(state0, r, w, k, v, kk, a, reverse):
    xs = tuple(jnp.moveaxis(z, 1, 0) for z in (r, w, k, v, kk, a))

    def step(S, inp):
        r_t, w_t, k_t, v_t, kk_t, a_t = inp
        sa = jnp.einsum('bhij,bhj->bhi', S, kk_t)
        S = (S * w_t[:, :, None, :] - sa[..., None] * (kk_t * a_t)[:, :, None, :]
             + v_t[..., None] * k_t[:, :, None, :])
        return S, jnp.einsum('bhij,bhj->bhi', S, r_t)

    s_final, ys = lax.scan(step, state0, xs, reverse=reverse)
    return s_final, jnp.moveaxis(ys, 0, 1)

def head_group_norm(y, gain, bias):
    B, T, H, N = y.shape
    mu = jnp.mean(y, axis=-1, keepdims=True)
    var = jnp.mean(jnp.square(y - mu), axis=-1, keepdims=True)
    return ((y - mu) * lax.rsqrt(var + RWKV_LNX_EPS)).reshape(B, T, H * N) * gain + bias

def rwkv_mixer(u, uc, shift, w0, w2, a0, a2, g2, k_k, k_a, r_k, lnx_g, lnx_b, with_ctx_out):
    B, S, _ = u.shape
    r, v, kk, g, dirs = rwkv_features(u, shift, w0, w2, a0, a2, g2, k_k, k_a)
    rc, vc, kkc, gc, dirs_c = rwkv_features(uc, shift, w0, w2, a0, a2, g2, k_k, k_a)
    ys, ys_c, bon, bon_c = [], [], [], []
    for (dec, kd, a), (dec_c, kd_c, a_c), rev in zip(dirs, dirs_c, (False, True)):
        s0 = jnp.zeros((B, RWKV_HEADS, RWKV_N, RWKV_N), jnp.float32)
        s_ctx, y_c = wkv_scan(s0, rc, dec_c, kd_c, vc, kkc, a_c, rev)
        _, y = wkv_scan(s_ctx, r, dec, kd, v, kk, a, rev)
        ys.append(y)
        ys_c.append(y_c)
        bon.append(jnp.sum(r * kd * r_k, axis=-1, keepdims=True) * v)
        bon_c.append(jnp.sum(rc * kd_c * r_k, axis=-1, keepdims=True) * vc)
    o = (head_group_norm(ys[0] + ys[1], lnx_g, lnx_b) + (bon[0] + bon[1]).reshape(B, S, GROUP_W)) * g
    o_ctx = None
    if with_ctx_out:
        o_ctx = ((head_group_norm(ys_c[0] + ys_c[1], lnx_g, lnx_b)
                  + (bon_c[0] + bon_c[1]).reshape(B, -1, GROUP_W)) * gc).astype(uc.dtype)
    return o.astype(u.dtype), o_ctx

def na_mixer(u, uc, qn, kn, rpb, with_ctx_out):
    def heads(t):
        B, T, _ = t.shape
        q, k, v = (z.reshape(B, T, NA_HEADS, HEAD_DIM) for z in jnp.split(t, 3, axis=-1))
        return rms_norm(q, qn), rms_norm(k, kn), v

    B, S, _ = u.shape
    scale = HEAD_DIM ** -0.5
    q, k, v = heads(u)
    qc, kc, vc = heads(uc)
    o = neighbourhood_attention(q, k, v, kc, vc, rpb, scale)
    o_ctx = blocked_attention(qc, kc, vc, scale).reshape(B, -1, GROUP_W) if with_ctx_out else None
    return o.reshape(B, S, GROUP_W), o_ctx

def gqa_mixer(u, uc, row, col, qn, kn, with_ctx_out):
    def heads(t, pos):
        B, T, _ = t.shape
        q, k, v = jnp.split(t, [GQA_Q_HEADS * HEAD_DIM, (GQA_Q_HEADS + GQA_KV_HEADS) * HEAD_DIM], axis=-1)
        q = rms_norm(q.reshape(B, T, GQA_Q_HEADS, HEAD_DIM), qn)
        k = rms_norm(k.reshape(B, T, GQA_KV_HEADS, HEAD_DIM), kn)
        v = v.reshape(B, T, GQA_KV_HEADS, HEAD_DIM)
        if pos is not None:
            q, k = rope_2d(q, *pos), rope_2d(k, *pos)
        return q, k, v

    B, S, _ = u.shape
    scale = HEAD_DIM ** -0.5
    q, k, v = heads(u, (row, col))
    qc, kc, vc = heads(uc, None)
    o = blocked_attention(q, jnp.concatenate([kc, k], axis=1), jnp.concatenate([vc, v], axis=1), scale)
    o_ctx = blocked_attention(qc, kc, vc, scale).reshape(B, -1, GROUP_W) if with_ctx_out else None
    return o.reshape(B, S, GROUP_W), o_ctx

def setup_inputs(seed: int = 0) -> dict:
    key = jax.random.key(seed)
    ks = iter(jax.random.split(key, 64))
    nrm = lambda shape, s: jax.random.normal(next(ks), shape, jnp.float32) * s
    gain = lambda shape: 1.0 + nrm(shape, 0.1)
    L, D = DEPTH, D_MODEL
    return {
        'x': nrm((BATCH, SEQ, D), 1.0),
        'c': nrm((BATCH, D), 1.0),
        'ctx': nrm((BATCH, CTX_LEN, D), 1.0),
        'c_ctx': nrm((D,), 1.0),
        'w_mod': nrm((L, D, 9 * D), 0.5 * D ** -0.5),
        'b_mod': nrm((L, 9 * D), 0.02),
        'norm_ffn1': gain((L, D)),
        'ffn1_w_gu': nrm((L, D, 2 * D_FF), D ** -0.5),
        'ffn1_w_down': nrm((L, D_FF, D), D_FF ** -0.5),
        'norm_mix': gain((L, D)),
        'w_in': nrm((L, D, N_IN_COLS), D ** -0.5),
        'w_out': nrm((L, D_MIX, D), D_MIX ** -0.5),
        'mla_q_norm': gain((L, MLA_Q_RANK)),
        'mla_kv_norm': gain((L, MLA_KV_RANK)),
        'mla_w_uq': nrm((L, MLA_Q_RANK, MLA_HEADS * (MLA_NOPE + MLA_ROPE)), MLA_Q_RANK ** -0.5),
        'mla_w_ukv': nrm((L, MLA_KV_RANK, MLA_HEADS * (MLA_NOPE + MLA_V)), MLA_KV_RANK ** -0.5),
        'mla_qn': gain((L, MLA_NOPE + MLA_ROPE)),
        'mla_kn': gain((L, MLA_NOPE + MLA_ROPE)),
        'rwkv_shift': jax.random.uniform(next(ks), (L, 2, RWKV_COLS), jnp.float32, 0.0, 0.5),
        'rwkv_w0': jax.random.uniform(next(ks), (L, 2, GROUP_W), jnp.float32, -4.0, 1.0),
        'rwkv_w2': nrm((L, 2, RWKV_W_LORA, GROUP_W), 0.5 * RWKV_W_LORA ** -0.5),
        'rwkv_a0': nrm((L, 2, GROUP_W), 0.5),
        'rwkv_a2': nrm((L, 2, RWKV_A_LORA, GROUP_W), 0.5 * RWKV_A_LORA ** -0.5),
        'rwkv_g2': nrm((L, RWKV_G_LORA, GROUP_W), RWKV_G_LORA ** -0.5),
        'rwkv_k_k': 0.85 + nrm((L, GROUP_W), 0.1),
        'rwkv_k_a': 1.0 + nrm((L, GROUP_W), 0.1),
        'rwkv_r_k': nrm((L, RWKV_HEADS, RWKV_N), 0.1),
        'rwkv_lnx_g': gain((L, GROUP_W)),
        'rwkv_lnx_b': nrm((L, GROUP_W), 0.02),
        'na_qn': gain((L, HEAD_DIM)),
        'na_kn': gain((L, HEAD_DIM)),
        'na_rpb': nrm((L, NA_HEADS, 2 * NA_WIN_R - 1, 2 * NA_WIN_C - 1), 0.5),
        'gqa_qn': gain((L, HEAD_DIM)),
        'gqa_kn': gain((L, HEAD_DIM)),
        'norm_ffn2': gain((L, D)),
        'ffn2_w_gu': nrm((L, D, 2 * D_FF), D ** -0.5),
        'ffn2_w_down': nrm((L, D_FF, D), D_FF ** -0.5),
    }

def reference(x, c, ctx, c_ctx, w_mod, b_mod, norm_ffn1, ffn1_w_gu, ffn1_w_down, norm_mix, w_in, w_out,
              mla_q_norm, mla_kv_norm, mla_w_uq, mla_w_ukv, mla_qn, mla_kn,
              rwkv_shift, rwkv_w0, rwkv_w2, rwkv_a0, rwkv_a2, rwkv_g2, rwkv_k_k, rwkv_k_a, rwkv_r_k,
              rwkv_lnx_g, rwkv_lnx_b, na_qn, na_kn, na_rpb, gqa_qn, gqa_kn,
              norm_ffn2, ffn2_w_gu, ffn2_w_down):
    S = x.shape[1]
    t = jnp.arange(S)
    row, col = t // GRID_W, t % GRID_W
    h, hc = x, ctx
    for l in range(DEPTH):
        ctx_needed = l < DEPTH - 1
        m = jnp.split((jax.nn.silu(c) @ w_mod[l] + b_mod[l])[:, None, :], 9, axis=-1)
        mc = jnp.split(jax.nn.silu(c_ctx) @ w_mod[l] + b_mod[l], 9, axis=-1)

        h = h + 0.5 * m[2] * swiglu(modulate(rms_norm(h, norm_ffn1[l]), m[0], m[1]), ffn1_w_gu[l], ffn1_w_down[l])
        hc = hc + 0.5 * mc[2] * swiglu(modulate(rms_norm(hc, norm_ffn1[l]), mc[0], mc[1]),
                                       ffn1_w_gu[l], ffn1_w_down[l])

        u = modulate(rms_norm(h, norm_mix[l]), m[3], m[4]) @ w_in[l]
        uc = modulate(rms_norm(hc, norm_mix[l]), mc[3], mc[4]) @ w_in[l]
        ua, ub, ucn, ud = jnp.split(u, MIX_SPLITS, axis=-1)
        uca, ucb, uccn, ucd = jnp.split(uc, MIX_SPLITS, axis=-1)
        oa, oca = mla_mixer(ua, uca, row, col, mla_q_norm[l], mla_kv_norm[l], mla_w_uq[l], mla_w_ukv[l],
                            mla_qn[l], mla_kn[l], ctx_needed)
        ob, ocb = rwkv_mixer(ub, ucb, rwkv_shift[l], rwkv_w0[l], rwkv_w2[l], rwkv_a0[l], rwkv_a2[l],
                             rwkv_g2[l], rwkv_k_k[l], rwkv_k_a[l], rwkv_r_k[l], rwkv_lnx_g[l], rwkv_lnx_b[l],
                             ctx_needed)
        on, ocn = na_mixer(ucn, uccn, na_qn[l], na_kn[l], na_rpb[l], ctx_needed)
        od, ocd = gqa_mixer(ud, ucd, row, col, gqa_qn[l], gqa_kn[l], ctx_needed)
        mix = jnp.concatenate([oa, ob, on, od], axis=-1).astype(h.dtype) @ w_out[l]
        h = h + m[5] * mix
        if ctx_needed:
            mix_c = jnp.concatenate([oca, ocb, ocn, ocd], axis=-1).astype(hc.dtype) @ w_out[l]
            hc = hc + mc[5] * mix_c

        h = h + 0.5 * m[8] * swiglu(modulate(rms_norm(h, norm_ffn2[l]), m[6], m[7]), ffn2_w_gu[l], ffn2_w_down[l])
        if ctx_needed:
            hc = hc + 0.5 * mc[8] * swiglu(modulate(rms_norm(hc, norm_ffn2[l]), mc[6], mc[7]),
                                           ffn2_w_gu[l], ffn2_w_down[l])
    return h


_drawn_inputs = setup_inputs


def setup_inputs(seed=0):
    import zlib

    import numpy as np

    out = dict(_drawn_inputs(seed))
    spreads = {}
    factors = {'mla_q_norm': 8.0,
     'mla_kv_norm': 8.0,
     'mla_w_uq': 2.827,
     'mla_qn': 8.0,
     'mla_kn': 8.0,
     'rwkv_w2': 6.679,
     'rwkv_a2': 3.053,
     'rwkv_k_k': 3.868,
     'rwkv_k_a': 2.691,
     'rwkv_lnx_g': 5.172,
     'rwkv_lnx_b': 8.0,
     'na_qn': 8.0,
     'na_kn': 8.0,
     'na_rpb': 8.0,
     'gqa_qn': 8.0,
     'gqa_kn': 8.0,
     'norm_ffn2': 2.775}
    for name, (base, spread) in spreads.items():
        noise = np.random.default_rng([zlib.crc32(name.encode()), seed]).standard_normal(out[name].shape)
        drawn = base * np.exp(spread * noise) if base else spread * noise
        out[name] = jnp.asarray(drawn.astype(out[name].dtype))
    for name, factor in factors.items():
        out[name] = (out[name] * factor).astype(out[name].dtype)
    return out
```

```python
from contextlib import ExitStack

import numpy as np
import concourse.bass as bass
from concourse import mybir

F32 = mybir.dt.float32
F32R = mybir.dt.float32r
ACT = mybir.ActivationFunctionType
ALU = mybir.AluOpType
AXX = mybir.AxisListType.X

P = 128
D_MODEL, SEQ, CTX, DEPTH, D_FF = 1024, 512, 256, 2, 2816
GRID_W, HEAD = 64, 64
KD = D_MODEL // P
NT = SEQ + CTX
LAT, CTXT = slice(0, SEQ), slice(SEQ, NT)
NF = D_FF // P
NFH = NF // 2
NTT = NT // P
LT_TILES = SEQ // P
N_MOD = 9 * KD
N_IN = 22
MLA_D, MLA_NOPE, MLA_ROPE = 96, 64, 32
CH = 64
NCH = NT // CH
G_DECAY = float(np.exp(-0.5))
MASKED = -1e30

U_QC, U_KV, U_KR, U_RW, U_WA, U_GD, U_NQ, U_NK, U_GQ, U_GK = 0, 2, 3, 4, 10, 11, 12, 14, 16, 18
U_TILES = 19

COLS = {}
_n = 0
for _name, _w in [("n1", 8), ("nm", 8), ("n2", 8), ("bmod", 72), ("mq", 2), ("mkv", 1), ("mu0", 8), ("mu1", 8),
                  ("w0", 4), ("a0", 4), ("kk", 2), ("ka", 2), ("rk", 2), ("lg", 2), ("lb", 2), ("nq", 1),
                  ("nk", 1), ("gq", 1), ("gk", 1), ("mqn", 1), ("mkn", 1)]:
    COLS[_name] = (_n, _n + _w)
    _n += _w
NCOL = _n
CONSTS = ["ident", "ones", "ones64", "rot_g", "rot_m", "sel_kr", "ident2"]


class Signal:

    def __init__(self, sem, first=0):
        self.sem, self.base = sem, first

    def at(self, n):
        return self.base + n

    def phase_end(self, n):
        self.base += n


def build_trunk(nc, A):
    with ExitStack() as ctx:
        start = (nc.sbuf_base + 63) // 64 * 64
        R_H = start
        R_N = R_H + KD * NT * 4
        R_G = R_N + 2 * KD * NT * 4
        R_W = R_G + 2 * NFH * NT * 4
        R_T = R_W + 6 * NFH * P * 4
        arena_size = nc.sbuf_usable_end - start
        ctx.enter_context(nc.sbuf_tensor("arena", [P, (arena_size - 64) // 4], F32))
        place = {"T": R_T}

        def at(name, shape, off, dt=F32):
            return nc.alloc_sbuf_tensor_at(name, shape, dt, offset=off)

        def tmp(name, shape, dt=F32):
            n = 4 * int(np.prod(shape[1:]))
            t = at(name, shape, place["T"], dt)
            place["T"] += (n + 31) // 32 * 32
            assert place["T"] <= start + arena_size, (name, place["T"])
            return t

        TOK = NT * 4
        h = at("h", [P, KD, NT], R_H)
        hn_hi = at("hn_hi", [P, KD, NT], R_N, F32R)
        hn_lo = at("hn_lo", [P, KD, NT], R_N + KD * TOK, F32R)
        g_hi = at("g_hi", [P, NFH, NT], R_G, F32R)
        g_lo = at("g_lo", [P, NFH, NT], R_G + NFH * TOK, F32R)
        u = at("u", [P, U_TILES, NT], R_G)
        v_nat = at("v_nat", [P, NTT, 3 * P], R_G + U_TILES * TOK)
        rstd = at("rstd", [P, NT], R_G + 2 * TOK)
        lnv = at("lnv", [P, NT], R_G + 3 * TOK)
        scaled = at("scaled", [P, 2, NT], R_G + 4 * TOK)
        moded = at("moded", [P, 2, NT], R_G + 6 * TOK)
        WS = NFH * P * 4
        raw = [at(f"raw{s}", [P, NFH * P], R_W + s * WS) for s in range(2)]
        w_hi = [at(f"w_hi{s}", [P, NFH, P], R_W + (2 + s) * WS, F32R) for s in range(2)]
        w_lo = [at(f"w_lo{s}", [P, NFH, P], R_W + (4 + s) * WS, F32R) for s in range(2)]
        const = tmp("const", [P, len(CONSTS), P])
        K_ = {n: const[:, i, :] for i, n in enumerate(CONSTS)}
        cols_all = tmp("cols", [P, DEPTH, NCOL])
        mod_all = tmp("mod", [P, DEPTH, 2, N_MOD])
        cols, mod = [cols_all[:, i, :] for i in range(DEPTH)], [mod_all[:, i, :, :] for i in range(DEPTH)]
        moda = tmp("moda", [P, 2, KD])
        small = tmp("small", [P, 16])
        c_raw = tmp("c_raw", [P, KD * 2])
        cond = tmp("cond", [P, 3, KD * 2])
        keep = tmp("keep", [P, KD])
        T0 = place["T"]
        sum_sq = tmp("sum_sq", [P, NT])
        tanh_g = tmp("tanh_g", [P, NT])
        silu_g = tmp("silu_g", [P, NT])
        glu = tmp("glu", [P, NT])
        h_sq = tmp("h_sq", [P, NT])
        MOD_SLOTS = 3
        mod_row = at("mod_row", [2, MOD_SLOTS * P], place["T"])
        place["T"] += 4 * MOD_SLOTS * P
        w_mod = [tmp(f"w_mod{i}", [P, D_MODEL]) for i in range(MOD_SLOTS)]
        MOD_FIRST = 16
        w_mod_first = at("w_mod_first", [P, MOD_FIRST, D_MODEL], R_N)
        mod_row_first = at("mod_row_first", [2, MOD_FIRST * P], R_T - MOD_FIRST * P * 4)

        ps = ctx.enter_context(nc.psum_tensor("ps", [P, 8, 512], F32))
        psf = ps[:, :, :].rearrange("p a b -> p (a b)")
        ps_slot = [psf[:, 0:NT], psf[:, 1024:1024 + NT]]

        def sem(name, first=0):
            return Signal(ctx.enter_context(nc.semaphore(name)), first)

        raw_loaded = [sem(f"raw_loaded{s}") for s in range(2)]
        hi_ready = [sem(f"w_hi_ready{s}") for s in range(2)]
        lo_ready = [sem(f"w_lo_ready{s}", 1) for s in range(2)]
        block_done = [sem(f"block_done{s}", 1) for s in range(2)]
        evacuated = [sem(f"psum_evacuated{s}", 1) for s in range(2)]
        setup_loaded = sem("setup_loaded")
        cond_step, cond_ready = sem("cond_step"), sem("cond_ready")
        mod_ready = sem("mod_ready")
        mod_loaded = [sem(f"w_mod_loaded{i}") for i in range(MOD_SLOTS)]
        mod_used = sem("w_mod_used", MOD_SLOTS)
        mod_first_ready = sem("mod_first_rows_ready")
        mod_copied, mod_turned = sem("mod_rows_copied"), sem("mod_rows_turned")
        sq_summed, h_squared = sem("h_sq_summed"), sem("h_squared")
        ms_ready, rstd_ready, ln_done = sem("ms_ready"), sem("rstd_ready"), sem("ln_done")
        scaled_ready, moded_ready, hn_hi_ready, hn_lo_ready = (sem("scaled_ready"), sem("moded_ready"),
                                                               sem("hn_hi_ready"), sem("hn_lo_ready"))
        moda_ready = sem("moda_ready")
        tanh_ready, silu_ready, glu_ready, g_hi_ready, g_lo_ready = (sem("tanh_ready"), sem("silu_ready", 1),
                                                                     sem("glu_ready", 1), sem("g_hi_ready"),
                                                                     sem("g_lo_ready"))
        stored = sem("out_stored")

        EPS, LN_Q64, LN_Q96, EPS_KK, EPS_LNX = 0, 1, 2, 3, 4
        SMALL = [1e-6, float(np.log(HEAD ** -0.5)), float(np.log(MLA_D ** -0.5)), 1e-12, 64e-5]

        def col(name, j=0, rows=slice(0, P)):
            a = COLS[name][0] + j
            return cols_all[rows, layer[0], a:a + 1]
        layer = [0]

        TWO = (("lat", LAT, 0), ("ctx", CTXT, 1))

        def load_block(sp, s, src, kt, use):
            sp.wait_ge(lo_ready[s].sem, lo_ready[s].at(use))
            sp.dma_start(raw[s][:, 0:kt * P], src).then_inc(raw_loaded[s].sem, 16)

        def split_hi(act, s, kt, use):
            act.wait_ge(raw_loaded[s].sem, 16 * use + raw_loaded[s].at(16))
            act.wait_ge(block_done[s].sem, block_done[s].at(use))
            act.activation(w_hi[s][:, 0:kt, :].rearrange("p k n -> p (k n)"), raw[s][:, 0:kt * P],
                           ACT.Copy).then_inc(hi_ready[s].sem, 1)

        def split_lo(dve, s, kt, use):
            dve.wait_ge(hi_ready[s].sem, hi_ready[s].at(use + 1))
            dve.tensor_tensor(w_lo[s][:, 0:kt, :].rearrange("p k n -> p (k n)"), raw[s][:, 0:kt * P],
                              w_hi[s][:, 0:kt, :].rearrange("p k n -> p (k n)").bitcast(F32),
                              ALU.subtract).then_inc(lo_ready[s].sem, 1)

        def stream_end(pairs):
            for s in range(2):
                raw_loaded[s].phase_end(16 * pairs)
                for x in (hi_ready[s], lo_ready[s], block_done[s]):
                    x.phase_end(pairs)

        def product(pe, s, kt, out, mov_hi, mov_lo, nt, tile_ready=None):
            spans = [(0, 512), (512, NT)] if nt == NT else [(0, 512)]
            for k in range(kt):
                if tile_ready is not None:
                    pe.wait_ge(tile_ready.sem, tile_ready.at(k + 1))
                for w, m in ((w_hi[s], mov_hi), (w_hi[s], mov_lo), (w_lo[s], mov_hi)):
                    for a, b in spans:
                        mm = pe.matmul(out[:, a:b], w[:, k, :], m[:, k, a:b],
                                       start=(k == 0 and w is w_hi[s] and m is mov_hi),
                                       stop=(k == kt - 1 and w is w_lo[s]))
            mm.then_inc(block_done[s].sem, 1)

        def mod_rows(pe, slots, use):
            for m in range(slots):
                pe.wait_ge(mod_loaded[m].sem, use(m) * 16 + mod_loaded[m].at(16))
                for k in range(KD):
                    mm = pe.matmul(ps[0:2, 4, m * P:(m + 1) * P], cond[:, 2, 2 * k:2 * k + 2],
                                   w_mod[m][:, k * P:(k + 1) * P], start=(k == 0), stop=(k == KD - 1))
                mm.then_inc(mod_used.sem, 1)

        def mod_turn(pe, slots, bank, column, copied):
            pe.wait_ge(mod_copied.sem, copied)
            for m in range(slots):
                mm = pe.matmul(ps[:, bank, bass.ds((column + m) * 2, 2)], mod_row[0:2, m * P:(m + 1) * P],
                               K_["ident"][0:2, 0:2], start=True, stop=True)
            mm.then_inc(mod_turned.sem, 1)

        def mod_copy(dve, slots, ready):
            dve.wait_ge(mod_used.sem, ready)
            dve.tensor_copy(mod_row[:, 0:slots * P], ps[0:2, 4, 0:slots * P]).then_inc(mod_copied.sem, 1)

        def mod_finish(dve, l, bank, j0, j1, n):
            a = COLS["bmod"][0]
            for w in range(2):
                dve.tensor_tensor(mod[l][:, w, j0:j1],
                                  ps[:, bank, 2 * j0:2 * j1].rearrange("p (j w) -> p w j", w=2)[:, w, :],
                                  cols[l][:, a + j0:a + j1], ALU.add).then_inc(mod_ready.sem, 1)
            n += 2
            dve.wait_ge(mod_ready.sem, mod_ready.at(n))
            for part in (2, 8):
                b0, b1 = max(j0, part * KD), min(j1, (part + 1) * KD)
                if b0 < b1:
                    v = mod[l][:, :, b0:b1]
                    dve.tensor_scalar(v, v, 0.5, None, ALU.mult).then_inc(mod_ready.sem, 1)
                    n += 1
            dve.wait_ge(mod_ready.sem, mod_ready.at(n))
            return n

        FIRST_GROUP = 4
        FIRST_LOADS = ((0, 4), (4, 8), (8, MOD_FIRST))

        def setup():
            n_setup = [0]
            with nc.Block() as block:
                @block.sync
                def _(sp):
                    sp.dma_start(c_raw[:, :], A["cT"]).then_inc(setup_loaded.sem, 16)
                    sp.dma_start(cols_all[:, :, :], A["cols"]).then_inc(setup_loaded.sem, 16)
                    for i, (a, b) in enumerate(FIRST_LOADS):
                        sp.dma_start(w_mod_first[:, a:b, :],
                                     A["wmod"][0, a:b].rearrange("j p n -> p j n")).then_inc(mod_loaded[i].sem, 16)
                    sp.wait_ge(setup_loaded.sem, 80)

                @block.gpsimd
                def _(pool):
                    for x in lo_ready + block_done + evacuated + [silu_ready, glu_ready]:
                        pool.sem_inc(x.sem, 1)
                    pool.sem_inc(mod_used.sem, MOD_SLOTS)
                    pool.wait_ge(setup_loaded.sem, 80)
                    pool.tensor_tensor(sum_sq[:, :], h[:, 0, :], h[:, 0, :], ALU.mult).then_inc(sq_summed.sem, 1)
                    for k in range(1, KD):
                        pool.tensor_tensor(h_sq[:, :], h[:, k, :], h[:, k, :], ALU.mult).then_inc(h_squared.sem, 1)
                        pool.wait_ge(h_squared.sem, k)
                        pool.wait_ge(sq_summed.sem, k)
                        pool.tensor_tensor(sum_sq[:, :], sum_sq[:, :], h_sq[:, :], ALU.add).then_inc(sq_summed.sem, 1)
                        if k < KD - 1:
                            pool.wait_ge(sq_summed.sem, k + 1)

                @block.scalar
                def _(act):
                    act.dma_start(h[:, :, :], A["xT"]).then_inc(setup_loaded.sem, 16)
                    act.dma_start(const[:, :, :], A["consts"]).then_inc(setup_loaded.sem, 16)
                    act.dma_start(small[:, :], A["small"]).then_inc(setup_loaded.sem, 16)
                    act.wait_ge(setup_loaded.sem, 80)
                    act.activation(cond[:, 0, :], c_raw[:, :], ACT.Tanh, scale=0.5).then_inc(cond_step.sem, 1)

                @block.vector
                def _(dve):
                    dve.wait_ge(cond_step.sem, 1)
                    dve.scalar_tensor_tensor(out=cond[:, 1, :], in0=cond[:, 0, :], scalar=1.0, in1=c_raw[:, :],
                                             op0=ALU.add, op1=ALU.mult).then_inc(cond_ready.sem, 1)
                    dve.wait_ge(cond_ready.sem, 1)
                    dve.tensor_scalar(cond[:, 2, :], cond[:, 1, :], 0.5, None, ALU.mult).then_inc(cond_ready.sem, 1)
                    for g in range(MOD_FIRST // FIRST_GROUP):
                        dve.wait_ge(mod_first_ready.sem, g + 1)
                        dve.tensor_copy(mod_row_first[:, g * 512:(g + 1) * 512], ps[0:2, g, :]).then_inc(mod_copied.sem, 1)
                    dve.wait_ge(mod_turned.sem, MOD_FIRST // FIRST_GROUP)
                    n_setup[0] = mod_finish(dve, 0, 5, 0, MOD_FIRST, 0)

                @block.tensor
                def _(pe):
                    pe.wait_ge(cond_ready.sem, 2)
                    for i, (a, b) in enumerate(FIRST_LOADS):
                        pe.wait_ge(mod_loaded[i].sem, 16)
                        for j in range(a, b, FIRST_GROUP):
                            for k in range(KD):
                                mm = pe.matmul(ps[0:2, j // FIRST_GROUP, :], cond[:, 2, 2 * k:2 * k + 2],
                                               w_mod_first[:, j:j + FIRST_GROUP, k * P:(k + 1) * P],
                                               start=(k == 0), stop=(k == KD - 1))
                            mm.then_inc(mod_first_ready.sem, 1)
                    for j in range(MOD_FIRST):
                        if j % FIRST_GROUP == 0:
                            pe.wait_ge(mod_copied.sem, j // FIRST_GROUP + 1)
                        mm = pe.matmul(ps[:, 5, 2 * j:2 * j + 2], mod_row_first[0:2, j * P:(j + 1) * P],
                                       K_["ident"][0:2, 0:2], start=True, stop=True)
                        if j % FIRST_GROUP == FIRST_GROUP - 1:
                            mm.then_inc(mod_turned.sem, 1)
            setup_loaded.phase_end(80)
            mod_copied.phase_end(MOD_FIRST // FIRST_GROUP)
            mod_turned.phase_end(MOD_FIRST // FIRST_GROUP)
            mod_ready.phase_end(n_setup[0])
            h_squared.phase_end(KD - 1)
            sq_summed.phase_end(KD)
            for i in range(MOD_SLOTS):
                mod_loaded[i].phase_end(16)

        def norm_act(act, nt, between):
            act.preload_act_table_set("natural_log_exp_and_others")
            act.wait_ge(ms_ready.sem, ms_ready.at(1))
            act.activation(lnv[:, 0:nt], ps_slot[1][:, 0:nt], ACT.Ln, bias=small[:, EPS:EPS + 1],
                           scale=1.0 / D_MODEL).then_inc(ln_done.sem, 1)
            act.wait_ge(ln_done.sem, ln_done.at(1))
            act.activation(rstd[:, 0:nt], lnv[:, 0:nt], ACT.Exp, scale=-0.5).then_inc(rstd_ready.sem, 1)
            between()
            for k in range(KD):
                act.wait_ge(moded_ready.sem, moded_ready.at(k + 1))
                act.activation(hn_hi[:, k, 0:nt], moded[:, k % 2, 0:nt], ACT.Copy).then_inc(hn_hi_ready.sem, 1)

        def norm_pool(pool, nt):
            pool.wait_ge(rstd_ready.sem, rstd_ready.at(1))
            for k in range(KD):
                if k >= 2:
                    pool.wait_ge(moded_ready.sem, moded_ready.at(k - 1))
                pool.tensor_tensor(scaled[:, k % 2, 0:nt], h[:, k, 0:nt], rstd[:, 0:nt],
                                   ALU.mult).then_inc(scaled_ready.sem, 1)

        def norm_pe(pe, nt):
            for a, b in ([(0, 512), (512, NT)] if nt == NT else [(0, 512)]):
                mm = pe.matmul(ps_slot[1][:, a:b], K_["ones"], sum_sq[:, a:b], start=True, stop=True)
            mm.then_inc(ms_ready.sem, 1)

        def square_residual(pool, s, tile, n, summed, first=False):
            pool.wait_ge(evacuated[s].sem, n)
            hv = h[:, bass.ds(tile, 1), :].rearrange("p a t -> p (a t)")
            if first:
                pool.tensor_tensor(sum_sq[:, :], hv, hv, ALU.mult).then_inc(sq_summed.sem, 1)
                return
            pool.wait_ge(sq_summed.sem, sq_summed.at(summed))
            pool.tensor_tensor(h_sq[:, :], hv, hv, ALU.mult).then_inc(h_squared.sem, 1)
            pool.wait_ge(h_squared.sem, h_squared.at(summed))
            pool.tensor_tensor(sum_sq[:, :], sum_sq[:, :], h_sq[:, :], ALU.add).then_inc(sq_summed.sem, 1)

        def square_residuals(pool, base):
            square_residual(pool, 0, 0, evacuated[0].at(base + 1), 0, first=True)
            square_residual(pool, 1, 1, evacuated[1].at(base + 1), 1)
            with pool.Fori(1, KD // 2) as i:
                for s in range(2):
                    square_residual(pool, s, i * 2 + s, i + evacuated[s].at(base + 1), i * 2 + s)

        def squares_end():
            sq_summed.phase_end(KD)
            h_squared.phase_end(KD - 1)

        def norm_dve(dve, nt, gain, part, between):
            a, b = COLS[gain]
            l = layer[0]
            for w in range(2):
                dve.scalar_tensor_tensor(out=moda[:, w, :], in0=mod[l][:, w, (part + 1) * KD:(part + 2) * KD],
                                         scalar=1.0, in1=cols[l][:, a:b], op0=ALU.add,
                                         op1=ALU.mult).then_inc(moda_ready.sem, 1)
            dve.wait_ge(moda_ready.sem, moda_ready.at(2))
            between()

            def lo(k):
                dve.wait_ge(hn_hi_ready.sem, hn_hi_ready.at(k + 1))
                dve.tensor_tensor(hn_lo[:, k, 0:nt], moded[:, k % 2, 0:nt], hn_hi[:, k, 0:nt].bitcast(F32),
                                  ALU.subtract).then_inc(hn_lo_ready.sem, 1)
            for k in range(KD):
                dve.wait_ge(scaled_ready.sem, scaled_ready.at(k + 1))
                if k >= 2:
                    dve.wait_ge(hn_lo_ready.sem, hn_lo_ready.at(k - 1))
                for _, span, w in TWO:
                    if span.start >= nt:
                        continue
                    mm = dve.tensor_scalar(moded[:, k % 2, span], scaled[:, k % 2, span], moda[:, w, k:k + 1],
                                           mod[l][:, w, part * KD + k:part * KD + k + 1], ALU.mult, ALU.add)
                mm.then_inc(moded_ready.sem, 1)
                if k >= 1:
                    lo(k - 1)
            lo(KD - 1)

        def norm_end():
            for x, n in ((ms_ready, 1), (ln_done, 1), (rstd_ready, 1), (scaled_ready, KD),
                         (moded_ready, KD), (hn_hi_ready, KD), (hn_lo_ready, KD), (moda_ready, 2)):
                x.phase_end(n)

        def add_residual(dve, s, tile, nt, part, n):
            dve.wait_ge(block_done[s].sem, n)
            for _, span, w in TWO:
                if span.start >= nt:
                    continue
                hv = h[:, bass.ds(tile, 1), span].rearrange("p a t -> p (a t)")
                mm = dve.scalar_tensor_tensor(out=hv, in0=ps_slot[s][:, span],
                                              scalar=mod_all[:, layer[0], w, bass.ds(part * KD + tile, 1)],
                                              in1=hv, op0=ALU.mult, op1=ALU.add)
            mm.then_inc(evacuated[s].sem, 1)

        def ffn(l, which, nt, mod_plan=None, more=True):
            part = 0 if which == 0 else 6
            gain = "n1" if which == 0 else "n2"
            PER_HALF = NFH + KD // 2
            ml, mj0, steps, extra = mod_plan or (0, 0, (0, 0), (0, 0))
            mod_from = [mj0, mj0 + NFH * steps[0] + extra[0]]
            mod_upto = [mod_from[1], mod_from[1] + NFH * steps[1] + extra[1]]
            turns = [0]
            for hf in range(2):
                turns.append(turns[-1] + (NFH if steps[hf] else 0) + (1 if extra[hf] else 0))
            n_mod = [0]
            uses = [[0] * MOD_SLOTS]
            for hf in range(2):
                uses.append([n + NFH * (i < steps[hf]) + (i < extra[hf]) for i, n in enumerate(uses[-1])])

            def mod_load(sp, slot, column, done):
                sp.wait_ge(mod_used.sem, done)
                sp.dma_start(w_mod[slot][:, :], A["wmod"][ml, column]).then_inc(mod_loaded[slot].sem, 16)

            with nc.Block() as block:
                @block.sync
                def _(sp):
                    for half in range(2):
                        b0 = half * PER_HALF
                        r, j0 = steps[half], mod_from[half]
                        seen = j0 - mj0
                        with sp.Fori(0, NFH) as i:
                            for s in range(2):
                                load_block(sp, s, A["wgu"][l, which, i * 2 + (half * NF + s)], KD, i + b0)
                            for s in range(r):
                                mod_load(sp, s, i * r + (j0 + s), i * r + mod_used.at(seen - r + s + 1))
                        for s in range(extra[half]):
                            mod_load(sp, s, j0 + NFH * r + s, mod_used.at(seen + NFH * r - r + s + 1))
                        with sp.Fori(0, KD // 2) as i:
                            for s in range(2):
                                load_block(sp, s, A["wdn"][l, which, half, i * 2 + s], NFH, i + (b0 + NFH))

                @block.gpsimd
                def _(pool):
                    norm_pool(pool, nt)
                    if more:
                        square_residuals(pool, KD // 2)

                @block.scalar
                def _(act):
                    norm_act(act, nt, lambda: [split_hi(act, s, KD, 0) for s in range(2)])

                    def gate_up(i, half, last):
                        b0 = half * PER_HALF
                        nk = NFH if last else KD
                        split_hi(act, 0, nk, i + (b0 + 1))
                        act.wait_ge(silu_ready.sem, i + silu_ready.at(half * NFH))
                        act.activation(tanh_g[:, 0:nt], ps_slot[0][:, 0:nt], ACT.Tanh,
                                       scale=0.5).then_inc(tanh_ready.sem, 1)
                        split_hi(act, 1, nk, i + (b0 + 1))
                        act.wait_ge(glu_ready.sem, i + glu_ready.at(half * NFH + 1))
                        act.activation(g_hi[:, bass.ds(i, 1), 0:nt].rearrange("p a t -> p (a t)"), glu[:, 0:nt],
                                       ACT.Copy).then_inc(g_hi_ready.sem, 1)

                    def down(i, half, last):
                        if not last:
                            for s in range(2):
                                split_hi(act, s, NFH, i + (half * PER_HALF + NFH + 1))
                        elif half == 0:
                            for s in range(2):
                                split_hi(act, s, KD, PER_HALF)
                    for half in range(2):
                        with act.Fori(0, NFH - 1) as i:
                            gate_up(i, half, False)
                        gate_up(NFH - 1, half, True)
                        with act.Fori(0, KD // 2 - 1) as i:
                            down(i, half, False)
                        down(KD // 2 - 1, half, True)

                @block.vector
                def _(dve):
                    norm_dve(dve, nt, gain, part, lambda: [split_lo(dve, s, KD, 0) for s in range(2)])
                    def gate_up(i, half, last):
                        b0 = half * PER_HALF
                        nk = NFH if last else KD
                        r = steps[half]
                        split_lo(dve, 0, nk, i + (b0 + 1))
                        dve.wait_ge(tanh_ready.sem, i + tanh_ready.at(half * NFH + 1))
                        dve.scalar_tensor_tensor(out=silu_g[:, 0:nt], in0=tanh_g[:, 0:nt], scalar=1.0,
                                                 in1=ps_slot[0][:, 0:nt], op0=ALU.add,
                                                 op1=ALU.mult).then_inc(silu_ready.sem, 1)
                        split_lo(dve, 1, nk, i + (b0 + 1))
                        dve.wait_ge(silu_ready.sem, i + silu_ready.at(half * NFH + 1))
                        dve.scalar_tensor_tensor(out=glu[:, 0:nt], in0=silu_g[:, 0:nt], scalar=0.5,
                                                 in1=ps_slot[1][:, 0:nt], op0=ALU.mult,
                                                 op1=ALU.mult).then_inc(glu_ready.sem, 1)
                        dve.wait_ge(g_hi_ready.sem, i + g_hi_ready.at(half * NFH + 1))
                        dve.tensor_tensor(g_lo[:, bass.ds(i, 1), 0:nt].rearrange("p a t -> p (a t)"), glu[:, 0:nt],
                                          g_hi[:, bass.ds(i, 1), 0:nt].rearrange("p a t -> p (a t)").bitcast(F32),
                                          ALU.subtract).then_inc(g_lo_ready.sem, 1)
                        if r:
                            mod_copy(dve, r, i * r + mod_used.at(mod_from[half] - mj0 + r))

                    def down(i, half, last):
                        done = half * PER_HALF + NFH
                        for s in range(2):
                            if not last:
                                split_lo(dve, s, NFH, i + (done + 1))
                            elif half == 0:
                                split_lo(dve, s, KD, PER_HALF)
                            add_residual(dve, s, i * 2 + s, nt, part + 2, i + block_done[s].at(done + 1))
                    for half in range(2):
                        with dve.Fori(0, NFH - 1) as i:
                            gate_up(i, half, False)
                        gate_up(NFH - 1, half, True)
                        if mod_upto[half] > mod_from[half]:
                            if extra[half]:
                                mod_copy(dve, extra[half], mod_used.at(mod_upto[half] - mj0))
                            dve.wait_ge(mod_turned.sem, mod_turned.at(turns[half + 1]))
                            n_mod[0] = mod_finish(dve, ml, 6 + half, mod_from[half], mod_upto[half], n_mod[0])
                        with dve.Fori(0, KD // 2 - 1) as i:
                            down(i, half, False)
                        down(KD // 2 - 1, half, True)

                @block.tensor
                def _(pe):
                    norm_pe(pe, nt)

                    def gate_up(i, half, first=False, is_first=False):
                        b0 = half * PER_HALF
                        pe.wait_ge(lo_ready[0].sem, i + lo_ready[0].at(b0 + 1))
                        pe.wait_ge(silu_ready.sem, i + silu_ready.at(half * NFH))
                        product(pe, 0, KD, ps_slot[0], hn_hi, hn_lo, nt, hn_lo_ready if first else None)
                        pe.wait_ge(lo_ready[1].sem, i + lo_ready[1].at(b0 + 1))
                        pe.wait_ge(glu_ready.sem, i + glu_ready.at(half * NFH))
                        product(pe, 1, KD, ps_slot[1], hn_hi, hn_lo, nt)
                        r = steps[half]
                        if r:
                            if not is_first:
                                mod_turn(pe, r, 6 + half, i * r + (mod_from[half] - r),
                                         i + mod_copied.at(turns[half]))
                            mod_rows(pe, r, lambda m: i + uses[half][m])
                    for half in range(2):
                        b0 = half * PER_HALF
                        if half == 1:
                            for s in range(2):
                                pe.wait_ge(evacuated[s].sem, evacuated[s].at(KD // 2))
                        if half == 0:
                            pe.wait_ge(rstd_ready.sem, rstd_ready.at(1))
                        gate_up(0, half, first=(half == 0), is_first=True)
                        with pe.Fori(1, NFH) as i:
                            gate_up(i, half)
                        if steps[half]:
                            mod_turn(pe, steps[half], 6 + half, mod_from[half] + (NFH - 1) * steps[half],
                                     mod_copied.at(turns[half] + NFH))
                        if extra[half]:
                            mod_rows(pe, extra[half], lambda m: uses[half][m] + NFH * (m < steps[half]))
                            mod_turn(pe, extra[half], 6 + half, mod_from[half] + NFH * steps[half],
                                     mod_copied.at(turns[half + 1]))
                        pe.wait_ge(g_lo_ready.sem, g_lo_ready.at((half + 1) * NFH))
                        with pe.Fori(0, KD // 2) as i:
                            for s in range(2):
                                pe.wait_ge(lo_ready[s].sem, i + lo_ready[s].at(b0 + NFH + 1))
                                pe.wait_ge(evacuated[s].sem, i + evacuated[s].at(half * KD // 2))
                                product(pe, s, NFH, ps_slot[s], g_hi, g_lo, nt)
            norm_end()
            stream_end(2 * PER_HALF)
            for x in (tanh_ready, silu_ready, glu_ready, g_hi_ready, g_lo_ready):
                x.phase_end(NF)
            for s in range(2):
                evacuated[s].phase_end(KD)
            if more:
                squares_end()
            mod_used.phase_end(mod_upto[1] - mj0)
            mod_copied.phase_end(turns[2])
            mod_turned.phase_end(turns[2])
            mod_ready.phase_end(n_mod[0])
            for i in range(MOD_SLOTS):
                mod_loaded[i].phase_end(16 * uses[-1][i])

        def in_proj(l):
            pairs = N_IN // 2
            LOOP = 9
            with nc.Block() as block:
                @block.sync
                def _(sp):
                    with sp.Fori(0, pairs) as i:
                        for s in range(2):
                            load_block(sp, s, A["win"][l, i * 2 + s], KD, i)

                @block.gpsimd
                def _(pool):
                    norm_pool(pool, NT)

                @block.scalar
                def _(act):
                    norm_act(act, NT, lambda: [split_hi(act, s, KD, 0) for s in range(2)])

                    def evacuate(i, s, dst):
                        act.wait_ge(block_done[s].sem, i + block_done[s].at(1))
                        act.activation(dst, ps_slot[s], ACT.Copy).then_inc(evacuated[s].sem, 1)
                    with act.Fori(0, LOOP) as i:
                        for s in range(2):
                            split_hi(act, s, KD, i + 1)
                            evacuate(i, s, u[:, bass.ds(i * 2 + s, 1), :].rearrange("p a t -> p (a t)"))
                    for n in range(2 * LOOP, N_IN):
                        i, s = n // 2, n % 2
                        if i + 1 < pairs:
                            split_hi(act, s, KD, i + 1)
                        if n < U_TILES:
                            evacuate(i, s, u[:, n, :])
                        else:
                            j = n - U_TILES
                            act.wait_ge(block_done[s].sem, i + block_done[s].at(1))
                            act.activation(v_nat[:, :, j * P:(j + 1) * P],
                                           ps_slot[s].rearrange("p (a b) -> p a b", b=P),
                                           ACT.Copy).then_inc(evacuated[s].sem, 1)

                @block.vector
                def _(dve):
                    norm_dve(dve, NT, "nm", 3, lambda: [split_lo(dve, s, KD, 0) for s in range(2)])
                    with dve.Fori(1, pairs) as i:
                        for s in range(2):
                            split_lo(dve, s, KD, i)

                @block.tensor
                def _(pe):
                    norm_pe(pe, NT)

                    def pair(i, first=False):
                        for s in range(2):
                            pe.wait_ge(lo_ready[s].sem, i + lo_ready[s].at(1))
                            pe.wait_ge(evacuated[s].sem, i + evacuated[s].at(0))
                            product(pe, s, KD, ps_slot[s], hn_hi, hn_lo, NT,
                                    hn_lo_ready if first and s == 0 else None)
                    pe.wait_ge(rstd_ready.sem, rstd_ready.at(1))
                    pair(0, first=True)
                    with pe.Fori(1, LOOP) as i:
                        pair(i)
                    for n in range(2 * LOOP, N_IN):
                        i, s = n // 2, n % 2
                        pe.wait_ge(lo_ready[s].sem, lo_ready[s].at(i + 1))
                        pe.wait_ge(evacuated[s].sem, evacuated[s].at(i))
                        if n < U_TILES:
                            product(pe, s, KD, ps_slot[s], hn_hi, hn_lo, NT)
                            continue
                        for tt in range(NTT):
                            for k in range(KD):
                                for m, (a, w) in enumerate(((hn_hi, w_hi[s]), (hn_lo, w_hi[s]), (hn_hi, w_lo[s]))):
                                    mm = pe.matmul(ps_slot[s][:, tt * P:(tt + 1) * P], a[:, k, tt * P:(tt + 1) * P],
                                                   w[:, k, :], start=(k == 0 and m == 0),
                                                   stop=(k == KD - 1 and m == 2))
                        mm.then_inc(block_done[s].sem, 1)
            norm_end()
            stream_end(pairs)
            for s in range(2):
                evacuated[s].phase_end(pairs)

        def out_proj(l, nt):
            pairs = KD // 2
            with nc.Block() as block:
                @block.sync
                def _(sp):
                    with sp.Fori(0, pairs) as i:
                        for s in range(2):
                            load_block(sp, s, A["wout"][l, i * 2 + s], KD, i)

                @block.gpsimd
                def _(pool):
                    square_residuals(pool, 0)

                @block.scalar
                def _(act):
                    with act.Fori(0, pairs) as i:
                        for s in range(2):
                            split_hi(act, s, KD, i)

                @block.vector
                def _(dve):
                    for s in range(2):
                        split_lo(dve, s, KD, 0)

                    def step(i, last):
                        for s in range(2):
                            if not last:
                                split_lo(dve, s, KD, i + 1)
                            add_residual(dve, s, i * 2 + s, nt, 5, i + block_done[s].at(1))
                    with dve.Fori(0, pairs - 1) as i:
                        step(i, False)
                    step(pairs - 1, True)

                @block.tensor
                def _(pe):
                    with pe.Fori(0, pairs) as i:
                        for s in range(2):
                            pe.wait_ge(lo_ready[s].sem, i + lo_ready[s].at(1))
                            pe.wait_ge(evacuated[s].sem, i + evacuated[s].at(0))
                            product(pe, s, KD, ps_slot[s], hn_hi, hn_lo, nt)
            stream_end(pairs)
            for s in range(2):
                evacuated[s].phase_end(pairs)
            squares_end()

        place["T"] = T0
        rope = tmp("rope", [P, 4, SEQ])
        bias = tmp("bias", [P, 4, 14 * GRID_W])
        w_mla = tmp("w_mla", [P, 3 * 4 * MLA_D + 256])
        o_nat = tmp("o_nat", [P, 2, 256])
        stats = tmp("stats", [P, 16])
        q_mla = [at(f"q_mla{i}", [P, NT], R_W + i * TOK) for i in range(4)]
        k_mla = [at(f"k_mla{i}", [P, NT], R_W + (4 + i) * TOK) for i in range(4)]
        v_mla = at("v_mla", [P, NTT, 256], R_W + 8 * TOK)
        hsq = at("hsq", [P, 2, NT], R_N)
        hln = at("hln", [P, NT], R_N + 2 * TOK)
        hrstd = at("hrstd", [P, 2, NT], R_N + 3 * TOK)
        rot_s = at("rot_s", [P, SEQ], R_N + 5 * TOK)
        rot_c = at("rot_c", [P, 2, SEQ], R_N + 6 * TOK)
        probs = at("probs", [P, 2, NT], R_G)
        probs_t = at("probs_t", [P, 2, NT], R_G + 2 * TOK)

        mix_loaded = sem("mix_loaded")
        hsq_ready, hms_ready, hln_done, hrstd_ready, hnorm_ready = (sem("hsq_ready"), sem("hms_ready"), sem("hln_done"),
                                                                    sem("hrstd_ready"), sem("hnorm_ready"))
        rot_ready, rot_c_ready, rot_s_ready, roped = sem("rot_ready"), sem("rot_c_ready"), sem("rot_s_ready"), sem("roped")
        proj_ready, proj_copied = sem("proj_ready"), sem("proj_copied")

        def head_norms():
            rows = slice(0, P)
            out = [([u[:, 0, :], u[:, 1, :]], rows, K_["ones"], 1 / 256, [col("mq", 0), col("mq", 1)], None, None, None),
                   ([u[:, 2, :]], rows, K_["ones"], 1 / 128, [col("mkv")], None, None, None)]
            for t in (U_NQ, U_NQ + 1, U_NK, U_NK + 1):
                q = t < U_NK
                out.append(([u[:, t, :]], rows, K_["ones64"], 1 / HEAD, [col("nq" if q else "nk")],
                            LN_Q64 if q else None, None, None))
            for t in (U_GQ, U_GQ + 1, U_GK):
                q = t < U_GK
                out.append(([u[:, t, :]], rows, K_["ones64"], 1 / HEAD, [col("gq" if q else "gk")],
                            LN_Q64 if q else None, 0, K_["rot_g"]))
            first = len(out)
            rows = slice(0, MLA_D)
            for t, q in [(t, True) for t in q_mla] + [(t, False) for t in k_mla]:
                out.append(([t[rows, :]], rows, K_["ones"][rows, 0:MLA_D], 1 / MLA_D, [col("mqn" if q else "mkn", 0, rows)],
                            LN_Q96 if q else None, 2, K_["rot_m"][rows, 0:MLA_D]))
            return out, first

        def qkv(l):
            units, first = head_norms()
            groups = (range(0, first), range(first, len(units)))
            roped_units = [n for n, x in enumerate(units) if x[6] is not None]
            rope_no = {n: r for r, n in enumerate(roped_units)}
            sq_no = [sum(len(x[0]) for x in units[:n]) for n in range(len(units) + 1)]
            N_PROJ = 10
            ps_projs = [psf[:, 3072:3072 + NT], psf[:, 2048:2048 + NT]]
            group0_ropes = sum(n < first for n in roped_units)

            with nc.Block() as block:
                @block.sync
                def _(sp):
                    sp.dma_start(w_mla[:, :], A["mla"][l]).then_inc(mix_loaded.sem, 16)
                    sp.dma_start(rope[:, :, :], A["rope"]).then_inc(mix_loaded.sem, 16)
                    sp.dma_start(bias[:, :, :], A["bias"][l]).then_inc(mix_loaded.sem, 16)
                    sp.wait_ge(mix_loaded.sem, mix_loaded.at(48))

                @block.scalar
                def _(act):
                    act.preload_act_table_set("natural_log_exp_and_others")

                    def squares(n):
                        tiles, rows = units[n][0:2]
                        for j, t in enumerate(tiles):
                            b = sq_no[n] + j
                            if b >= 2:
                                act.wait_ge(hms_ready.sem, hms_ready.at(b - 1))
                            act.activation(hsq[rows, b % 2, :], t, ACT.Square).then_inc(hsq_ready.sem, 1)

                    def rstd_of(n):
                        rows, inv, lnc = units[n][1], units[n][3], units[n][5]
                        act.wait_ge(hms_ready.sem, hms_ready.at(sq_no[n + 1]))
                        if n >= 1:
                            act.wait_ge(hrstd_ready.sem, hrstd_ready.at(n))
                        act.activation(hln[rows, :], ps_slot[n % 2][rows, :], ACT.Ln, bias=small[rows, EPS:EPS + 1],
                                       scale=inv).then_inc(hln_done.sem, 1)
                        act.wait_ge(hln_done.sem, hln_done.at(n + 1))
                        if n >= 2:
                            act.wait_ge(hnorm_ready.sem, hnorm_ready.at(n - 1))
                        act.activation(hrstd[rows, n % 2, :], hln[rows, :], ACT.Exp, scale=-0.5,
                                       bias=0.0 if lnc is None else small[rows, lnc:lnc + 1]).then_inc(hrstd_ready.sem, 1)
                    for gi, g in enumerate(groups):
                        for n in g:
                            squares(n)
                            if n > g[0]:
                                rstd_of(n - 1)
                        rstd_of(g[-1])
                        if gi == 0:
                            for m in range(N_PROJ):
                                act.wait_ge(proj_ready.sem, proj_ready.at(m + 1))
                                ps_proj = ps_projs[m % 2]
                                if m < 8:
                                    dst = (q_mla[m] if m < 4 else k_mla[m - 4])[0:MLA_D, :]
                                    act.activation(dst, ps_proj[0:MLA_D, :], ACT.Copy).then_inc(proj_copied.sem, 1)
                                else:
                                    act.activation(v_mla[:, 3 * (m - 8):3 * (m - 7), :].rearrange("p a b -> p (a b)"),
                                                   ps_proj, ACT.Copy).then_inc(proj_copied.sem, 1)
                            act.wait_ge(proj_copied.sem, proj_copied.at(N_PROJ))

                @block.tensor
                def _(pe):
                    def sums(n):
                        tiles, rows, ones = units[n][0:3]
                        M = rows.stop
                        if n >= 2:
                            pe.wait_ge(hln_done.sem, hln_done.at(n - 1))
                        for j in range(len(tiles)):
                            b = sq_no[n] + j
                            pe.wait_ge(hsq_ready.sem, hsq_ready.at(b + 1))
                            for a, e in ((0, 512), (512, NT)):
                                mm = pe.matmul(ps_slot[n % 2][0:M, a:e], ones, hsq[rows, b % 2, a:e], start=(j == 0),
                                               stop=(j == len(tiles) - 1))
                            mm.then_inc(hms_ready.sem, 1)

                    def rotate(n):
                        if n not in rope_no:
                            return
                        r = rope_no[n]
                        tiles, rows, rotm = units[n][0], units[n][1], units[n][7]
                        pe.wait_ge(hnorm_ready.sem, hnorm_ready.at(n + 1))
                        if r >= 2:
                            pe.wait_ge(rot_s_ready.sem, rot_s_ready.at(r - 1))
                        pe.matmul(ps[0:rows.stop, 4 + r % 2, :], rotm, tiles[0][:, LAT], start=True,
                                  stop=True).then_inc(rot_ready.sem, 1)

                    def projections():
                        pe.wait_ge(mix_loaded.sem, mix_loaded.at(48))
                        pe.wait_ge(hnorm_ready.sem, hnorm_ready.at(2))
                        W4 = 4 * MLA_D
                        for m in range(N_PROJ):
                            ps_proj = ps_projs[m % 2]
                            if m >= 2:
                                pe.wait_ge(proj_copied.sem, proj_copied.at(m - 1))
                            elif m == 1:
                                pe.wait_ge(rot_s_ready.sem, rot_s_ready.at(group0_ropes))
                            if m < 8:
                                hd = m % 4
                                for a, e in ((0, 512), (512, NT)):
                                    out = ps_proj[0:MLA_D, a:e]
                                    if m < 4:
                                        for k in range(2):
                                            w = w_mla[:, k * W4 + hd * MLA_D:k * W4 + (hd + 1) * MLA_D]
                                            mm = pe.matmul(out, w, u[:, k, a:e], start=(k == 0), stop=(k == 1))
                                    else:
                                        w = w_mla[:, 2 * W4 + hd * MLA_D:2 * W4 + (hd + 1) * MLA_D]
                                        pe.matmul(out, w, u[:, U_KV, a:e], start=True, stop=False)
                                        mm = pe.matmul(out, K_["sel_kr"][:, 0:MLA_D], u[:, U_KR, a:e], start=False,
                                                       stop=True)
                            else:
                                for j in range(3):
                                    tt = 3 * (m - 8) + j
                                    mm = pe.matmul(ps_proj[:, j * 256:(j + 1) * 256], u[:, U_KV, tt * P:(tt + 1) * P],
                                                   w_mla[:, 3 * W4:3 * W4 + 256], start=True, stop=True)
                            mm.then_inc(proj_ready.sem, 1)
                    for gi, g in enumerate(groups):
                        for n in g:
                            sums(n)
                            if n > g[0]:
                                rotate(n - 1)
                        rotate(g[-1])
                        if gi == 0:
                            projections()
                            pe.wait_ge(proj_copied.sem, proj_copied.at(N_PROJ))

                @block.gpsimd
                def _(pool):
                    pool.wait_ge(mix_loaded.sem, mix_loaded.at(48))
                    for n in roped_units:
                        r = rope_no[n]
                        tiles, rows, tab = units[n][0], units[n][1], units[n][6]
                        pool.wait_ge(hnorm_ready.sem, hnorm_ready.at(n + 1))
                        if r >= 2:
                            pool.wait_ge(roped.sem, roped.at(r - 1))
                        pool.tensor_tensor(rot_c[rows, r % 2, :], tiles[0][:, LAT], rope[rows, tab, :],
                                           ALU.mult).then_inc(rot_c_ready.sem, 1)

                @block.vector
                def _(dve):
                    dve.wait_ge(mix_loaded.sem, mix_loaded.at(48))

                    def scale_rows(n):
                        tiles, rows, gains = units[n][0], units[n][1], units[n][4]
                        dve.wait_ge(hrstd_ready.sem, hrstd_ready.at(n + 1))
                        for t, g in zip(tiles, gains):
                            mm = dve.scalar_tensor_tensor(out=t, in0=t, scalar=g, in1=hrstd[rows, n % 2, :],
                                                          op0=ALU.mult, op1=ALU.mult)
                        mm.then_inc(hnorm_ready.sem, 1)

                    def apply_rope(n):
                        if n not in rope_no:
                            return
                        r = rope_no[n]
                        tiles, rows, tab = units[n][0], units[n][1], units[n][6]
                        dve.wait_ge(rot_ready.sem, rot_ready.at(r + 1))
                        if r >= 1:
                            dve.wait_ge(roped.sem, roped.at(r))
                        dve.tensor_tensor(rot_s[rows, :], ps[rows, 4 + r % 2, :], rope[rows, tab + 1, :],
                                          ALU.mult).then_inc(rot_s_ready.sem, 1)
                        dve.wait_ge(rot_s_ready.sem, rot_s_ready.at(r + 1))
                        dve.wait_ge(rot_c_ready.sem, rot_c_ready.at(r + 1))
                        dve.tensor_tensor(tiles[0][:, LAT], rot_c[rows, r % 2, :], rot_s[rows, :],
                                          ALU.add).then_inc(roped.sem, 1)
                    for g in groups:
                        for n in g:
                            scale_rows(n)
                            if n > g[0]:
                                apply_rope(n - 1)
                        apply_rope(g[-1])
            NU, NR = len(units), len(roped_units)
            for x, n in ((mix_loaded, 48), (hsq_ready, sq_no[NU]), (hms_ready, sq_no[NU]), (hln_done, NU),
                         (hrstd_ready, NU), (hnorm_ready, NU), (rot_ready, NR), (rot_c_ready, NR), (rot_s_ready, NR),
                         (roped, NR), (proj_ready, N_PROJ), (proj_copied, N_PROJ)):
                x.phase_end(n)

        scores_ready, biased, max_ready, exp_ready = sem("scores_ready"), sem("scores_biased"), sem("max_ready"), sem("exp_ready")
        probs_turned, probs_t_ready, pv_ready = sem("probs_turned"), sem("probs_t_ready"), sem("pv_ready")
        sum_inverted, o_ready = sem("sum_inverted"), sem("o_ready")
        o_turned, mix_hi_ready, mix_lo_ready = sem("o_turned"), sem("mix_hi_ready"), sem("mix_lo_ready")
        keep_ready, shift_step = sem("keep_ready"), sem("shift_step")
        shift_prev, shift_next = [at(n, [P, NT], R_N + (2 + i) * TOK) for i, n in enumerate(("shift_prev", "shift_next"))]
        SHIFTED = U_NQ - U_RW
        MIX_TILE = {"mla": 0, "na": 4, "gqa": 6}

        def attention(l, nt):
            units = [(m, qt, hd) for m in ("mla", "na", "gqa") for qt in range(nt // P) for hd in range(4)]
            N = len(units)
            ps_s = [psf[:, 0:NT], psf[:, 1024:1024 + NT]]
            ps_t = psf[:, 2048:2048 + NT]

            def keys(n):
                return (0, 0) if units[n][1] < LT_TILES else (SEQ, LT_TILES)

            def qk(n):
                m, qt, hd = units[n]
                q = slice(qt * P, (qt + 1) * P)
                if m == "mla":
                    return q_mla[hd][0:MLA_D, q], k_mla[hd][0:MLA_D, :]
                if m == "na":
                    r = slice(64 * (hd % 2), 64 * (hd % 2) + 64)
                    return u[r, U_NQ + hd // 2, q], u[r, U_NK + hd // 2, :]
                i = (0, 2, 1, 3)[hd]
                r = slice(64 * (i % 2), 64 * (i % 2) + 64)
                return u[r, U_GQ + i // 2, q], u[r, U_GK, :]

            def values(n, kt):
                m, _, hd = units[n]
                if m == "mla":
                    return v_mla[:, kt, hd * HEAD:(hd + 1) * HEAD]
                c = hd * HEAD if m == "na" else 256 + (hd // 2) * HEAD
                return v_nat[:, kt, c:c + HEAD]

            def has_bias(n):
                return units[n][0] == "na" and units[n][1] < LT_TILES
            biases = [sum(has_bias(j) for j in range(n)) for n in range(N + 1)]

            def group_end(n):
                return 0 <= n < N and units[n][2] == 3

            with nc.Block() as block:
                @block.tensor
                def _(pe):
                    def scores(n):
                        k0, _ = keys(n)
                        q, k = qk(n)
                        if n >= 2:
                            pe.wait_ge(exp_ready.sem, exp_ready.at(n - 1))
                        for a, e in ((0, 512), (512, NT)):
                            if a >= k0:
                                mm = pe.matmul(ps_s[n % 2][:, a:e], q, k[:, a:e], start=True, stop=True)
                        mm.then_inc(scores_ready.sem, 1)

                    def turn(n):
                        _, kt0 = keys(n)
                        pe.wait_ge(exp_ready.sem, exp_ready.at(n + 1))
                        if n >= 1:
                            pe.wait_ge(probs_t_ready.sem, probs_t_ready.at(n))
                        for kt in range(kt0, NTT):
                            mm = pe.transpose(ps_t[:, kt * P:(kt + 1) * P], probs[:, n % 2, kt * P:(kt + 1) * P],
                                              K_["ident"])
                        mm.then_inc(probs_turned.sem, 1)

                    def turn_out(n):
                        g = n // 4
                        pe.wait_ge(o_ready.sem, o_ready.at(n + 1))
                        for i in range(2):
                            mm = pe.transpose(ps[:, 6 + n % 2, (i + 1) * P:(i + 2) * P], o_nat[:, g % 2, i * P:(i + 1) * P],
                                              K_["ident"])
                        mm.then_inc(o_turned.sem, 1)

                    def weigh(n):
                        _, kt0 = keys(n)
                        pe.wait_ge(probs_t_ready.sem, probs_t_ready.at(n + 1))
                        if n >= 2:
                            pe.wait_ge(o_ready.sem, o_ready.at(n - 1))
                            if group_end(n - 2):
                                pe.wait_ge(mix_lo_ready.sem, mix_lo_ready.at((n - 2) // 4 + 1))
                        for kt in range(kt0, NTT):
                            mm = pe.matmul(ps[:, 6 + n % 2, 0:HEAD], probs_t[:, n % 2, kt * P:(kt + 1) * P], values(n, kt),
                                           start=(kt == kt0), stop=(kt == NTT - 1))
                        mm.then_inc(pv_ready.sem, 1)
                    for n in range(N + 3):
                        if n < N:
                            scores(n)
                        if 1 <= n <= N:
                            turn(n - 1)
                        if group_end(n - 3):
                            turn_out(n - 3)
                        if 2 <= n <= N + 1:
                            weigh(n - 2)

                @block.scalar
                def _(act):
                    for n in range(N + 3):
                        if n < N:
                            k0, _ = keys(n)
                            act.wait_ge(max_ready.sem, max_ready.at(n + 1))
                            if n >= 2:
                                act.wait_ge(probs_turned.sem, probs_turned.at(n - 1))
                            act.activation(probs[:, n % 2, k0:NT], ps_s[n % 2][:, k0:NT], ACT.Exp,
                                           bias=stats[:, n % 4:n % 4 + 1],
                                           accum_out=stats[:, 4 + n % 4:5 + n % 4]).then_inc(exp_ready.sem, 1)
                        if 1 <= n <= N:
                            m = n - 1
                            k0, _ = keys(m)
                            act.wait_ge(probs_turned.sem, probs_turned.at(m + 1))
                            if m >= 2:
                                act.wait_ge(pv_ready.sem, pv_ready.at(m - 1))
                            act.activation(probs_t[:, m % 2, k0:NT], ps_t[:, k0:NT], ACT.Copy).then_inc(probs_t_ready.sem, 1)
                        if group_end(n - 3):
                            m = n - 3
                            t, qt = MIX_TILE[units[m][0]], units[m][1]
                            act.wait_ge(o_turned.sem, o_turned.at(m // 4 + 1))
                            act.activation(hn_hi[:, t:t + 2, qt * P:(qt + 1) * P],
                                           ps[:, 6 + m % 2, P:3 * P].rearrange("p (a b) -> p a b", b=P),
                                           ACT.Copy).then_inc(mix_hi_ready.sem, 1)

                @block.gpsimd
                def _(pool):
                    pool.wait_ge(keep_ready.sem, keep_ready.at(2))
                    own = 0
                    for n in range(SHIFTED):
                        t = u[:, U_RW + n, :]
                        wide = lambda c: c.broadcast_to([P, NT])
                        pool.tensor_tensor(shift_prev[:, :], t, wide(col("mu0", n)), ALU.mult)
                        pool.tensor_tensor(shift_next[:, :], t, wide(col("mu1", n)),
                                           ALU.mult).then_inc(shift_step.sem, 1)
                        pool.wait_ge(shift_step.sem, shift_step.at(own + 1))
                        pool.tensor_tensor(t, t, wide(keep[:, n:n + 1]), ALU.mult).then_inc(shift_step.sem, 1)
                        for i, (src, to, back) in enumerate(((shift_prev, 1, 0), (shift_next, 0, 1))):
                            pool.wait_ge(shift_step.sem, shift_step.at(own + 2 + i))
                            for x in (LAT, CTXT):
                                o = t[:, x.start + to:x.stop - back]
                                mm = pool.tensor_tensor(o, o, src[:, x.start + back:x.stop - to], ALU.add)
                            mm.then_inc(shift_step.sem, 1)
                        own += 4
                        pool.wait_ge(shift_step.sem, shift_step.at(own))

                @block.vector
                def _(dve):
                    a, b = COLS["mu0"]
                    a1, b1 = COLS["mu1"]
                    dve.tensor_tensor(keep[:, :], cols[l][:, a:b], cols[l][:, a1:b1], ALU.add).then_inc(keep_ready.sem, 1)
                    dve.wait_ge(keep_ready.sem, keep_ready.at(1))
                    dve.tensor_scalar(keep[:, :], keep[:, :], -1.0, 1.0, ALU.mult, ALU.add).then_inc(keep_ready.sem, 1)
                    for n in range(N + 3):
                        if n < N:
                            m, qt, hd = units[n]
                            k0, _ = keys(n)
                            dve.wait_ge(scores_ready.sem, scores_ready.at(n + 1))
                            if has_bias(n):
                                b0 = (7 - 2 * qt - 1) * GRID_W
                                dve.tensor_tensor(ps_s[n % 2][:, LAT], ps_s[n % 2][:, LAT], bias[:, hd, b0:b0 + SEQ],
                                                  ALU.add).then_inc(biased.sem, 1)
                                dve.wait_ge(biased.sem, biased.at(biases[n] + 1))
                            if n >= 4:
                                dve.wait_ge(exp_ready.sem, exp_ready.at(n - 3))
                            dve.tensor_reduce(stats[:, n % 4:n % 4 + 1], ps_s[n % 2][:, k0:NT], AXX, ALU.max,
                                              negate=True).then_inc(max_ready.sem, 1)
                        if 2 <= n <= N + 1:
                            m = n - 2
                            g = m // 4
                            dve.wait_ge(pv_ready.sem, pv_ready.at(m + 1))
                            dve.reciprocal(stats[:, 8 + m % 4:9 + m % 4],
                                           stats[:, 4 + m % 4:5 + m % 4]).then_inc(sum_inverted.sem, 1)
                            dve.wait_ge(sum_inverted.sem, sum_inverted.at(m + 1))
                            hd = units[m][2]
                            if hd == 0 and g >= 2:
                                dve.wait_ge(o_turned.sem, o_turned.at(g - 1))
                            dve.tensor_scalar(o_nat[:, g % 2, hd * HEAD:(hd + 1) * HEAD], ps[:, 6 + m % 2, 0:HEAD],
                                              stats[:, 8 + m % 4:9 + m % 4], None, ALU.mult).then_inc(o_ready.sem, 1)
                        if group_end(n - 3):
                            m = n - 3
                            t, qt = MIX_TILE[units[m][0]], units[m][1]
                            dve.wait_ge(mix_hi_ready.sem, mix_hi_ready.at(m // 4 + 1))
                            dve.tensor_tensor(hn_lo[:, t:t + 2, qt * P:(qt + 1) * P],
                                              ps[:, 6 + m % 2, P:3 * P].rearrange("p (a b) -> p a b", b=P),
                                              hn_hi[:, t:t + 2, qt * P:(qt + 1) * P].bitcast(F32),
                                              ALU.subtract).then_inc(mix_lo_ready.sem, 1)
            for x, n in ((scores_ready, N), (biased, biases[N]), (max_ready, N), (exp_ready, N), (probs_turned, N),
                         (probs_t_ready, N), (pv_ready, N), (sum_inverted, N), (o_ready, N), (o_turned, N // 4),
                         (mix_hi_ready, N // 4), (mix_lo_ready, N // 4), (keep_ready, 2), (shift_step, 4 * SHIFTED)):
                x.phase_end(n)

        place["T"] = T0
        N_MASK = 11
        masks = tmp("masks", [P, 2, N_MASK, P])
        scan_ones = tmp("scan_ones", [P, NT])
        kk_n = tmp("kk_n", [P, 2, NT])
        lora = tmp("lora", [P, 512])
        decay_diag = tmp("decay_diag", [P, NCH, CH])
        state = tmp("state", [P, 2, CH])
        chunk_decay = tmp("chunk_decay", [P, NCH])
        half_bias = tmp("half_bias", [P, 8])
        ka_rest = tmp("ka_rest", [P, 2])
        UNITS = 2 * NTT
        x_inv = at("x_inv", [P, UNITS, P], R_G)
        xt_inv = at("xt_inv", [P, UNITS, P], R_G + 2 * TOK)
        ar = at("ar", [P, NTT, 2, P], R_G + 12 * TOK)
        bk = at("bk", [P, 2, NT], R_G + 14 * TOK)
        bk_end = at("bk_end", [P, 2, NT], R_G + 16 * TOK)
        a_mv = at("a_mv", [P, UNITS, P], R_G + 18 * TOK)
        b_nat = at("b_nat", [P, NTT, P], R_G + 20 * TOK)
        k_nat = at("k_nat", [P, NTT, P], R_G + 21 * TOK)
        r_eff = at("r_eff", [P, NT], R_G + 14 * TOK)
        y_loc = at("y_loc", [P, NT], R_G + 15 * TOK)
        trans = at("trans", [P, NCH, CH], R_G + 16 * TOK)
        s_add = at("s_add", [P, NCH, CH], R_G + 17 * TOK)
        sc = at("sc", [P, UNITS, 4, P], R_W)
        f = [at(f"f{i}", [P, NT], R_W + i * TOK) for i in range(8)]
        lx = at("lx", [P, UNITS, P], R_W + 8 * TOK)
        neg_w = at("neg_w", [P, UNITS, P], R_W + 8 * TOK)
        v_rw = at("v_rw", [P, NTT, P], R_W + 10 * TOK)
        y_sum = [at(f"y_sum{i}", [P, NT], R_N + (2 + i) * TOK) for i in range(2)]
        kd_sum = [at(f"kd_sum{i}", [P, NT], R_N + (KD + 2 + i) * TOK) for i in range(2)]

        v_step = sem("vector_step")
        a_step = sem("scalar_step")
        tanh_done, kk_raw = sem("tanh_done"), sem("kk_raw")
        sums_ready, rsq_ready = sem("head_sums_ready"), sem("head_rsqrt_ready")
        lora_ready, gate_tanh, exps_in, exps_out = sem("lora_ready"), sem("gate_tanh"), sem("exp_args"), sem("exp_done")
        features, nat_turned, nat_copied = sem("features"), sem("nat_turned"), sem("nat_copied")
        wkv_scores, wkv_masked = sem("wkv_scores"), sem("wkv_masked")
        lx_ready, lx_masked, step_ready, x_ready = sem("lx_ready"), sem("lx_masked"), sem("inv_step"), sem("x_ready")
        mv_ready, mv_copied, w_ready, w_copied = sem("mv_ready"), sem("mv_copied"), sem("w_ready"), sem("w_copied")
        chunk_ready, reff_ready, yloc_copied, trans_ready, sadd_copied = (
            sem("chunk_products"), sem("r_eff_ready"), sem("y_loc_copied"), sem("trans_ready"), sem("s_add_copied"))
        state_ready, state_mm, y_ready, round_done = (sem("state_ready"), sem("state_product"), sem("y_ready"),
                                                      sem("round_done"))
        fin_ps, fin_v, fin_a = sem("final_products"), sem("final_vector"), sem("final_scalar")

        def rwkv(l, nt):
            ROUNDS = [(hp, d) for hp in range(2) for d in range(2)]
            SEGS = (LAT, CTXT)
            K_OF, R_OF, V_OF = U_RW + 2, U_RW, U_RW + 4
            slots = [psf[:, i * 1024:i * 1024 + NT] for i in range(4)]
            GROUPS, LEVELS = 3, 6
            UG = UNITS // GROUPS
            CTX_CH = list(range(SEQ // CH, NCH))
            LAT_CH = list(range(SEQ // CH))
            ORDER = [CTX_CH + LAT_CH, CTX_CH[::-1] + LAT_CH[::-1]]
            hr = lambda j: slice(64 * j, 64 * j + 64)
            by_chunk = lambda bank: ps[:, bank:bank + 2, 0:NTT * CH].rearrange("p b (t c) -> p t b c", c=CH)
            spans = ((0, 512), (512, NT))

            with nc.Block() as block:
                @block.sync
                def _(sp):
                    sp.dma_start(lora[:, :], A["lora"][l]).then_inc(mix_loaded.sem, 16)
                    sp.dma_start(scan_ones[:, :], A["scan"]).then_inc(mix_loaded.sem, 16)
                    sp.dma_start(masks[:, :, :, :], A["masks"]).then_inc(mix_loaded.sem, 16)
                    sp.wait_ge(mix_loaded.sem, mix_loaded.at(48))

                @block.scalar
                def _(act):
                    own = [0]

                    def link(ins):
                        own[0] += 1
                        ins.then_inc(a_step.sem, 1)
                        act.wait_ge(a_step.sem, a_step.at(own[0]))
                    link(act.activation(u[0:64, U_WA, :], u[0:64, U_WA, :], ACT.Tanh))
                    act.activation(u[0:64, U_GD, :], u[0:64, U_GD, :], ACT.Tanh, scale=0.5).then_inc(tanh_done.sem, 1)
                    act.preload_act_table_set("natural_log_exp_and_others")
                    for hp in range(2):
                        act.wait_ge(kk_raw.sem, kk_raw.at(hp + 1))
                        act.activation(f[2 + hp][:, :], kk_n[:, hp, :], ACT.Square).then_inc(rsq_ready.sem, 1)
                    for hp in range(2):
                        act.wait_ge(sums_ready.sem, sums_ready.at(hp + 1))
                        link(act.activation(f[4 + hp][:, :], slots[hp], ACT.Ln, bias=small[:, EPS_KK:EPS_KK + 1]))
                    for hp in range(2):
                        act.activation(f[6 + hp][:, :], f[4 + hp][:, :], ACT.Exp, scale=-0.5).then_inc(rsq_ready.sem, 1)
                    for r, (hp, d) in enumerate(ROUNDS):
                        for i in range(2):
                            act.wait_ge(lora_ready.sem, lora_ready.at(2 * r + i + 1))
                            c = 4 * i + 2 * d + hp
                            act.activation(f[i][:, :], slots[i], ACT.Tanh, scale=0.5,
                                           bias=half_bias[:, c:c + 1]).then_inc(gate_tanh.sem, 1)
                        before, through, rest = (f[4], f[3], f[5]) if d == 0 else (f[5], f[6], f[4])
                        act.wait_ge(exps_in.sem, exps_in.at(r + 1))
                        t3 = lambda x: x[:, :].rearrange("p (a b) -> p a b", b=P)
                        act.activation(ar[:, :, 0, :], t3(before), ACT.Exp, scale=-G_DECAY).then_inc(exps_out.sem, 1)
                        act.activation(ar[:, :, 1, :], t3(through), ACT.Exp, scale=-G_DECAY).then_inc(exps_out.sem, 1)
                        act.activation(bk[:, 0, :], through[:, :], ACT.Exp, scale=G_DECAY).then_inc(exps_out.sem, 1)
                        act.activation(bk_end[:, 0, :], rest[:, :], ACT.Exp, scale=-G_DECAY).then_inc(exps_out.sem, 1)
                        act.activation(chunk_decay[:, :], f[3][:, CH - 1::CH], ACT.Exp,
                                       scale=-G_DECAY).then_inc(exps_out.sem, 1)
                        for i in range(4):
                            act.wait_ge(nat_turned.sem, nat_turned.at(4 * r + i + 1))
                            src = slots[2 + i % 2]
                            if i == 0:
                                dst = a_mv[:, :, 0:64]
                                src = src.rearrange("p (a b) -> p a b", b=64)
                            else:
                                dst = (None, b_nat, k_nat, v_rw)[i][:, :, :].rearrange("p a b -> p (a b)")
                            act.activation(dst, src, ACT.Copy).then_inc(nat_copied.sem, 1)
                        act.wait_ge(mv_ready.sem, mv_ready.at(r + 1))
                        act.activation(a_mv[:, :, 64:128], slots[0].rearrange("p (a b) -> p a b", b=64),
                                       ACT.Copy).then_inc(mv_copied.sem, 1)
                        act.wait_ge(w_ready.sem, w_ready.at(r + 1))
                        act.activation(neg_w[:, :, :].rearrange("p a b -> p (a b)"), psf[:, 1024:1024 + UNITS * P],
                                       ACT.Copy, scale=-1.0).then_inc(w_copied.sem, 1)
                        act.wait_ge(chunk_ready.sem, chunk_ready.at(2 * r + 1))
                        act.activation(y_loc[:, :], slots[0], ACT.Copy).then_inc(yloc_copied.sem, 1)
                        act.wait_ge(chunk_ready.sem, chunk_ready.at(2 * r + 2))
                        act.activation(s_add[:, :, :].rearrange("p (t b) c -> p t b c", b=2), by_chunk(4),
                                       ACT.Copy).then_inc(sadd_copied.sem, 1)
                    act.preload_act_table_set("natural_log_exp_and_others")
                    for hp in range(2):
                        act.wait_ge(fin_v.sem, fin_v.at(4 * hp + 1))
                        act.activation(f[1][:, :], f[0][:, :], ACT.Square).then_inc(fin_a.sem, 1)
                        act.wait_ge(fin_ps.sem, fin_ps.at(3 * hp + 3))
                        link(act.activation(f[2][:, :], slots[1], ACT.Ln, bias=small[:, EPS_LNX:EPS_LNX + 1],
                                            scale=1.0 / HEAD))
                        act.activation(f[3][:, :], f[2][:, :], ACT.Exp, scale=-0.5).then_inc(fin_a.sem, 1)
                        act.wait_ge(fin_v.sem, fin_v.at(4 * hp + 3))
                        act.activation(hn_hi[:, 2 + hp, 0:nt], f[0][:, 0:nt], ACT.Copy).then_inc(fin_a.sem, 1)

                @block.tensor
                def _(pe):
                    for hp in range(2):
                        pe.wait_ge(rsq_ready.sem, rsq_ready.at(hp + 1))
                        for a, e in spans:
                            mm = pe.matmul(slots[hp][:, a:e], K_["ones64"], f[2 + hp][:, a:e], start=True, stop=True)
                        mm.then_inc(sums_ready.sem, 1)
                    pe.wait_ge(rsq_ready.sem, rsq_ready.at(4))
                    pe.wait_ge(tanh_done.sem, tanh_done.at(2))
                    pe.wait_ge(mix_loaded.sem, mix_loaded.at(48))
                    for r, (hp, d) in enumerate(ROUNDS):
                        if r >= 1:
                            pe.wait_ge(round_done.sem, round_done.at(r))
                        for i in range(2):
                            q = slice(64 * i + 32 * d, 64 * i + 32 * d + 32)
                            for a, e in spans:
                                mm = pe.matmul(slots[i][:, a:e], lora[q, hp * P:(hp + 1) * P], u[q, U_WA, a:e],
                                               start=True, stop=True)
                            mm.then_inc(lora_ready.sem, 1)
                        pe.wait_ge(features.sem, features.at(r + 1))
                        for i in range(4):
                            if i >= 2:
                                pe.wait_ge(nat_copied.sem, nat_copied.at(4 * r + i - 1))
                            for tt in range(NTT):
                                t = slice(tt * P, (tt + 1) * P)
                                src = (ar[:, tt, 0, :], bk_end[:, 0, t], bk_end[:, 1, t], u[:, V_OF + hp, t])[i]
                                mm = pe.transpose(slots[2 + i % 2][:, t], src, K_["ident"])
                            mm.then_inc(nat_turned.sem, 1)
                        for n in range(UNITS):
                            tt, j = n // 2, n % 2
                            t = slice(tt * P, (tt + 1) * P)
                            if n >= 4:
                                pe.wait_ge(wkv_masked.sem, wkv_masked.at(r * UNITS + n - 3))
                            for i in range(2):
                                mm = pe.matmul(ps[:, n % 4, i * 256:(i + 1) * 256], bk[hr(j), i, t],
                                               ar[hr(j), tt, :, :].rearrange("p a b -> p (a b)"), start=True, stop=True)
                            mm.then_inc(wkv_scores.sem, 1)
                        pe.wait_ge(wkv_masked.sem, wkv_masked.at((r + 1) * UNITS))
                        pe.wait_ge(nat_copied.sem, nat_copied.at(4 * r + 4))
                        X0, M0, S0 = r * GROUPS * LEVELS, r * GROUPS * (LEVELS - 1), r * GROUPS * (LEVELS - 1)
                        for li in range(LEVELS):
                            for g in range(GROUPS):
                                q = GROUPS * li + g
                                if li >= 1:
                                    pe.wait_ge(x_ready.sem, x_ready.at(X0 + q - GROUPS + 1))
                                if q >= 2:
                                    if q - 2 < GROUPS:
                                        pe.wait_ge(x_ready.sem, x_ready.at(X0 + q - 1))
                                    else:
                                        pe.wait_ge(lx_masked.sem, lx_masked.at(M0 + q - 1 - GROUPS))
                                for i in range(UG):
                                    n = g * UG + i
                                    mm = pe.matmul(ps[:, 6 + q % 2, i * P:(i + 1) * P], sc[:, n, 0, :],
                                                   K_["ident"] if li == 0 else x_inv[:, n, :], start=True, stop=True)
                                mm.then_inc(lx_ready.sem, 1)
                            if li == 0:
                                continue
                            for g in range(GROUPS):
                                pe.wait_ge(lx_masked.sem, lx_masked.at(M0 + GROUPS * (li - 1) + g + 1))
                                for i in range(UG):
                                    n = g * UG + i
                                    if li < LEVELS - 1:
                                        pe.matmul(ps[:, g, i * P:(i + 1) * P], xt_inv[:, n, :], lx[:, n, :], start=True,
                                                  stop=True)
                                    mm = pe.matmul(ps[:, 3 + g, i * P:(i + 1) * P], lx[:, n, :], xt_inv[:, n, :],
                                                   start=True, stop=True)
                                mm.then_inc(step_ready.sem, 1)
                        pe.wait_ge(x_ready.sem, x_ready.at(X0 + GROUPS * LEVELS))
                        for n in range(UNITS):
                            tt, j = n // 2, n % 2
                            mm = pe.matmul(slots[0][:, n * 64:(n + 1) * 64], sc[:, n, 2, :], v_rw[:, tt, hr(j)],
                                           start=True, stop=True)
                        mm.then_inc(mv_ready.sem, 1)
                        pe.wait_ge(mv_copied.sem, mv_copied.at(r + 1))
                        for n in range(UNITS):
                            mm = pe.matmul(psf[:, 1024 + n * P:1024 + (n + 1) * P], xt_inv[:, n, :], a_mv[:, n, :],
                                           start=True, stop=True)
                        mm.then_inc(w_ready.sem, 1)
                        pe.wait_ge(w_copied.sem, w_copied.at(r + 1))
                        for n in range(UNITS):
                            tt, j = n // 2, n % 2
                            t = slice(tt * P, (tt + 1) * P)
                            pe.matmul(slots[3][hr(j), t], neg_w[:, n, 0:64], sc[:, n, 1, :], start=True, stop=True)
                            pe.matmul(slots[0][hr(j), t], neg_w[:, n, 64:128], sc[:, n, 1, :], start=True, stop=False)
                            mm = pe.matmul(slots[0][hr(j), t], v_rw[:, tt, hr(j)], sc[:, n, 3, :], start=False, stop=True)
                        mm.then_inc(chunk_ready.sem, 1)
                        for c in range(NCH):
                            tt, b = c // 2, c % 2
                            cc = slice(tt * CH, (tt + 1) * CH)
                            for j in range(2):
                                n = 2 * tt + j
                                pe.matmul(ps[hr(j), 2 + b, cc], neg_w[hr(b), n, 0:64], b_nat[hr(b), tt, hr(j)],
                                          start=True, stop=True)
                                pe.matmul(ps[hr(j), 4 + b, cc], b_nat[hr(b), tt, hr(j)], neg_w[hr(b), n, 64:128],
                                          start=True, stop=False)
                                mm = pe.matmul(ps[hr(j), 4 + b, cc], k_nat[hr(b), tt, hr(j)], v_rw[hr(b), tt, hr(j)],
                                               start=False, stop=True)
                        mm.then_inc(chunk_ready.sem, 1)
                        pe.wait_ge(yloc_copied.sem, yloc_copied.at(r + 1))
                        pe.wait_ge(reff_ready.sem, reff_ready.at(r + 1))
                        pe.wait_ge(trans_ready.sem, trans_ready.at(r + 1))
                        for i, c in enumerate(ORDER[d]):
                            pe.wait_ge(state_ready.sem, state_ready.at(r * NCH + i + 1))
                            if i < NCH - 1:
                                for j in range(2):
                                    mm = pe.matmul(ps[hr(j), 2 + i % 2, 0:CH], trans[hr(j), c, :], state[hr(j), i % 2, :],
                                                   start=True, stop=True)
                                mm.then_inc(state_mm.sem, 1)
                            for j in range(2):
                                mm = pe.matmul(slots[0][hr(j), c * CH:(c + 1) * CH], state[hr(j), i % 2, :],
                                               r_eff[hr(j), c * CH:(c + 1) * CH], start=True, stop=True)
                        mm.then_inc(y_ready.sem, 1)
                    for hp in range(2):
                        if hp == 0:
                            pe.wait_ge(round_done.sem, round_done.at(4))
                        else:
                            pe.wait_ge(fin_v.sem, fin_v.at(4 * hp))
                        for a, e in spans:
                            pe.matmul(slots[3][:, a:e], lora[0:64, 256 + hp * P:256 + (hp + 1) * P], u[0:64, U_GD, a:e],
                                      start=True, stop=True)
                        for a, e in spans:
                            mm = pe.matmul(slots[0][:, a:e], K_["ones64"], y_sum[hp][:, a:e], start=True, stop=True)
                        mm.then_inc(fin_ps.sem, 1)
                        pe.wait_ge(fin_v.sem, fin_v.at(4 * hp + 2))
                        for a, e in spans:
                            mm = pe.matmul(slots[2][:, a:e], K_["ones64"], f[4][:, a:e], start=True, stop=True)
                        mm.then_inc(fin_ps.sem, 1)
                        pe.wait_ge(fin_a.sem, fin_a.at(3 * hp + 1))
                        for a, e in spans:
                            mm = pe.matmul(slots[1][:, a:e], K_["ones64"], f[1][:, a:e], start=True, stop=True)
                        mm.then_inc(fin_ps.sem, 1)

                @block.vector
                def _(dve):
                    own = [0]

                    def link(ins):
                        own[0] += 1
                        ins.then_inc(v_step.sem, 1)
                        dve.wait_ge(v_step.sem, v_step.at(own[0]))
                    a, b = COLS["w0"][0], COLS["a0"][1]
                    link(dve.tensor_scalar(half_bias[:, :], cols[l][:, a:b], 0.5, None, ALU.mult))
                    a, b = COLS["ka"]
                    link(dve.tensor_scalar(ka_rest[:, :], cols[l][:, a:b], -1.0, 1.0, ALU.mult, ALU.add))
                    for hp in range(2):
                        dve.tensor_scalar(kk_n[:, hp, :], u[:, K_OF + hp, :], col("kk", hp), None,
                                          ALU.mult).then_inc(kk_raw.sem, 1)
                    dve.wait_ge(tanh_done.sem, tanh_done.at(1))
                    dve.tensor_scalar(u[0:64, U_GD, :], u[0:64, U_GD, :], 0.5, 0.5, ALU.mult,
                                      ALU.add).then_inc(tanh_done.sem, 1)
                    for hp in range(2):
                        dve.wait_ge(rsq_ready.sem, rsq_ready.at(2 + hp + 1))
                        link(dve.tensor_tensor(kk_n[:, hp, :], kk_n[:, hp, :], f[6 + hp][:, :], ALU.mult))
                    dve.wait_ge(mix_loaded.sem, mix_loaded.at(48))

                    for r, (hp, d) in enumerate(ROUNDS):
                        k_u, r_u = u[:, K_OF + hp, :], u[:, R_OF + hp, :]
                        c3 = lambda x: x[:, :].rearrange("p (a b) -> p a b", b=CH)
                        t3 = lambda x: x.rearrange("p (a b) -> p a b", b=P)
                        dve.wait_ge(gate_tanh.sem, gate_tanh.at(2 * r + 1))
                        link(dve.tensor_scalar(f[2][:, :], f[0][:, :], 0.5, 0.5, ALU.mult, ALU.add))
                        link(dve.tensor_tensor_scan(f[3][:, :], scan_ones[:, :], f[2][:, :], 0.0, ALU.mult, ALU.add))
                        total = f[3][:, CH - 1::CH].rearrange("p (a b) -> p a b", b=1).broadcast_to([P, NCH, CH])
                        link(dve.tensor_tensor(f[4][:, :], f[3][:, :], f[2][:, :], ALU.subtract))
                        mm = dve.tensor_tensor(c3(f[5]), total, c3(f[3]), ALU.subtract)
                        if d == 1:
                            mm = dve.tensor_tensor(c3(f[6]), total, c3(f[4]), ALU.subtract)
                        mm.then_inc(exps_in.sem, 1)
                        dve.wait_ge(gate_tanh.sem, gate_tanh.at(2 * r + 2))
                        link(dve.tensor_scalar(f[0][:, :], f[1][:, :], 0.5, 0.5, ALU.mult, ALU.add))
                        dve.tensor_tensor(f[7][:, :], f[0][:, :], kk_n[:, hp, :], ALU.mult)
                        link(dve.tensor_scalar(f[1][:, :], f[0][:, :], col("ka", hp), ka_rest[:, hp:hp + 1], ALU.mult,
                                               ALU.add))
                        link(dve.tensor_tensor(f[1][:, :], f[1][:, :], k_u, ALU.mult))
                        if d == 0:
                            link(dve.tensor_copy(kd_sum[hp][:, :], f[1][:, :]))
                        else:
                            link(dve.tensor_tensor(kd_sum[hp][:, :], kd_sum[hp][:, :], f[1][:, :], ALU.add))
                        dve.wait_ge(exps_out.sem, exps_out.at(5 * r + 1))
                        dve.tensor_tensor(ar[:, :, 0, :], ar[:, :, 0, :], t3(kk_n[:, hp, :]), ALU.mult)
                        dve.wait_ge(exps_out.sem, exps_out.at(5 * r + 2))
                        dve.tensor_tensor(ar[:, :, 1, :], ar[:, :, 1, :], t3(r_u), ALU.mult)
                        dve.wait_ge(exps_out.sem, exps_out.at(5 * r + 3))
                        link(dve.tensor_tensor(bk[:, 1, :], bk[:, 0, :], f[1][:, :], ALU.mult))
                        dve.tensor_tensor(bk[:, 0, :], bk[:, 0, :], f[7][:, :], ALU.mult)
                        dve.wait_ge(exps_out.sem, exps_out.at(5 * r + 4))
                        link(dve.tensor_tensor(bk_end[:, 1, :], bk_end[:, 0, :], f[1][:, :], ALU.mult))
                        dve.tensor_tensor(bk_end[:, 0, :], bk_end[:, 0, :], f[7][:, :], ALU.mult).then_inc(features.sem, 1)
                        dve.wait_ge(features.sem, features.at(r + 1))
                        dve.wait_ge(exps_out.sem, exps_out.at(5 * r + 5))
                        i2 = K_["ident2"][:, 0:CH].rearrange("p (a b) -> p a b", a=1).broadcast_to([P, NCH, CH])
                        cd = chunk_decay[:, :].rearrange("p (a b) -> p a b", b=1).broadcast_to([P, NCH, CH])
                        dve.tensor_tensor(decay_diag[:, :, :], i2, cd, ALU.mult)
                        for n in range(UNITS):
                            dve.wait_ge(wkv_scores.sem, wkv_scores.at(r * UNITS + n + 1))
                            dve.tensor_tensor(sc[:, n, :, :].rearrange("p a b -> p (a b)"), ps[:, n % 4, :],
                                              masks[:, d, 0:4, :].rearrange("p a b -> p (a b)"),
                                              ALU.mult).then_inc(wkv_masked.sem, 1)
                        dve.wait_ge(wkv_masked.sem, wkv_masked.at((r + 1) * UNITS))
                        M0, S0 = r * GROUPS * (LEVELS - 1), r * GROUPS * (LEVELS - 1)
                        eye = K_["ident"].rearrange("p (a b) -> p a b", a=1).broadcast_to([P, UG, P])

                        def mask(i):
                            return masks[:, d, i:i + 1, :].broadcast_to([P, UG, P])
                        for g in range(GROUPS):
                            gs = slice(g * UG, (g + 1) * UG)
                            dve.tensor_tensor(xt_inv[:, gs, :], sc[:, gs, 0, :], mask(5), ALU.mult)
                            dve.wait_ge(lx_ready.sem, lx_ready.at(r * GROUPS * LEVELS + g + 1))
                            link(dve.tensor_tensor(x_inv[:, gs, :], ps[:, 6 + g % 2, :].rearrange("p (a b) -> p a b", b=P),
                                                   mask(4), ALU.mult))
                            dve.tensor_tensor(xt_inv[:, gs, :], xt_inv[:, gs, :], eye, ALU.add)
                            dve.tensor_tensor(x_inv[:, gs, :], x_inv[:, gs, :], eye, ALU.add).then_inc(x_ready.sem, 1)
                        for li in range(1, LEVELS):
                            for g in range(GROUPS):
                                q = GROUPS * li + g
                                gs = slice(g * UG, (g + 1) * UG)
                                dve.wait_ge(lx_ready.sem, lx_ready.at(r * GROUPS * LEVELS + q + 1))
                                dve.tensor_tensor(lx[:, gs, :], ps[:, 6 + q % 2, :].rearrange("p (a b) -> p a b", b=P),
                                                  mask(5 + li), ALU.mult).then_inc(lx_masked.sem, 1)
                            for g in range(GROUPS):
                                gs = slice(g * UG, (g + 1) * UG)
                                dve.wait_ge(step_ready.sem, step_ready.at(S0 + GROUPS * (li - 1) + g + 1))
                                dve.wait_ge(x_ready.sem, x_ready.at(r * GROUPS * LEVELS + GROUPS * (li - 1) + g + 1))
                                if li < LEVELS - 1:
                                    dve.tensor_tensor(x_inv[:, gs, :], x_inv[:, gs, :],
                                                      ps[:, g, :].rearrange("p (a b) -> p a b", b=P), ALU.subtract)
                                dve.tensor_tensor(xt_inv[:, gs, :], xt_inv[:, gs, :],
                                                  ps[:, 3 + g, :].rearrange("p (a b) -> p a b", b=P),
                                                  ALU.subtract).then_inc(x_ready.sem, 1)
                        dve.memset(state[:, 0, :], 0.0).then_inc(state_ready.sem, 1)
                        dve.wait_ge(chunk_ready.sem, chunk_ready.at(2 * r + 1))
                        dve.tensor_tensor(t3(r_eff[:, :]), t3(slots[3]), ar[:, :, 1, :], ALU.add).then_inc(reff_ready.sem, 1)
                        dve.wait_ge(chunk_ready.sem, chunk_ready.at(2 * r + 2))
                        dve.tensor_tensor(trans[:, :, :].rearrange("p (t b) c -> p t b c", b=2), by_chunk(2),
                                          decay_diag[:, :, :].rearrange("p (t b) c -> p t b c", b=2),
                                          ALU.add).then_inc(trans_ready.sem, 1)
                        dve.wait_ge(sadd_copied.sem, sadd_copied.at(r + 1))
                        for i, c in enumerate(ORDER[d][:-1]):
                            dve.wait_ge(state_mm.sem, state_mm.at(r * (NCH - 1) + i + 1))
                            dve.tensor_tensor(state[:, (i + 1) % 2, :], ps[:, 2 + i % 2, 0:CH], s_add[:, c, :],
                                              ALU.add).then_inc(state_ready.sem, 1)
                        dve.wait_ge(y_ready.sem, y_ready.at(r + 1))
                        dve.wait_ge(yloc_copied.sem, yloc_copied.at(r + 1))
                        if d == 0:
                            dve.tensor_tensor(y_sum[hp][:, :], slots[0], y_loc[:, :], ALU.add).then_inc(round_done.sem, 1)
                        else:
                            link(dve.tensor_tensor(y_loc[:, :], slots[0], y_loc[:, :], ALU.add))
                            dve.tensor_tensor(y_sum[hp][:, :], y_sum[hp][:, :], y_loc[:, :],
                                              ALU.add).then_inc(round_done.sem, 1)
                        dve.wait_ge(round_done.sem, round_done.at(r + 1))

                    for hp in range(2):
                        if hp == 1:
                            dve.wait_ge(fin_v.sem, fin_v.at(4))
                        dve.wait_ge(fin_ps.sem, fin_ps.at(3 * hp + 1))
                        dve.scalar_tensor_tensor(out=f[0][:, :], in0=slots[0], scalar=-1.0 / HEAD, in1=y_sum[hp][:, :],
                                                 op0=ALU.mult, op1=ALU.add).then_inc(fin_v.sem, 1)
                        dve.scalar_tensor_tensor(out=f[4][:, :], in0=u[:, R_OF + hp, :], scalar=col("rk", hp),
                                                 in1=kd_sum[hp][:, :], op0=ALU.mult, op1=ALU.mult).then_inc(fin_v.sem, 1)
                        dve.wait_ge(fin_ps.sem, fin_ps.at(3 * hp + 2))
                        link(dve.tensor_tensor(f[5][:, :], slots[2], u[:, V_OF + hp, :], ALU.mult))
                        dve.wait_ge(fin_a.sem, fin_a.at(3 * hp + 2))
                        link(dve.scalar_tensor_tensor(out=f[0][:, :], in0=f[0][:, :], scalar=col("lg", hp),
                                                      in1=f[3][:, :], op0=ALU.mult, op1=ALU.mult))
                        link(dve.scalar_tensor_tensor(out=f[0][:, :], in0=f[0][:, :], scalar=col("lb", hp),
                                                      in1=f[5][:, :], op0=ALU.add, op1=ALU.add))
                        dve.tensor_tensor(f[0][:, :], f[0][:, :], slots[3], ALU.mult).then_inc(fin_v.sem, 1)
                        dve.wait_ge(fin_a.sem, fin_a.at(3 * hp + 3))
                        dve.tensor_tensor(hn_lo[:, 2 + hp, 0:nt], f[0][:, 0:nt], hn_hi[:, 2 + hp, 0:nt].bitcast(F32),
                                          ALU.subtract).then_inc(fin_v.sem, 1)
                    own_v[0] = own[0]
            LINKS_A = 1 + 2 + 2
            for x, n in ((mix_loaded, 48), (a_step, LINKS_A), (v_step, own_v[0]),
                         (tanh_done, 2), (kk_raw, 2), (rsq_ready, 4), (sums_ready, 2), (lora_ready, 8), (gate_tanh, 8),
                         (exps_in, 4), (exps_out, 20), (features, 4), (nat_turned, 16), (nat_copied, 16),
                         (wkv_scores, 4 * UNITS), (wkv_masked, 4 * UNITS), (lx_ready, 4 * GROUPS * LEVELS),
                         (lx_masked, 4 * GROUPS * (LEVELS - 1)), (step_ready, 4 * GROUPS * (LEVELS - 1)),
                         (x_ready, 4 * GROUPS * LEVELS), (mv_ready, 4), (mv_copied, 4), (w_ready, 4), (w_copied, 4),
                         (chunk_ready, 8), (reff_ready, 4), (yloc_copied, 4), (trans_ready, 4), (sadd_copied, 4),
                         (state_ready, 4 * NCH), (state_mm, 4 * (NCH - 1)), (y_ready, 4), (round_done, 4),
                         (fin_ps, 6), (fin_v, 8), (fin_a, 6)):
                x.phase_end(n)
        own_v = [0]

        def store():
            with nc.Block() as block:
                @block.sync
                def _(sp):
                    sp.dma_start(A["yT"], h[:, :, LAT]).then_inc(stored.sem, 16)
                    sp.wait_ge(stored.sem, 16)

        setup()
        for l in range(DEPTH):
            last = l == DEPTH - 1
            layer[0] = l
            first = l == 0
            ffn(l, 0, NT, (0, MOD_FIRST, (3, 2), (1, 0)) if first else None)
            in_proj(l)
            qkv(l)
            attention(l, SEQ if last else NT)
            rwkv(l, SEQ if last else NT)
            out_proj(l, SEQ if last else NT)
            ffn(l, 1, SEQ if last else NT, None if last else (l + 1, 0, (3, 3), (3, 3)), more=not last)
        store()


def tiles_of(w, rows=P):
    r, c = w.shape[-2:]
    w = w.reshape(w.shape[:-2] + (r // P, P, c // P, P))
    n = w.ndim
    return np.ascontiguousarray(np.moveaxis(w, [n - 2, n - 3, n - 4, n - 1], [n - 4, n - 3, n - 2, n - 1]))


def blocks(w):
    t = tiles_of(w)
    return t.reshape(t.shape[:-2] + (-1,))


def layout(x, c, ctx, c_ctx, w_mod, b_mod, norm_ffn1, ffn1_w_gu, ffn1_w_down, norm_mix, w_in, w_out,
           mla_q_norm, mla_kv_norm, mla_w_uq, mla_w_ukv, mla_qn, mla_kn,
           rwkv_shift, rwkv_w0, rwkv_w2, rwkv_a0, rwkv_a2, rwkv_g2, rwkv_k_k, rwkv_k_a, rwkv_r_k,
           rwkv_lnx_g, rwkv_lnx_b, na_qn, na_kn, na_rpb, gqa_qn, gqa_kn,
           norm_ffn2, ffn2_w_gu, ffn2_w_down):
    L = DEPTH
    f = np.float32

    def colsof(v):
        return v.reshape(L, -1, P).transpose(0, 2, 1)
    A = {}
    xt = np.concatenate([x[0], ctx[0]], 0)
    A["xT"] = np.ascontiguousarray(xt.T.reshape(KD, P, NT).transpose(1, 0, 2))
    A["cT"] = np.ascontiguousarray(np.stack([c[0], c_ctx], 1).reshape(KD, P, 2).transpose(1, 0, 2)).reshape(P, 2 * KD)
    A["wmod"] = blocks(w_mod)
    gus = []
    for w in (ffn1_w_gu, ffn2_w_gu):
        g, up = blocks(w[:, :, :D_FF]), blocks(w[:, :, D_FF:])
        gus.append(np.stack([g, up], 2).reshape(L, 2 * NF, P, D_MODEL))
    A["wgu"] = np.stack(gus, 1)
    A["wdn"] = np.stack([blocks(w.reshape(L, 2, NFH * P, D_MODEL)) for w in (ffn1_w_down, ffn2_w_down)], 1)

    z96 = np.zeros((L, D_MODEL, 96), f)
    z64 = np.zeros((L, D_MODEL, 64), f)
    r0, n0 = 416, 1376
    g0 = n0 + 768
    gq = w_in[:, :, g0:g0 + 256].reshape(L, D_MODEL, 4, HEAD)[:, :, [0, 2, 1, 3]].reshape(L, D_MODEL, 256)
    w = np.concatenate([w_in[:, :, 0:416], z96, w_in[:, :, r0:r0 + 960], z64, w_in[:, :, n0:n0 + 512], gq,
                        w_in[:, :, g0 + 256:g0 + 384], w_in[:, :, n0 + 512:n0 + 768],
                        w_in[:, :, g0 + 384:g0 + 512]], 2)
    A["win"] = blocks(w)
    A["wout"] = blocks(w_out)

    sh = np.concatenate([rwkv_shift, np.zeros((L, 2, 64), f)], 2)
    two = lambda v: np.concatenate([v, v], 1)
    pad96 = lambda v: np.concatenate([v, np.zeros((L, 32), f)], 1)
    parts = {"n1": norm_ffn1, "nm": norm_mix, "n2": norm_ffn2, "bmod": b_mod, "mq": mla_q_norm, "mkv": mla_kv_norm,
             "mu0": sh[:, 0], "mu1": sh[:, 1], "w0": rwkv_w0.reshape(L, -1), "a0": rwkv_a0.reshape(L, -1),
             "kk": rwkv_k_k, "ka": rwkv_k_a, "rk": rwkv_r_k.reshape(L, -1), "lg": rwkv_lnx_g, "lb": rwkv_lnx_b,
             "nq": two(na_qn), "nk": two(na_kn), "gq": two(gqa_qn), "gk": two(gqa_kn), "mqn": pad96(mla_qn),
             "mkn": pad96(mla_kn)}
    A["cols"] = np.ascontiguousarray(np.concatenate([colsof(parts[n]) for n in COLS], 2).transpose(1, 0, 2))

    uq = mla_w_uq.reshape(L, 2, P, 4 * MLA_D).transpose(0, 2, 1, 3)
    ukv = mla_w_ukv.reshape(L, P, 4, 128)
    uk = np.concatenate([ukv[..., :64], np.zeros((L, P, 4, 32), f)], 3).reshape(L, P, 4 * MLA_D)
    uv = ukv[..., 64:].reshape(L, P, 256)
    A["mla"] = np.ascontiguousarray(np.concatenate([uq.reshape(L, P, -1), uk, uv], 2))
    A["lora"] = np.ascontiguousarray(np.concatenate([
        np.concatenate([rwkv_w2.reshape(L, 64, 256), rwkv_a2.reshape(L, 64, 256)], 1),
        np.concatenate([rwkv_g2, np.zeros((L, 64, 256), f)], 1)], 2))

    B = np.full((L, P, 4, 14, GRID_W), MASKED, f)
    cq = np.arange(GRID_W)
    c0 = np.clip(cq - 8, 0, GRID_W - 16)
    for ro in range(2):
        for q in range(GRID_W):
            ks = np.arange(c0[q], c0[q] + 16)
            dr = np.arange(1, 15) - ro
            B[:, ro * 64 + q, :, :, ks] = na_rpb[:, :, dr][:, :, :, ks - q + 15].transpose(3, 0, 1, 2)
    A["bias"] = B.reshape(L, P, 4, 14 * GRID_W)
    A.update(constants())
    return A


def constants():
    f = np.float32
    eye = np.eye(P, dtype=f)
    one64 = np.kron(np.eye(2), np.ones((64, 64))).astype(f)

    def rot(widths, offset=0):
        R = np.zeros((P, P))
        at = offset
        for w in widths:
            hf = w // 2
            for j in range(hf):
                R[at + j, at + hf + j] = -1
                R[at + hf + j, at + j] = 1
            at += w
        return np.ascontiguousarray(R.T).astype(f)
    sel = np.zeros((P, P), f)
    sel[0:32, 64:96] = np.eye(32)
    ident2 = np.zeros((P, P), f)
    ident2[:, 0:64] = np.concatenate([np.eye(64)] * 2, 0)
    mats = {"ident": eye, "ones": np.ones((P, P), f), "ones64": one64, "rot_g": rot([32] * 4),
            "rot_m": rot([16, 16], 64), "sel_kr": sel, "ident2": ident2}
    A = {"consts": np.ascontiguousarray(np.stack([mats[n] for n in CONSTS], 1))}
    small = np.zeros((P, 16), f)
    small[:, 0:5] = np.array([1e-6, np.log(HEAD ** -0.5), np.log(MLA_D ** -0.5), 1e-12, 64e-5])
    A["small"] = small

    t = np.arange(SEQ)
    pos = {"row": (t // GRID_W).astype(f), "col": (t % GRID_W).astype(f)}

    def table(axes):
        c, s = [], []
        for axis, w in axes:
            hf = w // 2
            inv = (f(10000.0) ** (-np.arange(hf, dtype=f) / f(hf))).astype(f)
            ang = (pos[axis][None, :] * inv[:, None]).astype(f)
            c += [np.cos(ang)] * 2
            s += [np.sin(ang)] * 2
        return np.concatenate(c, 0).astype(f), np.concatenate(s, 0).astype(f)
    cg, sg = table([("row", 32), ("col", 32)] * 2)
    cm, sm = table([("row", 16), ("col", 16)])
    o, z = np.ones((64, SEQ), f), np.zeros((64, SEQ), f)
    pad = np.zeros((32, SEQ), f)
    A["rope"] = np.ascontiguousarray(np.stack([cg, sg, np.concatenate([o, cm, pad]), np.concatenate([z, sm, pad])], 1))

    i = np.arange(P)
    same = (i[:, None] // CH) == (i[None, :] // CH)
    scan = np.ones((P, NT), f)
    scan[:, ::CH] = 0
    A["scan"] = scan
    M = []
    for d in range(2):
        before = (i[:, None] < i[None, :]) if d == 0 else (i[:, None] > i[None, :])
        strict, incl = same & before, same & (before | (i[:, None] == i[None, :]))
        lv = []
        for m in (1, 2, 4, 8, 16, 32):
            blk = (i[:, None] // (2 * m)) == (i[None, :] // (2 * m))
            hi_, lo_ = (i // m) % 2 == 1, (i // m) % 2 == 0
            q = blk & (hi_[:, None] & lo_[None, :] if d == 0 else lo_[:, None] & hi_[None, :])
            lv.append(q)
        M.append(np.stack([strict, incl, strict, incl, -1.0 * lv[0], -1.0 * lv[0].T] + lv[1:]))
    A["masks"] = np.ascontiguousarray(np.stack(M).astype(f).transpose(2, 0, 1, 3))
    return A


def kernel(**inputs):
    import concourse.bacc as bacc
    from concourse.bass_utils import run_bass_kernel_spmd

    arrays = layout(**{k: np.asarray(v) for k, v in inputs.items()})
    nc = bacc.Bacc("TRN2", target_bir_lowering=False, num_devices=1)
    A = {n: nc.dram_tensor(n, a.shape, mybir.dt.from_np(a.dtype), kind="ExternalInput").ap()
         for n, a in arrays.items()}
    A["yT"] = nc.dram_tensor("yT", (P, KD, SEQ), F32, kind="ExternalOutput").ap()
    build_trunk(nc, A)
    r = run_bass_kernel_spmd(nc, [arrays], core_ids=[0])
    y = r.results[0]["yT"]
    return np.ascontiguousarray(y.transpose(2, 1, 0)).reshape(1, SEQ, D_MODEL)
```

```python
from contextlib import ExitStack

import numpy as np
import concourse.bass as bass
from concourse import mybir

F32 = mybir.dt.float32
F32R = mybir.dt.float32r
ACT = mybir.ActivationFunctionType
ALU = mybir.AluOpType
AXX = mybir.AxisListType.X

P = 128
D_MODEL, SEQ, CTX, DEPTH, D_FF = 1024, 512, 256, 2, 2816
GRID_W, HEAD = 64, 64
KD = D_MODEL // P
NT = SEQ + CTX
LAT, CTXT = slice(0, SEQ), slice(SEQ, NT)
NF = D_FF // P
NFH = NF // 2
NTT = NT // P
LT_TILES = SEQ // P
N_MOD = 9 * KD
N_IN = 22
MLA_D, MLA_NOPE, MLA_ROPE = 96, 64, 32
CH = 64
NCH = NT // CH
G_DECAY = float(np.exp(-0.5))
MASKED = -1e30

U_QC, U_KV, U_KR, U_RW, U_WA, U_GD, U_NQ, U_NK, U_GQ, U_GK, U_V = 0, 2, 3, 4, 10, 11, 12, 14, 16, 18, 19
U_TILES = 22

COLS = {}
_n = 0
for _name, _w in [("n1", 8), ("nm", 8), ("n2", 8), ("bmod", 72), ("mq", 2), ("mkv", 1), ("mu0", 8), ("mu1", 8),
                  ("w0", 4), ("a0", 4), ("kk", 2), ("ka", 2), ("rk", 2), ("lg", 2), ("lb", 2), ("nq", 1),
                  ("nk", 1), ("gq", 1), ("gk", 1), ("mqn", 1), ("mkn", 1)]:
    COLS[_name] = (_n, _n + _w)
    _n += _w
NCOL = _n
CONSTS = ["ident", "ones", "ones64", "rot_g", "rot_m", "sel_kr", "ident2"]


class Signal:

    def __init__(self, sem, first=0):
        self.sem, self.base = sem, first

    def at(self, n):
        return self.base + n

    def phase_end(self, n):
        self.base += n


def build_trunk(nc, A):
    with ExitStack() as ctx:
        start = (nc.sbuf_base + 63) // 64 * 64
        R_H = start
        R_N = R_H + KD * NT * 4
        R_G = R_N + 2 * KD * NT * 4
        R_W = R_G + 2 * NFH * NT * 4
        R_T = R_W + 6 * NFH * P * 4
        arena_size = nc.sbuf_usable_end - start
        ctx.enter_context(nc.sbuf_tensor("arena", [P, (arena_size - 64) // 4], F32))
        place = {"T": R_T}

        def at(name, shape, off, dt=F32):
            return nc.alloc_sbuf_tensor_at(name, shape, dt, offset=off)

        def tmp(name, shape, dt=F32):
            n = 4 * int(np.prod(shape[1:]))
            t = at(name, shape, place["T"], dt)
            place["T"] += (n + 31) // 32 * 32
            assert place["T"] <= start + arena_size, (name, place["T"])
            return t

        TOK = NT * 4
        h = at("h", [P, KD, NT], R_H)
        hn_hi = at("hn_hi", [P, KD, NT], R_N, F32R)
        hn_lo = at("hn_lo", [P, KD, NT], R_N + KD * TOK, F32R)
        mix = at("mix", [P, KD, NT], R_N)
        g_hi = at("g_hi", [P, NFH, NT], R_G, F32R)
        g_lo = at("g_lo", [P, NFH, NT], R_G + NFH * TOK, F32R)
        u = at("u", [P, U_TILES, NT], R_G)
        v_nat = at("v_nat", [P, NTT, 3 * P], R_N + KD * TOK)
        rstd = at("rstd", [P, NT], R_G + 2 * TOK)
        lnv = at("lnv", [P, NT], R_G + 3 * TOK)
        scaled = at("scaled", [P, 2, NT], R_G + 4 * TOK)
        moded = at("moded", [P, 2, NT], R_G + 6 * TOK)
        WS = NFH * P * 4
        raw = [at(f"raw{s}", [P, NFH * P], R_W + s * WS) for s in range(2)]
        w_hi = [at(f"w_hi{s}", [P, NFH, P], R_W + (2 + s) * WS, F32R) for s in range(2)]
        w_lo = [at(f"w_lo{s}", [P, NFH, P], R_W + (4 + s) * WS, F32R) for s in range(2)]
        const = tmp("const", [P, len(CONSTS), P])
        K_ = {n: const[:, i, :] for i, n in enumerate(CONSTS)}
        cols_all = tmp("cols", [P, DEPTH, NCOL])
        mod_all = tmp("mod", [P, DEPTH, 2, N_MOD])
        cols, mod = [cols_all[:, i, :] for i in range(DEPTH)], [mod_all[:, i, :, :] for i in range(DEPTH)]
        moda = tmp("moda", [P, 2, KD])
        small = tmp("small", [P, 16])
        c_raw = tmp("c_raw", [P, KD * 2])
        cond = tmp("cond", [P, 3, KD * 2])
        keep = tmp("keep", [P, KD])
        T0 = place["T"]
        sum_sq = tmp("sum_sq", [P, NT])
        tanh_g = tmp("tanh_g", [P, NT])
        silu_g = tmp("silu_g", [P, NT])
        glu = tmp("glu", [P, NT])
        h_sq = tmp("h_sq", [P, NT])
        MOD_SLOTS = 3
        mod_row = at("mod_row", [2, MOD_SLOTS * P], place["T"])
        place["T"] += 4 * MOD_SLOTS * P
        w_mod = [tmp(f"w_mod{i}", [P, D_MODEL]) for i in range(MOD_SLOTS)]
        MOD_FIRST = 16
        w_mod_first = at("w_mod_first", [P, MOD_FIRST, D_MODEL], R_N)
        mod_row_first = at("mod_row_first", [2, MOD_FIRST * P], R_T - MOD_FIRST * P * 4)

        ps = ctx.enter_context(nc.psum_tensor("ps", [P, 8, 512], F32))
        psf = ps[:, :, :].rearrange("p a b -> p (a b)")
        ps_slot = [psf[:, 0:NT], psf[:, 1024:1024 + NT]]

        def sem(name, first=0):
            return Signal(ctx.enter_context(nc.semaphore(name)), first)

        raw_loaded = [sem(f"raw_loaded{s}") for s in range(2)]
        hi_ready = [sem(f"w_hi_ready{s}") for s in range(2)]
        lo_ready = [sem(f"w_lo_ready{s}", 1) for s in range(2)]
        block_done = [sem(f"block_done{s}", 1) for s in range(2)]
        evacuated = [sem(f"psum_evacuated{s}", 1) for s in range(2)]
        setup_loaded = sem("setup_loaded")
        cond_step, cond_ready = sem("cond_step"), sem("cond_ready")
        mod_ready = sem("mod_ready")
        mod_loaded = [sem(f"w_mod_loaded{i}") for i in range(MOD_SLOTS)]
        mod_used = sem("w_mod_used", MOD_SLOTS)
        mod_first_ready = sem("mod_first_rows_ready")
        mod_copied, mod_turned = sem("mod_rows_copied"), sem("mod_rows_turned")
        sum_ready = sem("sum_of_squares_ready")
        sq_summed, h_squared = sem("h_sq_summed"), sem("h_squared")
        ms_ready, rstd_ready, ln_done = sem("ms_ready"), sem("rstd_ready"), sem("ln_done")
        scaled_ready, moded_ready, hn_hi_ready, hn_lo_ready = (sem("scaled_ready"), sem("moded_ready"),
                                                               sem("hn_hi_ready"), sem("hn_lo_ready"))
        moda_ready = sem("moda_ready")
        tanh_ready, silu_ready, glu_ready, g_hi_ready, g_lo_ready = (sem("tanh_ready"), sem("silu_ready", 1),
                                                                     sem("glu_ready", 1), sem("g_hi_ready"),
                                                                     sem("g_lo_ready"))
        stored = sem("out_stored")

        EPS, LN_Q64, LN_Q96, EPS_KK, EPS_LNX = 0, 1, 2, 3, 4
        SMALL = [1e-6, float(np.log(HEAD ** -0.5)), float(np.log(MLA_D ** -0.5)), 1e-12, 64e-5]

        def col(name, j=0, rows=slice(0, P)):
            a = COLS[name][0] + j
            return cols_all[rows, layer[0], a:a + 1]
        layer = [0]

        TWO = (("lat", LAT, 0), ("ctx", CTXT, 1))

        def load_block(sp, s, src, kt, use):
            sp.wait_ge(lo_ready[s].sem, lo_ready[s].at(use))
            sp.dma_start(raw[s][:, 0:kt * P], src).then_inc(raw_loaded[s].sem, 16)

        def next_loads(sp, srcs, kt, use):
            for s, src in enumerate(srcs):
                load_block(sp, s, src, kt, use)

        def split_hi(act, s, kt, use):
            act.wait_ge(raw_loaded[s].sem, 16 * use + raw_loaded[s].at(16))
            act.wait_ge(block_done[s].sem, block_done[s].at(use))
            act.activation(w_hi[s][:, 0:kt, :].rearrange("p k n -> p (k n)"), raw[s][:, 0:kt * P],
                           ACT.Copy).then_inc(hi_ready[s].sem, 1)

        def split_lo(dve, s, kt, use):
            dve.wait_ge(hi_ready[s].sem, hi_ready[s].at(use + 1))
            dve.tensor_tensor(w_lo[s][:, 0:kt, :].rearrange("p k n -> p (k n)"), raw[s][:, 0:kt * P],
                              w_hi[s][:, 0:kt, :].rearrange("p k n -> p (k n)").bitcast(F32),
                              ALU.subtract).then_inc(lo_ready[s].sem, 1)

        def stream_end(pairs):
            for s in range(2):
                raw_loaded[s].phase_end(16 * pairs)
                for x in (hi_ready[s], lo_ready[s], block_done[s]):
                    x.phase_end(pairs)

        def product(pe, s, kt, out, mov_hi, mov_lo, nt, tile_ready=None):
            spans = [(0, 512), (512, NT)] if nt == NT else [(0, 512)]
            for k in range(kt):
                if tile_ready is not None:
                    pe.wait_ge(tile_ready.sem, tile_ready.at(k + 1))
                for w, m in ((w_hi[s], mov_hi), (w_hi[s], mov_lo), (w_lo[s], mov_hi)):
                    for a, b in spans:
                        mm = pe.matmul(out[:, a:b], w[:, k, :], m[:, k, a:b],
                                       start=(k == 0 and w is w_hi[s] and m is mov_hi),
                                       stop=(k == kt - 1 and w is w_lo[s]))
            mm.then_inc(block_done[s].sem, 1)

        def mod_rows(pe, slots, use):
            for m in range(slots):
                pe.wait_ge(mod_loaded[m].sem, use(m) * 16 + mod_loaded[m].at(16))
                for k in range(KD):
                    mm = pe.matmul(ps[0:2, 4, m * P:(m + 1) * P], cond[:, 2, 2 * k:2 * k + 2],
                                   w_mod[m][:, k * P:(k + 1) * P], start=(k == 0), stop=(k == KD - 1))
                mm.then_inc(mod_used.sem, 1)

        def mod_turn(pe, slots, bank, column, copied):
            pe.wait_ge(mod_copied.sem, copied)
            for m in range(slots):
                mm = pe.matmul(ps[:, bank, bass.ds((column + m) * 2, 2)], mod_row[0:2, m * P:(m + 1) * P],
                               K_["ident"][0:2, 0:2], start=True, stop=True)
            mm.then_inc(mod_turned.sem, 1)

        def mod_copy(dve, slots, ready):
            dve.wait_ge(mod_used.sem, ready)
            dve.tensor_copy(mod_row[:, 0:slots * P], ps[0:2, 4, 0:slots * P]).then_inc(mod_copied.sem, 1)

        def mod_finish(dve, l, bank, j0, j1, n):
            a = COLS["bmod"][0]
            for w in range(2):
                dve.tensor_tensor(mod[l][:, w, j0:j1],
                                  ps[:, bank, 2 * j0:2 * j1].rearrange("p (j w) -> p w j", w=2)[:, w, :],
                                  cols[l][:, a + j0:a + j1], ALU.add).then_inc(mod_ready.sem, 1)
            n += 2
            dve.wait_ge(mod_ready.sem, mod_ready.at(n))
            for part in (2, 8):
                b0, b1 = max(j0, part * KD), min(j1, (part + 1) * KD)
                if b0 < b1:
                    v = mod[l][:, :, b0:b1]
                    dve.tensor_scalar(v, v, 0.5, None, ALU.mult).then_inc(mod_ready.sem, 1)
                    n += 1
            dve.wait_ge(mod_ready.sem, mod_ready.at(n))
            return n

        FIRST_GROUP = 4
        FIRST_LOADS = ((0, 4), (4, 8), (8, MOD_FIRST))

        def setup():
            n_setup = [0]
            with nc.Block() as block:
                @block.sync
                def _(sp):
                    sp.dma_start(c_raw[:, :], A["cT"]).then_inc(setup_loaded.sem, 16)
                    sp.dma_start(cols_all[:, :, :], A["cols"]).then_inc(setup_loaded.sem, 16)
                    for i, (a, b) in enumerate(FIRST_LOADS):
                        sp.dma_start(w_mod_first[:, a:b, :],
                                     A["wmod"][0, a:b].rearrange("j p n -> p j n")).then_inc(mod_loaded[i].sem, 16)
                    for s in range(2):
                        sp.dma_start(raw[s][:, 0:KD * P], A["wgu"][0, 0, s]).then_inc(raw_loaded[s].sem, 16)
                    sp.wait_ge(setup_loaded.sem, 80)

                @block.gpsimd
                def _(pool):
                    for x in lo_ready + block_done + evacuated + [silu_ready, glu_ready]:
                        pool.sem_inc(x.sem, 1)
                    pool.sem_inc(mod_used.sem, MOD_SLOTS)
                    pool.wait_ge(setup_loaded.sem, 80)
                    pool.tensor_tensor(sum_sq[:, :], h[:, 0, :], h[:, 0, :], ALU.mult).then_inc(sq_summed.sem, 1)
                    for k in range(1, KD - 1):
                        pool.tensor_tensor(h_sq[:, :], h[:, k, :], h[:, k, :], ALU.mult).then_inc(h_squared.sem, 1)
                        pool.wait_ge(h_squared.sem, k)
                        pool.wait_ge(sq_summed.sem, k)
                        pool.tensor_tensor(sum_sq[:, :], sum_sq[:, :], h_sq[:, :], ALU.add).then_inc(sq_summed.sem, 1)
                        if k < KD - 2:
                            pool.wait_ge(sq_summed.sem, k + 1)

                @block.scalar
                def _(act):
                    act.dma_start(h[:, :, :], A["xT"]).then_inc(setup_loaded.sem, 16)
                    act.dma_start(const[:, :, :], A["consts"]).then_inc(setup_loaded.sem, 16)
                    act.dma_start(small[:, :], A["small"]).then_inc(setup_loaded.sem, 16)
                    act.wait_ge(setup_loaded.sem, 80)
                    act.activation(cond[:, 0, :], c_raw[:, :], ACT.Tanh, scale=0.5).then_inc(cond_step.sem, 1)

                @block.vector
                def _(dve):
                    dve.wait_ge(cond_step.sem, 1)
                    dve.scalar_tensor_tensor(out=cond[:, 1, :], in0=cond[:, 0, :], scalar=1.0, in1=c_raw[:, :],
                                             op0=ALU.add, op1=ALU.mult).then_inc(cond_ready.sem, 1)
                    dve.wait_ge(cond_ready.sem, 1)
                    dve.tensor_scalar(cond[:, 2, :], cond[:, 1, :], 0.5, None, ALU.mult).then_inc(cond_ready.sem, 1)
                    for g in range(MOD_FIRST // FIRST_GROUP):
                        dve.wait_ge(mod_first_ready.sem, g + 1)
                        dve.tensor_copy(mod_row_first[:, g * 512:(g + 1) * 512], ps[0:2, g, :]).then_inc(mod_copied.sem, 1)
                    dve.wait_ge(mod_turned.sem, MOD_FIRST // FIRST_GROUP)
                    n_setup[0] = mod_finish(dve, 0, 5, 0, MOD_FIRST, 0)

                @block.tensor
                def _(pe):
                    pe.wait_ge(cond_ready.sem, 2)
                    for i, (a, b) in enumerate(FIRST_LOADS):
                        pe.wait_ge(mod_loaded[i].sem, 16)
                        for j in range(a, b, FIRST_GROUP):
                            for k in range(KD):
                                mm = pe.matmul(ps[0:2, j // FIRST_GROUP, :], cond[:, 2, 2 * k:2 * k + 2],
                                               w_mod_first[:, j:j + FIRST_GROUP, k * P:(k + 1) * P],
                                               start=(k == 0), stop=(k == KD - 1))
                            mm.then_inc(mod_first_ready.sem, 1)
                    for j in range(MOD_FIRST):
                        if j % FIRST_GROUP == 0:
                            pe.wait_ge(mod_copied.sem, j // FIRST_GROUP + 1)
                        mm = pe.matmul(ps[:, 5, 2 * j:2 * j + 2], mod_row_first[0:2, j * P:(j + 1) * P],
                                       K_["ident"][0:2, 0:2], start=True, stop=True)
                        if j % FIRST_GROUP == FIRST_GROUP - 1:
                            mm.then_inc(mod_turned.sem, 1)
            setup_loaded.phase_end(80)
            mod_copied.phase_end(MOD_FIRST // FIRST_GROUP)
            mod_turned.phase_end(MOD_FIRST // FIRST_GROUP)
            mod_ready.phase_end(n_setup[0])
            h_squared.phase_end(KD - 2)
            sq_summed.phase_end(KD - 1)
            for i in range(MOD_SLOTS):
                mod_loaded[i].phase_end(16)

        def norm_act(act, nt, between):
            act.preload_act_table_set("natural_log_exp_and_others")
            between()
            act.wait_ge(ms_ready.sem, ms_ready.at(1))
            act.activation(lnv[:, 0:nt], ps_slot[1][:, 0:nt], ACT.Ln, bias=small[:, EPS:EPS + 1],
                           scale=1.0 / D_MODEL).then_inc(ln_done.sem, 1)
            act.wait_ge(ln_done.sem, ln_done.at(1))
            act.activation(rstd[:, 0:nt], lnv[:, 0:nt], ACT.Exp, scale=-0.5).then_inc(rstd_ready.sem, 1)
            for k in range(KD):
                act.wait_ge(moded_ready.sem, moded_ready.at(k + 1))
                act.activation(hn_hi[:, k, 0:nt], moded[:, k % 2, 0:nt], ACT.Copy).then_inc(hn_hi_ready.sem, 1)

        def norm_pool(pool, nt):
            pool.wait_ge(rstd_ready.sem, rstd_ready.at(1))
            for k in range(1, KD):
                if k >= 2:
                    pool.wait_ge(moded_ready.sem, moded_ready.at(k - 1))
                pool.tensor_tensor(scaled[:, k % 2, 0:nt], h[:, k, 0:nt], rstd[:, 0:nt],
                                   ALU.mult).then_inc(scaled_ready.sem, 1)

        def norm_pe(pe, nt):
            pe.wait_ge(sum_ready.sem, sum_ready.at(2))
            for a, b in ([(0, 512), (512, NT)] if nt == NT else [(0, 512)]):
                mm = pe.matmul(ps_slot[1][:, a:b], K_["ones"], sum_sq[:, a:b], start=True, stop=True)
            mm.then_inc(ms_ready.sem, 1)

        def square_residual(pool, s, tile, n, summed, first=False):
            pool.wait_ge(evacuated[s].sem, n)
            hv = h[:, bass.ds(tile, 1), :].rearrange("p a t -> p (a t)")
            if first:
                pool.tensor_tensor(sum_sq[:, :], hv, hv, ALU.mult).then_inc(sq_summed.sem, 1)
                return
            pool.wait_ge(sq_summed.sem, sq_summed.at(summed))
            pool.tensor_tensor(h_sq[:, :], hv, hv, ALU.mult).then_inc(h_squared.sem, 1)
            pool.wait_ge(h_squared.sem, h_squared.at(summed))
            pool.tensor_tensor(sum_sq[:, :], sum_sq[:, :], h_sq[:, :], ALU.add).then_inc(sq_summed.sem, 1)

        def square_residuals(pool, base):
            square_residual(pool, 0, 0, evacuated[0].at(base + 1), 0, first=True)
            square_residual(pool, 1, 1, evacuated[1].at(base + 1), 1)
            with pool.Fori(1, KD // 2 - 1) as i:
                for s in range(2):
                    square_residual(pool, s, i * 2 + s, i + evacuated[s].at(base + 1), i * 2 + s)
            square_residual(pool, 0, KD - 2, evacuated[0].at(base + KD // 2), KD - 2)

        def squares_end():
            sq_summed.phase_end(KD - 1)
            h_squared.phase_end(KD - 2)

        def norm_dve(dve, nt, gain, part, between):
            a, b = COLS[gain]
            l = layer[0]
            dve.tensor_tensor(h_sq[:, 0:nt], h[:, KD - 1, 0:nt], h[:, KD - 1, 0:nt], ALU.mult).then_inc(sum_ready.sem, 1)
            dve.wait_ge(sum_ready.sem, sum_ready.at(1))
            dve.tensor_tensor(sum_sq[:, 0:nt], sum_sq[:, 0:nt], h_sq[:, 0:nt], ALU.add).then_inc(sum_ready.sem, 1)
            for w in range(2):
                dve.scalar_tensor_tensor(out=moda[:, w, :], in0=mod[l][:, w, (part + 1) * KD:(part + 2) * KD],
                                         scalar=1.0, in1=cols[l][:, a:b], op0=ALU.add,
                                         op1=ALU.mult).then_inc(moda_ready.sem, 1)
            dve.wait_ge(moda_ready.sem, moda_ready.at(2))
            between()

            def lo(k):
                dve.wait_ge(hn_hi_ready.sem, hn_hi_ready.at(k + 1))
                dve.tensor_tensor(hn_lo[:, k, 0:nt], moded[:, k % 2, 0:nt], hn_hi[:, k, 0:nt].bitcast(F32),
                                  ALU.subtract).then_inc(hn_lo_ready.sem, 1)
            for k in range(KD):
                if k == 0:
                    dve.wait_ge(rstd_ready.sem, rstd_ready.at(1))
                    dve.tensor_tensor(scaled[:, 0, 0:nt], h[:, 0, 0:nt], rstd[:, 0:nt], ALU.mult).then_inc(sum_ready.sem, 1)
                    dve.wait_ge(sum_ready.sem, sum_ready.at(3))
                else:
                    dve.wait_ge(scaled_ready.sem, scaled_ready.at(k))
                if k >= 2:
                    dve.wait_ge(hn_lo_ready.sem, hn_lo_ready.at(k - 1))
                for _, span, w in TWO:
                    if span.start >= nt:
                        continue
                    mm = dve.tensor_scalar(moded[:, k % 2, span], scaled[:, k % 2, span], moda[:, w, k:k + 1],
                                           mod[l][:, w, part * KD + k:part * KD + k + 1], ALU.mult, ALU.add)
                mm.then_inc(moded_ready.sem, 1)
                if k == 0:
                    lo(0)
                elif k >= 2:
                    lo(k - 1)
            lo(KD - 1)

        def norm_end():
            for x, n in ((sum_ready, 3), (ms_ready, 1), (ln_done, 1), (rstd_ready, 1), (scaled_ready, KD - 1),
                         (moded_ready, KD), (hn_hi_ready, KD), (hn_lo_ready, KD), (moda_ready, 2)):
                x.phase_end(n)

        def add_residual(dve, s, tile, nt, part, n):
            dve.wait_ge(block_done[s].sem, n)
            for _, span, w in TWO:
                if span.start >= nt:
                    continue
                hv = h[:, bass.ds(tile, 1), span].rearrange("p a t -> p (a t)")
                mm = dve.scalar_tensor_tensor(out=hv, in0=ps_slot[s][:, span],
                                              scalar=mod_all[:, layer[0], w, bass.ds(part * KD + tile, 1)],
                                              in1=hv, op0=ALU.mult, op1=ALU.add)
            mm.then_inc(evacuated[s].sem, 1)

        def ffn(l, which, nt, following, mod_plan=None, more=True):
            part = 0 if which == 0 else 6
            gain = "n1" if which == 0 else "n2"
            PER_HALF = NFH + KD // 2
            ml, mj0, steps, extra = mod_plan or (0, 0, (0, 0), (0, 0))
            mod_from = [mj0, mj0 + NFH * steps[0] + extra[0]]
            mod_upto = [mod_from[1], mod_from[1] + NFH * steps[1] + extra[1]]
            turns = [0]
            for hf in range(2):
                turns.append(turns[-1] + (NFH if steps[hf] else 0) + (1 if extra[hf] else 0))
            n_mod = [0]
            uses = [[0] * MOD_SLOTS]
            for hf in range(2):
                uses.append([n + NFH * (i < steps[hf]) + (i < extra[hf]) for i, n in enumerate(uses[-1])])

            def mod_load(sp, slot, column, done):
                sp.wait_ge(mod_used.sem, done)
                sp.dma_start(w_mod[slot][:, :], A["wmod"][ml, column]).then_inc(mod_loaded[slot].sem, 16)

            with nc.Block() as block:
                @block.sync
                def _(sp):
                    for half in range(2):
                        b0 = half * PER_HALF
                        r, j0 = steps[half], mod_from[half]
                        seen = j0 - mj0
                        def step(i, loads=True):
                            for s in range(2 if loads else 0):
                                load_block(sp, s, A["wgu"][l, which, i * 2 + (half * NF + s)], KD, i + b0)
                            for s in range(r):
                                mod_load(sp, s, i * r + (j0 + s), i * r + mod_used.at(seen - r + s + 1))
                        if half == 0:
                            step(0, loads=False)
                        with sp.Fori(1 if half == 0 else 0, NFH) as i:
                            step(i)

                        def load_down(i):
                            for s in range(2):
                                load_block(sp, s, A["wdn"][l, which, half, i * 2 + s], NFH, i + (b0 + NFH))
                        load_down(0)
                        for s in range(extra[half]):
                            mod_load(sp, s, j0 + NFH * r + s, mod_used.at(seen + NFH * r - r + s + 1))
                        with sp.Fori(1, KD // 2) as i:
                            load_down(i)
                    next_loads(sp, following, KD, 2 * PER_HALF)

                @block.gpsimd
                def _(pool):
                    norm_pool(pool, nt)
                    if more:
                        square_residuals(pool, KD // 2)

                @block.scalar
                def _(act):
                    norm_act(act, nt, lambda: [split_hi(act, s, KD, 0) for s in range(2)])

                    def gate_up(i, half, last):
                        b0 = half * PER_HALF
                        nk = NFH if last else KD
                        split_hi(act, 0, nk, i + (b0 + 1))
                        act.wait_ge(silu_ready.sem, i + silu_ready.at(half * NFH))
                        act.activation(tanh_g[:, 0:nt], ps_slot[0][:, 0:nt], ACT.Tanh,
                                       scale=0.5).then_inc(tanh_ready.sem, 1)
                        split_hi(act, 1, nk, i + (b0 + 1))
                        act.wait_ge(glu_ready.sem, i + glu_ready.at(half * NFH + 1))
                        act.activation(g_hi[:, bass.ds(i, 1), 0:nt].rearrange("p a t -> p (a t)"), glu[:, 0:nt],
                                       ACT.Copy).then_inc(g_hi_ready.sem, 1)

                    def down(i, half, last):
                        if not last:
                            for s in range(2):
                                split_hi(act, s, NFH, i + (half * PER_HALF + NFH + 1))
                        elif half == 0:
                            for s in range(2):
                                split_hi(act, s, KD, PER_HALF)
                    for half in range(2):
                        with act.Fori(0, NFH - 1) as i:
                            gate_up(i, half, False)
                        gate_up(NFH - 1, half, True)
                        with act.Fori(0, KD // 2 - 1) as i:
                            down(i, half, False)
                        down(KD // 2 - 1, half, True)

                @block.vector
                def _(dve):
                    norm_dve(dve, nt, gain, part, lambda: [split_lo(dve, s, KD, 0) for s in range(2)])
                    def gate_up(i, half, last):
                        b0 = half * PER_HALF
                        nk = NFH if last else KD
                        r = steps[half]
                        split_lo(dve, 0, nk, i + (b0 + 1))
                        dve.wait_ge(tanh_ready.sem, i + tanh_ready.at(half * NFH + 1))
                        dve.scalar_tensor_tensor(out=silu_g[:, 0:nt], in0=tanh_g[:, 0:nt], scalar=1.0,
                                                 in1=ps_slot[0][:, 0:nt], op0=ALU.add,
                                                 op1=ALU.mult).then_inc(silu_ready.sem, 1)
                        split_lo(dve, 1, nk, i + (b0 + 1))
                        dve.wait_ge(silu_ready.sem, i + silu_ready.at(half * NFH + 1))
                        dve.scalar_tensor_tensor(out=glu[:, 0:nt], in0=silu_g[:, 0:nt], scalar=0.5,
                                                 in1=ps_slot[1][:, 0:nt], op0=ALU.mult,
                                                 op1=ALU.mult).then_inc(glu_ready.sem, 1)
                        dve.wait_ge(g_hi_ready.sem, i + g_hi_ready.at(half * NFH + 1))
                        dve.tensor_tensor(g_lo[:, bass.ds(i, 1), 0:nt].rearrange("p a t -> p (a t)"), glu[:, 0:nt],
                                          g_hi[:, bass.ds(i, 1), 0:nt].rearrange("p a t -> p (a t)").bitcast(F32),
                                          ALU.subtract).then_inc(g_lo_ready.sem, 1)
                        if r:
                            mod_copy(dve, r, i * r + mod_used.at(mod_from[half] - mj0 + r))

                    def down(i, half, last):
                        done = half * PER_HALF + NFH
                        for s in range(2):
                            if not last:
                                split_lo(dve, s, NFH, i + (done + 1))
                            elif half == 0:
                                split_lo(dve, s, KD, PER_HALF)
                            add_residual(dve, s, i * 2 + s, nt, part + 2, i + block_done[s].at(done + 1))
                    for half in range(2):
                        with dve.Fori(0, NFH - 1) as i:
                            gate_up(i, half, False)
                        gate_up(NFH - 1, half, True)
                        if mod_upto[half] > mod_from[half]:
                            if extra[half]:
                                mod_copy(dve, extra[half], mod_used.at(mod_upto[half] - mj0))
                            dve.wait_ge(mod_turned.sem, mod_turned.at(turns[half + 1]))
                            n_mod[0] = mod_finish(dve, ml, 6 + half, mod_from[half], mod_upto[half], n_mod[0])
                        with dve.Fori(0, KD // 2 - 1) as i:
                            down(i, half, False)
                        down(KD // 2 - 1, half, True)

                @block.tensor
                def _(pe):
                    norm_pe(pe, nt)

                    def gate_up(i, half, first=False, is_first=False):
                        b0 = half * PER_HALF
                        pe.wait_ge(lo_ready[0].sem, i + lo_ready[0].at(b0 + 1))
                        pe.wait_ge(silu_ready.sem, i + silu_ready.at(half * NFH))
                        product(pe, 0, KD, ps_slot[0], hn_hi, hn_lo, nt, hn_lo_ready if first else None)
                        pe.wait_ge(lo_ready[1].sem, i + lo_ready[1].at(b0 + 1))
                        pe.wait_ge(glu_ready.sem, i + glu_ready.at(half * NFH))
                        product(pe, 1, KD, ps_slot[1], hn_hi, hn_lo, nt)
                        r = steps[half]
                        if r:
                            if not is_first:
                                mod_turn(pe, r, 6 + half, i * r + (mod_from[half] - r),
                                         i + mod_copied.at(turns[half]))
                            mod_rows(pe, r, lambda m: i + uses[half][m])
                    for half in range(2):
                        b0 = half * PER_HALF
                        if half == 1:
                            for s in range(2):
                                pe.wait_ge(evacuated[s].sem, evacuated[s].at(KD // 2))
                        if half == 0:
                            pe.wait_ge(rstd_ready.sem, rstd_ready.at(1))
                        gate_up(0, half, first=(half == 0), is_first=True)
                        with pe.Fori(1, NFH) as i:
                            gate_up(i, half)
                        if steps[half]:
                            mod_turn(pe, steps[half], 6 + half, mod_from[half] + (NFH - 1) * steps[half],
                                     mod_copied.at(turns[half] + NFH))
                        if extra[half]:
                            mod_rows(pe, extra[half], lambda m: uses[half][m] + NFH * (m < steps[half]))
                            mod_turn(pe, extra[half], 6 + half, mod_from[half] + NFH * steps[half],
                                     mod_copied.at(turns[half + 1]))
                        pe.wait_ge(g_lo_ready.sem, g_lo_ready.at((half + 1) * NFH))
                        with pe.Fori(0, KD // 2) as i:
                            for s in range(2):
                                pe.wait_ge(lo_ready[s].sem, i + lo_ready[s].at(b0 + NFH + 1))
                                pe.wait_ge(evacuated[s].sem, i + evacuated[s].at(half * KD // 2))
                                product(pe, s, NFH, ps_slot[s], g_hi, g_lo, nt)
            norm_end()
            stream_end(2 * PER_HALF)
            for x in (tanh_ready, silu_ready, glu_ready, g_hi_ready, g_lo_ready):
                x.phase_end(NF)
            for s in range(2):
                evacuated[s].phase_end(KD)
            if more:
                squares_end()
            mod_used.phase_end(mod_upto[1] - mj0)
            mod_copied.phase_end(turns[2])
            mod_turned.phase_end(turns[2])
            mod_ready.phase_end(n_mod[0])
            for i in range(MOD_SLOTS):
                mod_loaded[i].phase_end(16 * uses[-1][i])

        def in_proj(l):
            pairs = N_IN // 2
            with nc.Block() as block:
                @block.sync
                def _(sp):
                    with sp.Fori(1, pairs) as i:
                        for s in range(2):
                            load_block(sp, s, A["win"][l, i * 2 + s], KD, i)

                @block.gpsimd
                def _(pool):
                    norm_pool(pool, NT)

                @block.scalar
                def _(act):
                    norm_act(act, NT, lambda: [split_hi(act, s, KD, 0) for s in range(2)])

                    def evacuate(i, s, dst):
                        act.wait_ge(block_done[s].sem, i + block_done[s].at(1))
                        act.activation(dst, ps_slot[s], ACT.Copy).then_inc(evacuated[s].sem, 1)
                    with act.Fori(0, pairs - 1) as i:
                        for s in range(2):
                            split_hi(act, s, KD, i + 1)
                            evacuate(i, s, u[:, bass.ds(i * 2 + s, 1), :].rearrange("p a t -> p (a t)"))
                    for s in range(2):
                        evacuate(pairs - 1, s, u[:, N_IN - 2 + s, :])

                @block.vector
                def _(dve):
                    norm_dve(dve, NT, "nm", 3, lambda: [split_lo(dve, s, KD, 0) for s in range(2)])
                    with dve.Fori(1, pairs) as i:
                        for s in range(2):
                            split_lo(dve, s, KD, i)

                @block.tensor
                def _(pe):
                    norm_pe(pe, NT)

                    def pair(i, first=False):
                        for s in range(2):
                            pe.wait_ge(lo_ready[s].sem, i + lo_ready[s].at(1))
                            pe.wait_ge(evacuated[s].sem, i + evacuated[s].at(0))
                            product(pe, s, KD, ps_slot[s], hn_hi, hn_lo, NT,
                                    hn_lo_ready if first and s == 0 else None)
                    pe.wait_ge(rstd_ready.sem, rstd_ready.at(1))
                    pair(0, first=True)
                    with pe.Fori(1, pairs) as i:
                        pair(i)
            norm_end()
            stream_end(pairs)
            for s in range(2):
                evacuated[s].phase_end(pairs)

        mix_hi_ready, mix_lo_ready = sem("mix_hi_ready"), sem("mix_lo_ready")

        def out_proj(l, nt, following):
            pairs = KD // 2
            with nc.Block() as block:
                @block.sync
                def _(sp):
                    with sp.Fori(1, pairs) as i:
                        for s in range(2):
                            load_block(sp, s, A["wout"][l, i * 2 + s], KD, i)
                    next_loads(sp, following, KD, pairs)

                @block.gpsimd
                def _(pool):
                    square_residuals(pool, 0)

                @block.scalar
                def _(act):
                    split_hi(act, 0, KD, 0)
                    for k in range(KD):
                        act.activation(g_hi[:, k, 0:nt], mix[:, k, 0:nt], ACT.Copy).then_inc(mix_hi_ready.sem, 1)
                        if k == 1:
                            split_hi(act, 1, KD, 0)
                    with act.Fori(1, pairs) as i:
                        for s in range(2):
                            split_hi(act, s, KD, i)

                @block.vector
                def _(dve):
                    split_lo(dve, 0, KD, 0)
                    for k in range(KD):
                        dve.wait_ge(mix_hi_ready.sem, mix_hi_ready.at(k + 1))
                        dve.tensor_tensor(g_lo[:, k, 0:nt], mix[:, k, 0:nt], g_hi[:, k, 0:nt].bitcast(F32),
                                          ALU.subtract).then_inc(mix_lo_ready.sem, 1)
                        if k == 2:
                            split_lo(dve, 1, KD, 0)

                    def step(i, last):
                        for s in range(2):
                            if not last:
                                split_lo(dve, s, KD, i + 1)
                            add_residual(dve, s, i * 2 + s, nt, 5, i + block_done[s].at(1))
                    with dve.Fori(0, pairs - 1) as i:
                        step(i, False)
                    step(pairs - 1, True)

                @block.tensor
                def _(pe):
                    def pair(i, first=False):
                        for s in range(2):
                            pe.wait_ge(lo_ready[s].sem, i + lo_ready[s].at(1))
                            pe.wait_ge(evacuated[s].sem, i + evacuated[s].at(0))
                            product(pe, s, KD, ps_slot[s], g_hi, g_lo, nt,
                                    mix_lo_ready if first and s == 0 else None)
                    pair(0, first=True)
                    with pe.Fori(1, pairs) as i:
                        pair(i)
            stream_end(pairs)
            for s in range(2):
                evacuated[s].phase_end(pairs)
            squares_end()
            mix_hi_ready.phase_end(KD)
            mix_lo_ready.phase_end(KD)

        place["T"] = T0
        rope = tmp("rope", [P, 4, SEQ])
        bias = tmp("bias", [P, 4, 14 * GRID_W])
        w_mla = tmp("w_mla", [P, 3 * 4 * MLA_D + 256])
        o_nat = tmp("o_nat", [P, 2, 256])
        stats = tmp("stats", [P, 16])
        q_mla = [at(f"q_mla{i}", [P, NT], R_W + i * TOK) for i in range(4)]
        k_mla = [at(f"k_mla{i}", [P, NT], R_W + (4 + i) * TOK) for i in range(4)]
        v_mla = at("v_mla", [P, NTT, 256], R_W + 8 * TOK)
        hsq = at("hsq", [P, 2, NT], R_N)
        hln = at("hln", [P, NT], R_N + 2 * TOK)
        hrstd = at("hrstd", [P, 2, NT], R_N + 3 * TOK)
        rot_s = at("rot_s", [P, SEQ], R_N + 5 * TOK)
        rot_c = at("rot_c", [P, 2, SEQ], R_N + 6 * TOK)
        probs = at("probs", [P, 2, NT], R_G)
        probs_t = at("probs_t", [P, 2, NT], R_G + 2 * TOK)

        mix_loaded = sem("mix_loaded")
        v_turned, v_copied = sem("values_turned"), sem("values_copied")
        hsq_ready, hms_ready, hln_done, hrstd_ready, hnorm_ready = (sem("hsq_ready"), sem("hms_ready"), sem("hln_done"),
                                                                    sem("hrstd_ready"), sem("hnorm_ready"))
        rot_ready, rot_c_ready, rot_s_ready, roped = sem("rot_ready"), sem("rot_c_ready"), sem("rot_s_ready"), sem("roped")
        proj_ready, proj_copied = sem("proj_ready"), sem("proj_copied")

        def head_norms():
            rows = slice(0, P)
            out = [([u[:, 0, :], u[:, 1, :]], rows, K_["ones"], 1 / 256, [col("mq", 0), col("mq", 1)], None, None, None),
                   ([u[:, 2, :]], rows, K_["ones"], 1 / 128, [col("mkv")], None, None, None)]
            for t in (U_NQ, U_NQ + 1, U_NK, U_NK + 1):
                q = t < U_NK
                out.append(([u[:, t, :]], rows, K_["ones64"], 1 / HEAD, [col("nq" if q else "nk")],
                            LN_Q64 if q else None, None, None))
            for t in (U_GQ, U_GQ + 1, U_GK):
                q = t < U_GK
                out.append(([u[:, t, :]], rows, K_["ones64"], 1 / HEAD, [col("gq" if q else "gk")],
                            LN_Q64 if q else None, 0, K_["rot_g"]))
            first = len(out)
            rows = slice(0, MLA_D)
            for t, q in [(t, True) for t in q_mla] + [(t, False) for t in k_mla]:
                out.append(([t[rows, :]], rows, K_["ones"][rows, 0:MLA_D], 1 / MLA_D, [col("mqn" if q else "mkn", 0, rows)],
                            LN_Q96 if q else None, 2, K_["rot_m"][rows, 0:MLA_D]))
            return out, first

        def qkv(l):
            units, first = head_norms()
            groups = (range(0, first), range(first, len(units)))
            roped_units = [n for n, x in enumerate(units) if x[6] is not None]
            rope_no = {n: r for r, n in enumerate(roped_units)}
            sq_no = [sum(len(x[0]) for x in units[:n]) for n in range(len(units) + 1)]
            N_PROJ = 10
            ps_projs = [psf[:, 3072:3072 + NT], psf[:, 2048:2048 + NT]]
            ps_values = ps_projs[::-1]
            group0_ropes = sum(n < first for n in roped_units)

            with nc.Block() as block:
                @block.sync
                def _(sp):
                    sp.dma_start(w_mla[:, :], A["mla"][l]).then_inc(mix_loaded.sem, 16)
                    sp.dma_start(rope[:, :, :], A["rope"]).then_inc(mix_loaded.sem, 16)
                    sp.dma_start(bias[:, :, :], A["bias"][l]).then_inc(mix_loaded.sem, 16)
                    sp.wait_ge(mix_loaded.sem, mix_loaded.at(48))

                @block.scalar
                def _(act):
                    act.preload_act_table_set("natural_log_exp_and_others")

                    def squares(n):
                        tiles, rows = units[n][0:2]
                        for j, t in enumerate(tiles):
                            b = sq_no[n] + j
                            if b >= 2:
                                act.wait_ge(hms_ready.sem, hms_ready.at(b - 1))
                            act.activation(hsq[rows, b % 2, :], t, ACT.Square).then_inc(hsq_ready.sem, 1)

                    def rstd_of(n):
                        rows, inv, lnc = units[n][1], units[n][3], units[n][5]
                        act.wait_ge(hms_ready.sem, hms_ready.at(sq_no[n + 1]))
                        if n >= 1:
                            act.wait_ge(hrstd_ready.sem, hrstd_ready.at(n))
                        act.activation(hln[rows, :], ps_slot[n % 2][rows, :], ACT.Ln, bias=small[rows, EPS:EPS + 1],
                                       scale=inv).then_inc(hln_done.sem, 1)
                        act.wait_ge(hln_done.sem, hln_done.at(n + 1))
                        if n >= 2:
                            act.wait_ge(hnorm_ready.sem, hnorm_ready.at(n - 1))
                        act.activation(hrstd[rows, n % 2, :], hln[rows, :], ACT.Exp, scale=-0.5,
                                       bias=0.0 if lnc is None else small[rows, lnc:lnc + 1]).then_inc(hrstd_ready.sem, 1)
                    for gi, g in enumerate(groups):
                        for n in g:
                            squares(n)
                            if n > g[0]:
                                rstd_of(n - 1)
                        rstd_of(g[-1])
                        if gi == 0:
                            for m in range(N_PROJ):
                                act.wait_ge(proj_ready.sem, proj_ready.at(m + 1))
                                ps_proj = ps_projs[m % 2]
                                if m < 8:
                                    dst = (q_mla[m] if m < 4 else k_mla[m - 4])[0:MLA_D, :]
                                    act.activation(dst, ps_proj[0:MLA_D, :], ACT.Copy).then_inc(proj_copied.sem, 1)
                                else:
                                    act.activation(v_mla[:, 3 * (m - 8):3 * (m - 7), :].rearrange("p a b -> p (a b)"),
                                                   ps_proj, ACT.Copy).then_inc(proj_copied.sem, 1)
                            act.wait_ge(proj_copied.sem, proj_copied.at(N_PROJ))

                @block.tensor
                def _(pe):
                    for j in range(3):
                        if j == 2:
                            pe.wait_ge(v_copied.sem, v_copied.at(1))
                        for tt in range(NTT):
                            t = slice(tt * P, (tt + 1) * P)
                            mm = pe.transpose(ps_values[j % 2][:, t], u[:, U_V + j, t], K_["ident"])
                        mm.then_inc(v_turned.sem, 1)

                    def sums(n):
                        tiles, rows, ones = units[n][0:3]
                        M = rows.stop
                        if n >= 2:
                            pe.wait_ge(hln_done.sem, hln_done.at(n - 1))
                        for j in range(len(tiles)):
                            b = sq_no[n] + j
                            pe.wait_ge(hsq_ready.sem, hsq_ready.at(b + 1))
                            for a, e in ((0, 512), (512, NT)):
                                mm = pe.matmul(ps_slot[n % 2][0:M, a:e], ones, hsq[rows, b % 2, a:e], start=(j == 0),
                                               stop=(j == len(tiles) - 1))
                            mm.then_inc(hms_ready.sem, 1)

                    def rotate(n):
                        if n not in rope_no:
                            return
                        r = rope_no[n]
                        tiles, rows, rotm = units[n][0], units[n][1], units[n][7]
                        pe.wait_ge(hnorm_ready.sem, hnorm_ready.at(n + 1))
                        if r == 0:
                            pe.wait_ge(v_copied.sem, v_copied.at(3))
                        if r >= 2:
                            pe.wait_ge(rot_s_ready.sem, rot_s_ready.at(r - 1))
                        pe.matmul(ps[0:rows.stop, 4 + r % 2, :], rotm, tiles[0][:, LAT], start=True,
                                  stop=True).then_inc(rot_ready.sem, 1)

                    def projections():
                        pe.wait_ge(mix_loaded.sem, mix_loaded.at(48))
                        pe.wait_ge(hnorm_ready.sem, hnorm_ready.at(2))
                        W4 = 4 * MLA_D
                        for m in range(N_PROJ):
                            ps_proj = ps_projs[m % 2]
                            if m >= 2:
                                pe.wait_ge(proj_copied.sem, proj_copied.at(m - 1))
                            elif m == 1:
                                pe.wait_ge(rot_s_ready.sem, rot_s_ready.at(group0_ropes))
                            if m < 8:
                                hd = m % 4
                                for a, e in ((0, 512), (512, NT)):
                                    out = ps_proj[0:MLA_D, a:e]
                                    if m < 4:
                                        for k in range(2):
                                            w = w_mla[:, k * W4 + hd * MLA_D:k * W4 + (hd + 1) * MLA_D]
                                            mm = pe.matmul(out, w, u[:, k, a:e], start=(k == 0), stop=(k == 1))
                                    else:
                                        w = w_mla[:, 2 * W4 + hd * MLA_D:2 * W4 + (hd + 1) * MLA_D]
                                        pe.matmul(out, w, u[:, U_KV, a:e], start=True, stop=False)
                                        mm = pe.matmul(out, K_["sel_kr"][:, 0:MLA_D], u[:, U_KR, a:e], start=False,
                                                       stop=True)
                            else:
                                for j in range(3):
                                    tt = 3 * (m - 8) + j
                                    mm = pe.matmul(ps_proj[:, j * 256:(j + 1) * 256], u[:, U_KV, tt * P:(tt + 1) * P],
                                                   w_mla[:, 3 * W4:3 * W4 + 256], start=True, stop=True)
                            mm.then_inc(proj_ready.sem, 1)
                    for gi, g in enumerate(groups):
                        for n in g:
                            sums(n)
                            if n > g[0]:
                                rotate(n - 1)
                        rotate(g[-1])
                        if gi == 0:
                            projections()
                            pe.wait_ge(proj_copied.sem, proj_copied.at(N_PROJ))

                @block.gpsimd
                def _(pool):
                    pool.wait_ge(mix_loaded.sem, mix_loaded.at(48))
                    for n in roped_units:
                        r = rope_no[n]
                        tiles, rows, tab = units[n][0], units[n][1], units[n][6]
                        pool.wait_ge(hnorm_ready.sem, hnorm_ready.at(n + 1))
                        if r >= 2:
                            pool.wait_ge(roped.sem, roped.at(r - 1))
                        pool.tensor_tensor(rot_c[rows, r % 2, :], tiles[0][:, LAT], rope[rows, tab, :],
                                           ALU.mult).then_inc(rot_c_ready.sem, 1)

                @block.vector
                def _(dve):
                    for j in range(3):
                        dve.wait_ge(v_turned.sem, v_turned.at(j + 1))
                        dve.tensor_copy(v_nat[:, :, j * P:(j + 1) * P],
                                        ps_values[j % 2].rearrange("p (a b) -> p a b", b=P)).then_inc(v_copied.sem, 1)

                    def scale_rows(n):
                        tiles, rows, gains = units[n][0], units[n][1], units[n][4]
                        dve.wait_ge(hrstd_ready.sem, hrstd_ready.at(n + 1))
                        for t, g in zip(tiles, gains):
                            mm = dve.scalar_tensor_tensor(out=t, in0=t, scalar=g, in1=hrstd[rows, n % 2, :],
                                                          op0=ALU.mult, op1=ALU.mult)
                        mm.then_inc(hnorm_ready.sem, 1)

                    def apply_rope(n):
                        if n not in rope_no:
                            return
                        r = rope_no[n]
                        tiles, rows, tab = units[n][0], units[n][1], units[n][6]
                        if r == 0:
                            dve.wait_ge(mix_loaded.sem, mix_loaded.at(48))
                        dve.wait_ge(rot_ready.sem, rot_ready.at(r + 1))
                        if r >= 1:
                            dve.wait_ge(roped.sem, roped.at(r))
                        dve.tensor_tensor(rot_s[rows, :], ps[rows, 4 + r % 2, :], rope[rows, tab + 1, :],
                                          ALU.mult).then_inc(rot_s_ready.sem, 1)
                        dve.wait_ge(rot_s_ready.sem, rot_s_ready.at(r + 1))
                        dve.wait_ge(rot_c_ready.sem, rot_c_ready.at(r + 1))
                        dve.tensor_tensor(tiles[0][:, LAT], rot_c[rows, r % 2, :], rot_s[rows, :],
                                          ALU.add).then_inc(roped.sem, 1)
                    for g in groups:
                        for n in g:
                            scale_rows(n)
                            if n > g[0]:
                                apply_rope(n - 1)
                        apply_rope(g[-1])
            NU, NR = len(units), len(roped_units)
            for x, n in ((v_turned, 3), (v_copied, 3), (mix_loaded, 48), (hsq_ready, sq_no[NU]), (hms_ready, sq_no[NU]), (hln_done, NU),
                         (hrstd_ready, NU), (hnorm_ready, NU), (rot_ready, NR), (rot_c_ready, NR), (rot_s_ready, NR),
                         (roped, NR), (proj_ready, N_PROJ), (proj_copied, N_PROJ)):
                x.phase_end(n)

        scores_ready, biased, max_ready, exp_ready = sem("scores_ready"), sem("scores_biased"), sem("max_ready"), sem("exp_ready")
        probs_turned, probs_t_ready, pv_ready = sem("probs_turned"), sem("probs_t_ready"), sem("pv_ready")
        sum_inverted, o_ready = sem("sum_inverted"), sem("o_ready")
        o_turned, mix_ready = sem("o_turned"), sem("mix_ready")
        keep_ready, shift_step = sem("keep_ready"), sem("shift_step")
        shift_prev, shift_next = [at(n, [P, NT], R_N + (2 + i) * TOK) for i, n in enumerate(("shift_prev", "shift_next"))]
        SHIFTED = U_NQ - U_RW
        MIX_TILE = {"mla": 0, "na": 4, "gqa": 6}

        def attention(l, nt):
            units = [(m, qt, hd) for m in ("mla", "na", "gqa") for qt in range(nt // P) for hd in range(4)]
            N = len(units)
            ps_s = [psf[:, 0:NT], psf[:, 1024:1024 + NT]]
            ps_t = psf[:, 2048:2048 + NT]

            def keys(n):
                return (0, 0) if units[n][1] < LT_TILES else (SEQ, LT_TILES)

            def qk(n):
                m, qt, hd = units[n]
                q = slice(qt * P, (qt + 1) * P)
                if m == "mla":
                    return q_mla[hd][0:MLA_D, q], k_mla[hd][0:MLA_D, :]
                if m == "na":
                    r = slice(64 * (hd % 2), 64 * (hd % 2) + 64)
                    return u[r, U_NQ + hd // 2, q], u[r, U_NK + hd // 2, :]
                i = (0, 2, 1, 3)[hd]
                r = slice(64 * (i % 2), 64 * (i % 2) + 64)
                return u[r, U_GQ + i // 2, q], u[r, U_GK, :]

            def values(n, kt):
                m, _, hd = units[n]
                if m == "mla":
                    return v_mla[:, kt, hd * HEAD:(hd + 1) * HEAD]
                c = hd * HEAD if m == "na" else 256 + (hd // 2) * HEAD
                return v_nat[:, kt, c:c + HEAD]

            def has_bias(n):
                return units[n][0] == "na" and units[n][1] < LT_TILES
            biases = [sum(has_bias(j) for j in range(n)) for n in range(N + 1)]

            def group_end(n):
                return 0 <= n < N and units[n][2] == 3

            with nc.Block() as block:
                @block.tensor
                def _(pe):
                    def scores(n):
                        k0, _ = keys(n)
                        q, k = qk(n)
                        if n >= 2:
                            pe.wait_ge(exp_ready.sem, exp_ready.at(n - 1))
                        for a, e in ((0, 512), (512, NT)):
                            if a >= k0:
                                mm = pe.matmul(ps_s[n % 2][:, a:e], q, k[:, a:e], start=True, stop=True)
                        mm.then_inc(scores_ready.sem, 1)

                    def turn(n):
                        _, kt0 = keys(n)
                        pe.wait_ge(exp_ready.sem, exp_ready.at(n + 1))
                        if n >= 1:
                            pe.wait_ge(probs_t_ready.sem, probs_t_ready.at(n))
                        for kt in range(kt0, NTT):
                            mm = pe.transpose(ps_t[:, kt * P:(kt + 1) * P], probs[:, n % 2, kt * P:(kt + 1) * P],
                                              K_["ident"])
                        mm.then_inc(probs_turned.sem, 1)

                    def turn_out(n):
                        g = n // 4
                        pe.wait_ge(o_ready.sem, o_ready.at(n + 1))
                        for i in range(2):
                            mm = pe.transpose(ps[:, 6 + n % 2, (i + 1) * P:(i + 2) * P], o_nat[:, g % 2, i * P:(i + 1) * P],
                                              K_["ident"])
                        mm.then_inc(o_turned.sem, 1)

                    def weigh(n):
                        _, kt0 = keys(n)
                        pe.wait_ge(probs_t_ready.sem, probs_t_ready.at(n + 1))
                        if n >= 2:
                            pe.wait_ge(o_ready.sem, o_ready.at(n - 1))
                            if group_end(n - 2):
                                pe.wait_ge(mix_ready.sem, mix_ready.at((n - 2) // 4 + 1))
                        for kt in range(kt0, NTT):
                            mm = pe.matmul(ps[:, 6 + n % 2, 0:HEAD], probs_t[:, n % 2, kt * P:(kt + 1) * P], values(n, kt),
                                           start=(kt == kt0), stop=(kt == NTT - 1))
                        mm.then_inc(pv_ready.sem, 1)
                    for n in range(N + 3):
                        if n < N:
                            scores(n)
                        if 1 <= n <= N:
                            turn(n - 1)
                        if group_end(n - 3):
                            turn_out(n - 3)
                        if 2 <= n <= N + 1:
                            weigh(n - 2)

                @block.scalar
                def _(act):
                    for n in range(N + 3):
                        if n < N:
                            k0, _ = keys(n)
                            act.wait_ge(max_ready.sem, max_ready.at(n + 1))
                            if n >= 2:
                                act.wait_ge(probs_turned.sem, probs_turned.at(n - 1))
                            act.activation(probs[:, n % 2, k0:NT], ps_s[n % 2][:, k0:NT], ACT.Exp,
                                           bias=stats[:, n % 4:n % 4 + 1],
                                           accum_out=stats[:, 4 + n % 4:5 + n % 4]).then_inc(exp_ready.sem, 1)
                        if 1 <= n <= N:
                            m = n - 1
                            k0, _ = keys(m)
                            act.wait_ge(probs_turned.sem, probs_turned.at(m + 1))
                            if m >= 2:
                                act.wait_ge(pv_ready.sem, pv_ready.at(m - 1))
                            act.activation(probs_t[:, m % 2, k0:NT], ps_t[:, k0:NT], ACT.Copy).then_inc(probs_t_ready.sem, 1)
                        if group_end(n - 3):
                            m = n - 3
                            t, qt = MIX_TILE[units[m][0]], units[m][1]
                            act.wait_ge(o_turned.sem, o_turned.at(m // 4 + 1))
                            act.activation(mix[:, t:t + 2, qt * P:(qt + 1) * P],
                                           ps[:, 6 + m % 2, P:3 * P].rearrange("p (a b) -> p a b", b=P),
                                           ACT.Copy).then_inc(mix_ready.sem, 1)

                @block.gpsimd
                def _(pool):
                    pool.wait_ge(keep_ready.sem, keep_ready.at(2))
                    own = 0
                    for n in range(SHIFTED):
                        t = u[:, U_RW + n, :]
                        wide = lambda c: c.broadcast_to([P, NT])
                        pool.tensor_tensor(shift_prev[:, :], t, wide(col("mu0", n)), ALU.mult)
                        pool.tensor_tensor(shift_next[:, :], t, wide(col("mu1", n)),
                                           ALU.mult).then_inc(shift_step.sem, 1)
                        pool.wait_ge(shift_step.sem, shift_step.at(own + 1))
                        pool.tensor_tensor(t, t, wide(keep[:, n:n + 1]), ALU.mult).then_inc(shift_step.sem, 1)
                        for i, (src, to, back) in enumerate(((shift_prev, 1, 0), (shift_next, 0, 1))):
                            pool.wait_ge(shift_step.sem, shift_step.at(own + 2 + i))
                            for x in (LAT, CTXT):
                                o = t[:, x.start + to:x.stop - back]
                                mm = pool.tensor_tensor(o, o, src[:, x.start + back:x.stop - to], ALU.add)
                            mm.then_inc(shift_step.sem, 1)
                        own += 4
                        pool.wait_ge(shift_step.sem, shift_step.at(own))

                @block.vector
                def _(dve):
                    a, b = COLS["mu0"]
                    a1, b1 = COLS["mu1"]
                    dve.tensor_tensor(keep[:, :], cols[l][:, a:b], cols[l][:, a1:b1], ALU.add).then_inc(keep_ready.sem, 1)
                    dve.wait_ge(keep_ready.sem, keep_ready.at(1))
                    dve.tensor_scalar(keep[:, :], keep[:, :], -1.0, 1.0, ALU.mult, ALU.add).then_inc(keep_ready.sem, 1)
                    for n in range(N + 3):
                        if n < N:
                            m, qt, hd = units[n]
                            k0, _ = keys(n)
                            dve.wait_ge(scores_ready.sem, scores_ready.at(n + 1))
                            if has_bias(n):
                                b0 = (7 - 2 * qt - 1) * GRID_W
                                dve.tensor_tensor(ps_s[n % 2][:, LAT], ps_s[n % 2][:, LAT], bias[:, hd, b0:b0 + SEQ],
                                                  ALU.add).then_inc(biased.sem, 1)
                                dve.wait_ge(biased.sem, biased.at(biases[n] + 1))
                            if n >= 4:
                                dve.wait_ge(exp_ready.sem, exp_ready.at(n - 3))
                            dve.tensor_reduce(stats[:, n % 4:n % 4 + 1], ps_s[n % 2][:, k0:NT], AXX, ALU.max,
                                              negate=True).then_inc(max_ready.sem, 1)
                        if 2 <= n <= N + 1:
                            m = n - 2
                            g = m // 4
                            dve.wait_ge(pv_ready.sem, pv_ready.at(m + 1))
                            dve.reciprocal(stats[:, 8 + m % 4:9 + m % 4],
                                           stats[:, 4 + m % 4:5 + m % 4]).then_inc(sum_inverted.sem, 1)
                            dve.wait_ge(sum_inverted.sem, sum_inverted.at(m + 1))
                            hd = units[m][2]
                            if hd == 0 and g >= 2:
                                dve.wait_ge(o_turned.sem, o_turned.at(g - 1))
                            dve.tensor_scalar(o_nat[:, g % 2, hd * HEAD:(hd + 1) * HEAD], ps[:, 6 + m % 2, 0:HEAD],
                                              stats[:, 8 + m % 4:9 + m % 4], None, ALU.mult).then_inc(o_ready.sem, 1)
            for x, n in ((scores_ready, N), (biased, biases[N]), (max_ready, N), (exp_ready, N), (probs_turned, N),
                         (probs_t_ready, N), (pv_ready, N), (sum_inverted, N), (o_ready, N), (o_turned, N // 4),
                         (mix_ready, N // 4), (keep_ready, 2), (shift_step, 4 * SHIFTED)):
                x.phase_end(n)

        place["T"] = T0
        N_MASK = 11
        masks = tmp("masks", [P, 2, N_MASK, P])
        scan_ones = tmp("scan_ones", [P, NT])
        kk_n = tmp("kk_n", [P, 2, NT])
        lora = tmp("lora", [P, 512])
        k_nat = tmp("k_nat", [P, NTT, P])
        state = tmp("state", [P, 2, CH])
        chunk_decay = tmp("chunk_decay", [P, 2, NCH])
        half_bias = tmp("half_bias", [P, 8])
        ka_rest = tmp("ka_rest", [P, 2])
        UNITS = 2 * NTT
        x_inv = at("x_inv", [P, UNITS, P], R_G)
        xt_inv = at("xt_inv", [P, UNITS, P], R_G + 2 * TOK)
        ar = at("ar", [P, 3, NT], R_G + 12 * TOK)
        bk = at("bk", [P, 2, NT], R_G + 15 * TOK)
        bk_end = at("bk_end", [P, 2, NT], R_G + 17 * TOK)
        a_mv = at("a_mv", [P, UNITS, P], R_G + 19 * TOK)
        b_nat = at("b_nat", [P, NTT, P], R_G + 21 * TOK)
        r_eff = at("r_eff", [P, NT], R_G)
        y_loc = at("y_loc", [P, NT], R_G + TOK)
        trans = at("trans", [P, NCH, CH], R_G + 2 * TOK)
        s_add = at("s_add", [P, NCH, CH], R_G + 3 * TOK)
        sc = at("sc", [P, UNITS, 4, P], R_W)
        lx = at("lx", [P, UNITS, P], R_W + 8 * TOK)
        neg_w = at("neg_w", [P, UNITS, P], R_W + 8 * TOK)
        v_rw = at("v_rw", [P, NTT, P], R_W + 10 * TOK)
        f = [at(f"f{i}", [P, NT], R_N + (KD + k) * TOK) for i, k in enumerate((0, 1, 4, 5, 6, 7))]
        f.append(tmp("f6", [P, NT]))
        y_sum = [at(f"y_sum{i}", [P, NT], R_N + (2 + i) * TOK) for i in range(2)]
        kd_sum = [at(f"kd_sum{i}", [P, NT], R_N + (KD + 2 + i) * TOK) for i in range(2)]

        p_step = sem("pool_step")
        v_step = sem("vector_step")
        a_step = sem("scalar_step")
        tanh_done, kk_raw = sem("tanh_done"), sem("kk_raw")
        sums_ready, rsq_ready = sem("head_sums_ready"), sem("head_rsqrt_ready")
        lora_ready, gate_tanh, exps_in, exps_out = sem("lora_ready"), sem("gate_tanh"), sem("exp_args"), sem("exp_done")
        gates_ready = sem("gates_ready")
        lora_loaded, scan_loaded = sem("lora_loaded"), sem("scan_loaded")
        features, nat_turned, nat_copied = sem("features"), sem("nat_turned"), sem("nat_copied")
        wkv_scores, wkv_masked = sem("wkv_scores"), sem("wkv_masked")
        lx_ready, lx_masked, step_ready, x_ready = sem("lx_ready"), sem("lx_masked"), sem("inv_step"), sem("x_ready")
        mv_ready, mv_copied, w_ready, w_copied = sem("mv_ready"), sem("mv_copied"), sem("w_ready"), sem("w_copied")
        chunk_ready, reff_ready, yloc_copied, trans_ready, sadd_copied = (
            sem("chunk_products"), sem("r_eff_ready"), sem("y_loc_copied"), sem("trans_ready"), sem("s_add_copied"))
        state_ready, state_mm, y_ready, round_done = (sem("state_ready"), sem("state_product"), sem("y_ready"),
                                                      sem("round_done"))
        fin_ps, fin_v, fin_a = sem("final_products"), sem("final_vector"), sem("final_scalar")

        def rwkv(l, nt, following):
            ROUNDS = [(hp, d) for hp in range(2) for d in range(2)]
            K_OF, R_OF, V_OF = U_RW + 2, U_RW, U_RW + 4
            slots = [psf[:, i * 1024:i * 1024 + NT] for i in range(4)]
            GROUPS, LEVELS = 3, 6
            UG = UNITS // GROUPS
            CTX_CH = list(range(SEQ // CH, NCH))
            LAT_CH = list(range(SEQ // CH))
            ORDER = [CTX_CH + LAT_CH, CTX_CH[::-1] + LAT_CH[::-1]]
            hr = lambda j: slice(64 * j, 64 * j + 64)
            by_chunk = lambda bank: ps[:, bank:bank + 2, 0:NTT * CH].rearrange("p b (t c) -> p t b c", c=CH)
            spans = ((0, 512), (512, NT))

            def gates(dve, link, r):
                hp, d = ROUNDS[r]
                dve.wait_ge(gate_tanh.sem, gate_tanh.at(2 * r + 1))
                if r >= 1:
                    dve.wait_ge(features.sem, features.at(r))
                    dve.wait_ge(exps_out.sem, exps_out.at(5 * r))
                link(dve.tensor_scalar(f[2][:, :], f[0][:, :], 0.5, 0.5, ALU.mult, ALU.add))
                dve.tensor_tensor_scan(f[3][:, :], scan_ones[:, :], f[2][:, :], 0.0, ALU.mult,
                                       ALU.add).then_inc(gates_ready.sem, 1)
                dve.wait_ge(gate_tanh.sem, gate_tanh.at(2 * r + 2))
                link(dve.tensor_scalar(f[0][:, :], f[1][:, :], 0.5, 0.5, ALU.mult, ALU.add))
                dve.tensor_scalar(f[1][:, :], f[0][:, :], col("ka", hp), ka_rest[:, hp:hp + 1], ALU.mult,
                                  ALU.add).then_inc(gates_ready.sem, 1)

            def feature_products(eng, link, r, before_keys=None):
                hp, d = ROUNDS[r]
                rho = ar[:, 1 + r % 2, :]
                c3 = lambda x: x[:, :].rearrange("p (a b) -> p a b", b=CH)
                eng.wait_ge(gates_ready.sem, gates_ready.at(2 * r + 1))
                total = f[3][:, CH - 1::CH].rearrange("p (a b) -> p a b", b=1).broadcast_to([P, NCH, CH])
                link(eng.tensor_tensor(f[4][:, :], f[3][:, :], f[2][:, :], ALU.subtract))
                mm = eng.tensor_tensor(c3(f[5]), total, c3(f[3]), ALU.subtract)
                if d == 1:
                    mm = eng.tensor_tensor(c3(f[6]), total, c3(f[4]), ALU.subtract)
                mm.then_inc(exps_in.sem, 1)
                if before_keys:
                    before_keys()
                eng.wait_ge(gates_ready.sem, gates_ready.at(2 * r + 2))
                eng.tensor_tensor(f[2][:, :], f[0][:, :], kk_n[:, hp, :], ALU.mult)
                link(eng.tensor_tensor(f[1][:, :], f[1][:, :], u[:, K_OF + hp, :], ALU.mult))
                if d == 0:
                    link(eng.tensor_copy(kd_sum[hp][:, :], f[1][:, :]))
                else:
                    link(eng.tensor_tensor(kd_sum[hp][:, :], kd_sum[hp][:, :], f[1][:, :], ALU.add))
                eng.wait_ge(exps_out.sem, exps_out.at(5 * r + 1))
                eng.tensor_tensor(ar[:, 0, :], ar[:, 0, :], kk_n[:, hp, :], ALU.mult)
                eng.wait_ge(exps_out.sem, exps_out.at(5 * r + 2))
                eng.tensor_tensor(rho, rho, u[:, R_OF + hp, :], ALU.mult)
                eng.wait_ge(exps_out.sem, exps_out.at(5 * r + 3))
                link(eng.tensor_tensor(bk[:, 1, :], bk[:, 0, :], f[1][:, :], ALU.mult))
                eng.tensor_tensor(bk[:, 0, :], bk[:, 0, :], f[2][:, :], ALU.mult)
                eng.wait_ge(exps_out.sem, exps_out.at(5 * r + 4))
                link(eng.tensor_tensor(bk_end[:, 1, :], bk_end[:, 0, :], f[1][:, :], ALU.mult))
                eng.tensor_tensor(bk_end[:, 0, :], bk_end[:, 0, :], f[2][:, :], ALU.mult).then_inc(features.sem, 1)

            with nc.Block() as block:
                @block.sync
                def _(sp):
                    sp.dma_start(lora[:, :], A["lora"][l]).then_inc(lora_loaded.sem, 16)
                    sp.dma_start(scan_ones[:, :], A["scan"]).then_inc(scan_loaded.sem, 16)
                    sp.dma_start(masks[:, :, :, :], A["masks"]).then_inc(mix_loaded.sem, 16)
                    sp.wait_ge(chunk_ready.sem, chunk_ready.at(8))
                    next_loads(sp, following, KD, 0)

                @block.scalar
                def _(act):
                    own = [0]

                    def link(ins):
                        own[0] += 1
                        ins.then_inc(a_step.sem, 1)
                        act.wait_ge(a_step.sem, a_step.at(own[0]))
                    link(act.activation(u[0:64, U_WA, :], u[0:64, U_WA, :], ACT.Tanh))
                    act.activation(u[0:64, U_GD, :], u[0:64, U_GD, :], ACT.Tanh, scale=0.5).then_inc(tanh_done.sem, 1)

                    def copy_mv(r):
                        act.wait_ge(mv_ready.sem, mv_ready.at(r + 1))
                        act.activation(a_mv[:, :, 64:128], slots[2].rearrange("p (a b) -> p a b", b=64),
                                       ACT.Copy).then_inc(mv_copied.sem, 1)

                    def gate_tanhs(r):
                        hp, d = ROUNDS[r]
                        for i in range(2):
                            act.wait_ge(lora_ready.sem, lora_ready.at(2 * r + i + 1))
                            c = 4 * i + 2 * d + hp
                            act.activation(f[i][:, :], slots[i], ACT.Tanh, scale=0.5,
                                           bias=half_bias[:, c:c + 1]).then_inc(gate_tanh.sem, 1)

                    def decays(r):
                        hp, d = ROUNDS[r]
                        before, through, rest = (f[4], f[3], f[5]) if d == 0 else (f[5], f[6], f[4])
                        if r >= 1:
                            act.wait_ge(wkv_scores.sem, wkv_scores.at(r * UNITS))
                        act.wait_ge(exps_in.sem, exps_in.at(r + 1))
                        act.activation(ar[:, 0, :], before[:, :], ACT.Exp, scale=-G_DECAY).then_inc(exps_out.sem, 1)
                        act.activation(ar[:, 1 + r % 2, :], through[:, :], ACT.Exp, scale=-G_DECAY).then_inc(exps_out.sem, 1)
                        if r == 0:
                            act.wait_ge(kk_raw.sem, kk_raw.at(4))
                        act.activation(bk[:, 0, :], through[:, :], ACT.Exp, scale=G_DECAY).then_inc(exps_out.sem, 1)
                        act.activation(bk_end[:, 0, :], rest[:, :], ACT.Exp, scale=-G_DECAY).then_inc(exps_out.sem, 1)
                        act.activation(chunk_decay[:, r % 2, :], f[3][:, CH - 1::CH], ACT.Exp,
                                       scale=-G_DECAY).then_inc(exps_out.sem, 1)

                    def copy_natural(r):
                        for i in range(4):
                            act.wait_ge(nat_turned.sem, nat_turned.at(4 * r + i + 1))
                            src = slots[2 + i % 2]
                            if i == 0:
                                dst = a_mv[:, :, 0:64]
                                src = src.rearrange("p (a b) -> p a b", b=64)
                            else:
                                dst = (None, b_nat, k_nat, v_rw)[i][:, :, :].rearrange("p a b -> p (a b)")
                            act.activation(dst, src, ACT.Copy).then_inc(nat_copied.sem, 1)
                    for hp in range(2):
                        act.wait_ge(kk_raw.sem, kk_raw.at(hp + 1))
                        act.activation(bk[:, hp, :], kk_n[:, hp, :], ACT.Square).then_inc(rsq_ready.sem, 1)
                    gate_tanhs(0)
                    act.preload_act_table_set("natural_log_exp_and_others")
                    for hp in range(2):
                        act.wait_ge(sums_ready.sem, sums_ready.at(hp + 1))
                        link(act.activation(bk[:, hp, :], slots[2 + hp], ACT.Ln, bias=small[:, EPS_KK:EPS_KK + 1]))
                    for hp in range(2):
                        act.activation(bk[:, hp, :], bk[:, hp, :], ACT.Exp, scale=-0.5).then_inc(rsq_ready.sem, 1)
                    decays(0)
                    copy_natural(0)
                    for r, (hp, d) in enumerate(ROUNDS):
                        if r + 1 < len(ROUNDS):
                            gate_tanhs(r + 1)
                        copy_mv(r)
                        if r + 1 < len(ROUNDS):
                            decays(r + 1)
                        for g in range(GROUPS):
                            gs = slice(g * UG, (g + 1) * UG)
                            act.wait_ge(w_ready.sem, w_ready.at(GROUPS * r + g + 1))
                            act.activation(neg_w[:, gs, :], ps[:, 2 + g, :].rearrange("p (a b) -> p a b", b=P),
                                           ACT.Copy, scale=-1.0).then_inc(w_copied.sem, 1)
                        act.wait_ge(chunk_ready.sem, chunk_ready.at(2 * r + 1))
                        act.activation(s_add[:, :, :].rearrange("p (t b) c -> p t b c", b=2), by_chunk(4),
                                       ACT.Copy).then_inc(sadd_copied.sem, 1)
                        act.wait_ge(chunk_ready.sem, chunk_ready.at(2 * r + 2))
                        act.activation(y_loc[:, :], slots[0], ACT.Copy).then_inc(yloc_copied.sem, 1)
                        if r + 1 < len(ROUNDS):
                            copy_natural(r + 1)
                    act.preload_act_table_set("natural_log_exp_and_others")
                    for hp in range(2):
                        act.wait_ge(fin_v.sem, fin_v.at(3 * hp + 1))
                        act.activation(f[1][:, :], f[0][:, :], ACT.Square).then_inc(fin_a.sem, 1)
                        act.wait_ge(fin_ps.sem, fin_ps.at(3 * hp + 3))
                        link(act.activation(f[2][:, :], slots[1], ACT.Ln, bias=small[:, EPS_LNX:EPS_LNX + 1],
                                            scale=1.0 / HEAD))
                        act.activation(f[3][:, :], f[2][:, :], ACT.Exp, scale=-0.5).then_inc(fin_a.sem, 1)

                @block.tensor
                def _(pe):
                    def low_rank(r):
                        hp, d = ROUNDS[r]
                        for i in range(2):
                            q = slice(64 * i + 32 * d, 64 * i + 32 * d + 32)
                            for a, e in spans:
                                mm = pe.matmul(slots[i][:, a:e], lora[q, hp * P:(hp + 1) * P], u[q, U_WA, a:e],
                                               start=True, stop=True)
                            mm.then_inc(lora_ready.sem, 1)

                    def turn(r, m):
                        hp = ROUNDS[r][0]
                        i, tt = m // NTT, m % NTT
                        if m == 0:
                            pe.wait_ge(features.sem, features.at(r + 1))
                            if r >= 1:
                                pe.wait_ge(sadd_copied.sem, sadd_copied.at(r))
                        if i >= 2 and tt == 0:
                            pe.wait_ge(nat_copied.sem, nat_copied.at(4 * r + i - 1))
                        t = slice(tt * P, (tt + 1) * P)
                        src = (ar[:, 0, t], bk_end[:, 0, t], bk_end[:, 1, t], u[:, V_OF + hp, t])[i]
                        mm = pe.transpose(slots[2 + i % 2][:, t], src, K_["ident"])
                        if tt == NTT - 1:
                            mm.then_inc(nat_turned.sem, 1)
                    pe.wait_ge(tanh_done.sem, tanh_done.at(2))
                    pe.wait_ge(lora_loaded.sem, lora_loaded.at(16))
                    low_rank(0)
                    for hp in range(2):
                        pe.wait_ge(rsq_ready.sem, rsq_ready.at(hp + 1))
                        for a, e in spans:
                            mm = pe.matmul(slots[2 + hp][:, a:e], K_["ones64"], bk[:, hp, a:e], start=True, stop=True)
                        mm.then_inc(sums_ready.sem, 1)
                    for m in range(4 * NTT):
                        turn(0, m)
                    for r, (hp, d) in enumerate(ROUNDS):
                        if r >= 1:
                            pe.wait_ge(round_done.sem, round_done.at(r))
                        for n in range(UNITS):
                            tt, j = n // 2, n % 2
                            t = slice(tt * P, (tt + 1) * P)
                            if n >= 4:
                                pe.wait_ge(wkv_masked.sem, wkv_masked.at(r * UNITS + n - 3))
                            for i in range(2):
                                mm = pe.matmul(ps[:, n % 4, i * 256:(i + 1) * 256], bk[hr(j), i, t],
                                               ar[hr(j), 0:2 + r % 2:1 + r % 2, t], start=True, stop=True)
                            mm.then_inc(wkv_scores.sem, 1)
                        pe.wait_ge(wkv_masked.sem, wkv_masked.at((r + 1) * UNITS))
                        pe.wait_ge(nat_copied.sem, nat_copied.at(4 * r + 4))
                        X0, M0, S0 = r * GROUPS * LEVELS, r * GROUPS * (LEVELS - 1), r * GROUPS * (LEVELS - 1)
                        for li in range(LEVELS):
                            for g in range(GROUPS):
                                q = GROUPS * li + g
                                if li >= 1:
                                    pe.wait_ge(x_ready.sem, x_ready.at(X0 + q - GROUPS + 1))
                                if q >= 2:
                                    if q - 2 < GROUPS:
                                        pe.wait_ge(x_ready.sem, x_ready.at(X0 + q - 1))
                                    else:
                                        pe.wait_ge(lx_masked.sem, lx_masked.at(M0 + q - 1 - GROUPS))
                                for i in range(UG):
                                    n = g * UG + i
                                    mm = pe.matmul(ps[:, 6 + q % 2, i * P:(i + 1) * P], sc[:, n, 0, :],
                                                   K_["ident"] if li == 0 else x_inv[:, n, :], start=True, stop=True)
                                mm.then_inc(lx_ready.sem, 1)
                            if li == 0:
                                if r + 1 < len(ROUNDS):
                                    low_rank(r + 1)
                                for n in range(UNITS):
                                    mm = pe.matmul(slots[2][:, n * 64:(n + 1) * 64], sc[:, n, 2, :],
                                                   v_rw[:, n // 2, hr(n % 2)], start=True, stop=True)
                                mm.then_inc(mv_ready.sem, 1)
                                continue
                            if li == 1:
                                if r + 1 < len(ROUNDS):
                                    pe.wait_ge(gate_tanh.sem, gate_tanh.at(2 * (r + 1) + 2))
                                pe.wait_ge(mv_copied.sem, mv_copied.at(r + 1))
                            for g in range(GROUPS):
                                pe.wait_ge(lx_masked.sem, lx_masked.at(M0 + GROUPS * (li - 1) + g + 1))
                                for i in range(UG):
                                    n = g * UG + i
                                    if li < LEVELS - 1:
                                        pe.matmul(ps[:, g, i * P:(i + 1) * P], xt_inv[:, n, :], lx[:, n, :], start=True,
                                                  stop=True)
                                    mm = pe.matmul(ps[:, 3 + g, i * P:(i + 1) * P], lx[:, n, :], xt_inv[:, n, :],
                                                   start=True, stop=True)
                                mm.then_inc(step_ready.sem, 1)
                        pe.wait_ge(x_ready.sem, x_ready.at(X0 + GROUPS * LEVELS))
                        for n in range(UNITS):
                            mm = pe.matmul(psf[:, 1024 + n * P:1024 + (n + 1) * P], xt_inv[:, n, :], a_mv[:, n, :],
                                           start=True, stop=True)
                            if n % UG == UG - 1:
                                mm.then_inc(w_ready.sem, 1)
                        pe.wait_ge(w_copied.sem, w_copied.at(GROUPS * (r + 1)))
                        for c in range(NCH):
                            tt, b = c // 2, c % 2
                            cc = slice(tt * CH, (tt + 1) * CH)
                            for j in range(2):
                                n = 2 * tt + j
                                pe.matmul(ps[hr(j), 2 + b, cc], neg_w[hr(b), n, 0:64], b_nat[hr(b), tt, hr(j)],
                                          start=True, stop=True)
                                pe.matmul(ps[hr(j), 4 + b, cc], b_nat[hr(b), tt, hr(j)], neg_w[hr(b), n, 64:128],
                                          start=True, stop=False)
                                mm = pe.matmul(ps[hr(j), 4 + b, cc], k_nat[hr(b), tt, hr(j)], v_rw[hr(b), tt, hr(j)],
                                               start=False, stop=True)
                        mm.then_inc(chunk_ready.sem, 1)
                        for n in range(UNITS):
                            tt, j = n // 2, n % 2
                            t = slice(tt * P, (tt + 1) * P)
                            pe.matmul(slots[3][hr(j), t], neg_w[:, n, 0:64], sc[:, n, 1, :], start=True, stop=True)
                            pe.matmul(slots[0][hr(j), t], neg_w[:, n, 64:128], sc[:, n, 1, :], start=True, stop=False)
                            mm = pe.matmul(slots[0][hr(j), t], v_rw[:, tt, hr(j)], sc[:, n, 3, :], start=False, stop=True)
                        mm.then_inc(chunk_ready.sem, 1)
                        pe.wait_ge(trans_ready.sem, trans_ready.at(r + 1))
                        for i, c in enumerate(ORDER[d]):
                            pe.wait_ge(state_ready.sem, state_ready.at(r * NCH + i + 1))
                            if i < NCH - 1:
                                for j in range(2):
                                    mm = pe.matmul(ps[hr(j), 2 + i % 2, 0:CH], trans[hr(j), c, :], state[hr(j), i % 2, :],
                                                   start=True, stop=True)
                                mm.then_inc(state_mm.sem, 1)
                            if i == 0:
                                pe.wait_ge(yloc_copied.sem, yloc_copied.at(r + 1))
                                pe.wait_ge(reff_ready.sem, reff_ready.at(r + 1))
                            for j in range(2):
                                mm = pe.matmul(slots[0][hr(j), c * CH:(c + 1) * CH], state[hr(j), i % 2, :],
                                               r_eff[hr(j), c * CH:(c + 1) * CH], start=True, stop=True)
                            if i == NCH - 1:
                                mm.then_inc(y_ready.sem, 1)
                        if r + 1 < len(ROUNDS):
                            for m in range(4 * NTT):
                                turn(r + 1, m)
                    for hp in range(2):
                        if hp == 0:
                            pe.wait_ge(round_done.sem, round_done.at(4))
                        else:
                            pe.wait_ge(fin_v.sem, fin_v.at(3 * hp))
                        for a, e in spans:
                            pe.matmul(slots[3][:, a:e], lora[0:64, 256 + hp * P:256 + (hp + 1) * P], u[0:64, U_GD, a:e],
                                      start=True, stop=True)
                        for a, e in spans:
                            mm = pe.matmul(slots[0][:, a:e], K_["ones64"], y_sum[hp][:, a:e], start=True, stop=True)
                        mm.then_inc(fin_ps.sem, 1)
                        pe.wait_ge(fin_v.sem, fin_v.at(3 * hp + 2))
                        for a, e in spans:
                            mm = pe.matmul(slots[2][:, a:e], K_["ones64"], f[4][:, a:e], start=True, stop=True)
                        mm.then_inc(fin_ps.sem, 1)
                        pe.wait_ge(fin_a.sem, fin_a.at(2 * hp + 1))
                        for a, e in spans:
                            mm = pe.matmul(slots[1][:, a:e], K_["ones64"], f[1][:, a:e], start=True, stop=True)
                        mm.then_inc(fin_ps.sem, 1)

                @block.vector
                def _(dve):
                    own = [0]

                    def link(ins):
                        own[0] += 1
                        ins.then_inc(v_step.sem, 1)
                        dve.wait_ge(v_step.sem, v_step.at(own[0]))
                    a, b = COLS["w0"][0], COLS["a0"][1]
                    link(dve.tensor_scalar(half_bias[:, :], cols[l][:, a:b], 0.5, None, ALU.mult))
                    a, b = COLS["ka"]
                    link(dve.tensor_scalar(ka_rest[:, :], cols[l][:, a:b], -1.0, 1.0, ALU.mult, ALU.add))
                    for hp in range(2):
                        dve.tensor_scalar(kk_n[:, hp, :], u[:, K_OF + hp, :], col("kk", hp), None,
                                          ALU.mult).then_inc(kk_raw.sem, 1)
                    dve.wait_ge(tanh_done.sem, tanh_done.at(1))
                    dve.tensor_scalar(u[0:64, U_GD, :], u[0:64, U_GD, :], 0.5, 0.5, ALU.mult,
                                      ALU.add).then_inc(tanh_done.sem, 1)

                    def scale_keys():
                        for hp in range(2):
                            dve.wait_ge(rsq_ready.sem, rsq_ready.at(2 + hp + 1))
                            dve.tensor_tensor(kk_n[:, hp, :], kk_n[:, hp, :], bk[:, hp, :], ALU.mult).then_inc(kk_raw.sem, 1)
                        dve.wait_ge(kk_raw.sem, kk_raw.at(4))
                    dve.wait_ge(scan_loaded.sem, scan_loaded.at(16))

                    gates(dve, link, 0)
                    feature_products(dve, link, 0, scale_keys)
                    dve.wait_ge(mix_loaded.sem, mix_loaded.at(16))

                    for r, (hp, d) in enumerate(ROUNDS):
                        for n in range(UNITS):
                            dve.wait_ge(wkv_scores.sem, wkv_scores.at(r * UNITS + n + 1))
                            dve.tensor_tensor(sc[:, n, :, :].rearrange("p a b -> p (a b)"), ps[:, n % 4, :],
                                              masks[:, d, 0:4, :].rearrange("p a b -> p (a b)"),
                                              ALU.mult).then_inc(wkv_masked.sem, 1)
                        dve.wait_ge(wkv_masked.sem, wkv_masked.at((r + 1) * UNITS))
                        M0, S0 = r * GROUPS * (LEVELS - 1), r * GROUPS * (LEVELS - 1)
                        eye = K_["ident"].rearrange("p (a b) -> p a b", a=1).broadcast_to([P, UG, P])

                        def mask(i):
                            return masks[:, d, i:i + 1, :].broadcast_to([P, UG, P])
                        for g in range(GROUPS):
                            gs = slice(g * UG, (g + 1) * UG)
                            dve.tensor_tensor(xt_inv[:, gs, :], sc[:, gs, 0, :], mask(5), ALU.mult)
                            dve.wait_ge(lx_ready.sem, lx_ready.at(r * GROUPS * LEVELS + g + 1))
                            link(dve.tensor_tensor(x_inv[:, gs, :], ps[:, 6 + g % 2, :].rearrange("p (a b) -> p a b", b=P),
                                                   mask(4), ALU.mult))
                            dve.tensor_tensor(xt_inv[:, gs, :], xt_inv[:, gs, :], eye, ALU.add)
                            dve.tensor_tensor(x_inv[:, gs, :], x_inv[:, gs, :], eye, ALU.add).then_inc(x_ready.sem, 1)
                        for li in range(1, LEVELS):
                            for g in range(GROUPS):
                                q = GROUPS * li + g
                                gs = slice(g * UG, (g + 1) * UG)
                                dve.wait_ge(lx_ready.sem, lx_ready.at(r * GROUPS * LEVELS + q + 1))
                                dve.tensor_tensor(lx[:, gs, :], ps[:, 6 + q % 2, :].rearrange("p (a b) -> p a b", b=P),
                                                  mask(5 + li), ALU.mult).then_inc(lx_masked.sem, 1)
                            if li == 1 and r + 1 < len(ROUNDS):
                                gates(dve, link, r + 1)
                            for g in range(GROUPS):
                                gs = slice(g * UG, (g + 1) * UG)
                                dve.wait_ge(step_ready.sem, step_ready.at(S0 + GROUPS * (li - 1) + g + 1))
                                dve.wait_ge(x_ready.sem, x_ready.at(r * GROUPS * LEVELS + GROUPS * (li - 1) + g + 1))
                                if li < LEVELS - 1:
                                    dve.tensor_tensor(x_inv[:, gs, :], x_inv[:, gs, :],
                                                      ps[:, g, :].rearrange("p (a b) -> p a b", b=P), ALU.subtract)
                                dve.tensor_tensor(xt_inv[:, gs, :], xt_inv[:, gs, :],
                                                  ps[:, 3 + g, :].rearrange("p (a b) -> p a b", b=P),
                                                  ALU.subtract).then_inc(x_ready.sem, 1)
                        dve.memset(state[:, 0, :], 0.0).then_inc(state_ready.sem, 1)
                        dve.wait_ge(w_ready.sem, w_ready.at(GROUPS * (r + 1)))
                        i2 = K_["ident2"][:, 0:CH].rearrange("p (a b) -> p a b", a=1).broadcast_to([P, NCH, CH])
                        cd = chunk_decay[:, r % 2, :].rearrange("p (a b) -> p a b", b=1).broadcast_to([P, NCH, CH])
                        dve.wait_ge(exps_out.sem, exps_out.at(5 * r + 5))
                        link(dve.tensor_tensor(trans[:, :, :], i2, cd, ALU.mult))
                        dve.wait_ge(chunk_ready.sem, chunk_ready.at(2 * r + 1))
                        dve.tensor_tensor(trans[:, :, :].rearrange("p (t b) c -> p t b c", b=2), by_chunk(2),
                                          trans[:, :, :].rearrange("p (t b) c -> p t b c", b=2),
                                          ALU.add).then_inc(trans_ready.sem, 1)
                        dve.wait_ge(chunk_ready.sem, chunk_ready.at(2 * r + 2))
                        dve.tensor_tensor(r_eff[:, :], slots[3], ar[:, 1 + r % 2, :], ALU.add).then_inc(reff_ready.sem, 1)
                        dve.wait_ge(sadd_copied.sem, sadd_copied.at(r + 1))
                        for i, c in enumerate(ORDER[d][:-1]):
                            dve.wait_ge(state_mm.sem, state_mm.at(r * (NCH - 1) + i + 1))
                            dve.tensor_tensor(state[:, (i + 1) % 2, :], ps[:, 2 + i % 2, 0:CH], s_add[:, c, :],
                                              ALU.add).then_inc(state_ready.sem, 1)
                        dve.wait_ge(y_ready.sem, y_ready.at(r + 1))
                        dve.wait_ge(yloc_copied.sem, yloc_copied.at(r + 1))
                        if d == 0:
                            dve.tensor_tensor(y_sum[hp][:, :], slots[0], y_loc[:, :], ALU.add).then_inc(round_done.sem, 1)
                        else:
                            link(dve.tensor_tensor(y_loc[:, :], slots[0], y_loc[:, :], ALU.add))
                            dve.tensor_tensor(y_sum[hp][:, :], y_sum[hp][:, :], y_loc[:, :],
                                              ALU.add).then_inc(round_done.sem, 1)
                        dve.wait_ge(round_done.sem, round_done.at(r + 1))

                    for hp in range(2):
                        if hp == 1:
                            dve.wait_ge(fin_v.sem, fin_v.at(3))
                        dve.wait_ge(fin_ps.sem, fin_ps.at(3 * hp + 1))
                        dve.scalar_tensor_tensor(out=f[0][:, :], in0=slots[0], scalar=-1.0 / HEAD, in1=y_sum[hp][:, :],
                                                 op0=ALU.mult, op1=ALU.add).then_inc(fin_v.sem, 1)
                        dve.scalar_tensor_tensor(out=f[4][:, :], in0=u[:, R_OF + hp, :], scalar=col("rk", hp),
                                                 in1=kd_sum[hp][:, :], op0=ALU.mult, op1=ALU.mult).then_inc(fin_v.sem, 1)
                        dve.wait_ge(fin_ps.sem, fin_ps.at(3 * hp + 2))
                        link(dve.tensor_tensor(f[5][:, :], slots[2], u[:, V_OF + hp, :], ALU.mult))
                        dve.wait_ge(fin_a.sem, fin_a.at(2 * hp + 2))
                        link(dve.scalar_tensor_tensor(out=f[0][:, :], in0=f[0][:, :], scalar=col("lg", hp),
                                                      in1=f[3][:, :], op0=ALU.mult, op1=ALU.mult))
                        link(dve.scalar_tensor_tensor(out=f[0][:, :], in0=f[0][:, :], scalar=col("lb", hp),
                                                      in1=f[5][:, :], op0=ALU.add, op1=ALU.add))
                        dve.tensor_tensor(mix[:, 2 + hp, :], f[0][:, :], slots[3], ALU.mult).then_inc(fin_v.sem, 1)
                    own_v[0] = own[0]

                @block.gpsimd
                def _(pool):
                    own = [0]

                    def link(ins):
                        own[0] += 1
                        ins.then_inc(p_step.sem, 1)
                        pool.wait_ge(p_step.sem, p_step.at(own[0]))
                    for r in range(1, len(ROUNDS)):
                        feature_products(pool, link, r)
                    own_p[0] = own[0]
            LINKS_A = 1 + 2 + 2
            for x, n in ((lora_loaded, 16), (scan_loaded, 16), (mix_loaded, 16), (a_step, LINKS_A), (v_step, own_v[0]), (p_step, own_p[0]),
                         (tanh_done, 2), (kk_raw, 4), (rsq_ready, 4), (sums_ready, 2), (lora_ready, 8), (gate_tanh, 8),
                         (gates_ready, 8), (exps_in, 4), (exps_out, 20), (features, 4), (nat_turned, 16), (nat_copied, 16),
                         (wkv_scores, 4 * UNITS), (wkv_masked, 4 * UNITS), (lx_ready, 4 * GROUPS * LEVELS),
                         (lx_masked, 4 * GROUPS * (LEVELS - 1)), (step_ready, 4 * GROUPS * (LEVELS - 1)),
                         (x_ready, 4 * GROUPS * LEVELS), (mv_ready, 4), (mv_copied, 4), (w_ready, 4 * GROUPS), (w_copied, 4 * GROUPS),
                         (chunk_ready, 8), (reff_ready, 4), (yloc_copied, 4), (trans_ready, 4), (sadd_copied, 4),
                         (state_ready, 4 * NCH), (state_mm, 4 * (NCH - 1)), (y_ready, 4), (round_done, 4),
                         (fin_ps, 6), (fin_v, 6), (fin_a, 4)):
                x.phase_end(n)
        own_v, own_p = [0], [0]

        def store():
            with nc.Block() as block:
                @block.sync
                def _(sp):
                    sp.dma_start(A["yT"], h[:, :, LAT]).then_inc(stored.sem, 16)
                    sp.wait_ge(stored.sem, 16)

        setup()
        for l in range(DEPTH):
            last = l == DEPTH - 1
            layer[0] = l
            first = l == 0
            ffn(l, 0, NT, [A["win"][l, s] for s in range(2)], (0, MOD_FIRST, (3, 2), (1, 0)) if first else None)
            in_proj(l)
            qkv(l)
            attention(l, SEQ if last else NT)
            rwkv(l, SEQ if last else NT, [A["wout"][l, s] for s in range(2)])
            out_proj(l, SEQ if last else NT, [A["wgu"][l, 1, s] for s in range(2)])
            ffn(l, 1, SEQ if last else NT, [] if last else [A["wgu"][l + 1, 0, s] for s in range(2)], None if last else (l + 1, 0, (3, 3), (3, 3)), more=not last)
        store()


def tiles_of(w, rows=P):
    r, c = w.shape[-2:]
    w = w.reshape(w.shape[:-2] + (r // P, P, c // P, P))
    n = w.ndim
    return np.ascontiguousarray(np.moveaxis(w, [n - 2, n - 3, n - 4, n - 1], [n - 4, n - 3, n - 2, n - 1]))


def blocks(w):
    t = tiles_of(w)
    return t.reshape(t.shape[:-2] + (-1,))


def layout(x, c, ctx, c_ctx, w_mod, b_mod, norm_ffn1, ffn1_w_gu, ffn1_w_down, norm_mix, w_in, w_out,
           mla_q_norm, mla_kv_norm, mla_w_uq, mla_w_ukv, mla_qn, mla_kn,
           rwkv_shift, rwkv_w0, rwkv_w2, rwkv_a0, rwkv_a2, rwkv_g2, rwkv_k_k, rwkv_k_a, rwkv_r_k,
           rwkv_lnx_g, rwkv_lnx_b, na_qn, na_kn, na_rpb, gqa_qn, gqa_kn,
           norm_ffn2, ffn2_w_gu, ffn2_w_down):
    L = DEPTH
    f = np.float32

    def colsof(v):
        return v.reshape(L, -1, P).transpose(0, 2, 1)
    A = {}
    xt = np.concatenate([x[0], ctx[0]], 0)
    A["xT"] = np.ascontiguousarray(xt.T.reshape(KD, P, NT).transpose(1, 0, 2))
    A["cT"] = np.ascontiguousarray(np.stack([c[0], c_ctx], 1).reshape(KD, P, 2).transpose(1, 0, 2)).reshape(P, 2 * KD)
    A["wmod"] = blocks(w_mod)
    gus = []
    for w in (ffn1_w_gu, ffn2_w_gu):
        g, up = blocks(w[:, :, :D_FF]), blocks(w[:, :, D_FF:])
        gus.append(np.stack([g, up], 2).reshape(L, 2 * NF, P, D_MODEL))
    A["wgu"] = np.stack(gus, 1)
    A["wdn"] = np.stack([blocks(w.reshape(L, 2, NFH * P, D_MODEL)) for w in (ffn1_w_down, ffn2_w_down)], 1)

    z96 = np.zeros((L, D_MODEL, 96), f)
    z64 = np.zeros((L, D_MODEL, 64), f)
    r0, n0 = 416, 1376
    g0 = n0 + 768
    gq = w_in[:, :, g0:g0 + 256].reshape(L, D_MODEL, 4, HEAD)[:, :, [0, 2, 1, 3]].reshape(L, D_MODEL, 256)
    w = np.concatenate([w_in[:, :, 0:416], z96, w_in[:, :, r0:r0 + 960], z64, w_in[:, :, n0:n0 + 512], gq,
                        w_in[:, :, g0 + 256:g0 + 384], w_in[:, :, n0 + 512:n0 + 768],
                        w_in[:, :, g0 + 384:g0 + 512]], 2)
    A["win"] = blocks(w)
    A["wout"] = blocks(w_out)

    sh = np.concatenate([rwkv_shift, np.zeros((L, 2, 64), f)], 2)
    two = lambda v: np.concatenate([v, v], 1)
    pad96 = lambda v: np.concatenate([v, np.zeros((L, 32), f)], 1)
    parts = {"n1": norm_ffn1, "nm": norm_mix, "n2": norm_ffn2, "bmod": b_mod, "mq": mla_q_norm, "mkv": mla_kv_norm,
             "mu0": sh[:, 0], "mu1": sh[:, 1], "w0": rwkv_w0.reshape(L, -1), "a0": rwkv_a0.reshape(L, -1),
             "kk": rwkv_k_k, "ka": rwkv_k_a, "rk": rwkv_r_k.reshape(L, -1), "lg": rwkv_lnx_g, "lb": rwkv_lnx_b,
             "nq": two(na_qn), "nk": two(na_kn), "gq": two(gqa_qn), "gk": two(gqa_kn), "mqn": pad96(mla_qn),
             "mkn": pad96(mla_kn)}
    A["cols"] = np.ascontiguousarray(np.concatenate([colsof(parts[n]) for n in COLS], 2).transpose(1, 0, 2))

    uq = mla_w_uq.reshape(L, 2, P, 4 * MLA_D).transpose(0, 2, 1, 3)
    ukv = mla_w_ukv.reshape(L, P, 4, 128)
    uk = np.concatenate([ukv[..., :64], np.zeros((L, P, 4, 32), f)], 3).reshape(L, P, 4 * MLA_D)
    uv = ukv[..., 64:].reshape(L, P, 256)
    A["mla"] = np.ascontiguousarray(np.concatenate([uq.reshape(L, P, -1), uk, uv], 2))
    A["lora"] = np.ascontiguousarray(np.concatenate([
        np.concatenate([rwkv_w2.reshape(L, 64, 256), rwkv_a2.reshape(L, 64, 256)], 1),
        np.concatenate([rwkv_g2, np.zeros((L, 64, 256), f)], 1)], 2))

    B = np.full((L, P, 4, 14, GRID_W), MASKED, f)
    cq = np.arange(GRID_W)
    c0 = np.clip(cq - 8, 0, GRID_W - 16)
    for ro in range(2):
        for q in range(GRID_W):
            ks = np.arange(c0[q], c0[q] + 16)
            dr = np.arange(1, 15) - ro
            B[:, ro * 64 + q, :, :, ks] = na_rpb[:, :, dr][:, :, :, ks - q + 15].transpose(3, 0, 1, 2)
    A["bias"] = B.reshape(L, P, 4, 14 * GRID_W)
    A.update(constants())
    return A


def constants():
    f = np.float32
    eye = np.eye(P, dtype=f)
    one64 = np.kron(np.eye(2), np.ones((64, 64))).astype(f)

    def rot(widths, offset=0):
        R = np.zeros((P, P))
        at = offset
        for w in widths:
            hf = w // 2
            for j in range(hf):
                R[at + j, at + hf + j] = -1
                R[at + hf + j, at + j] = 1
            at += w
        return np.ascontiguousarray(R.T).astype(f)
    sel = np.zeros((P, P), f)
    sel[0:32, 64:96] = np.eye(32)
    ident2 = np.zeros((P, P), f)
    ident2[:, 0:64] = np.concatenate([np.eye(64)] * 2, 0)
    mats = {"ident": eye, "ones": np.ones((P, P), f), "ones64": one64, "rot_g": rot([32] * 4),
            "rot_m": rot([16, 16], 64), "sel_kr": sel, "ident2": ident2}
    A = {"consts": np.ascontiguousarray(np.stack([mats[n] for n in CONSTS], 1))}
    small = np.zeros((P, 16), f)
    small[:, 0:5] = np.array([1e-6, np.log(HEAD ** -0.5), np.log(MLA_D ** -0.5), 1e-12, 64e-5])
    A["small"] = small

    t = np.arange(SEQ)
    pos = {"row": (t // GRID_W).astype(f), "col": (t % GRID_W).astype(f)}

    def table(axes):
        c, s = [], []
        for axis, w in axes:
            hf = w // 2
            inv = (f(10000.0) ** (-np.arange(hf, dtype=f) / f(hf))).astype(f)
            ang = (pos[axis][None, :] * inv[:, None]).astype(f)
            c += [np.cos(ang)] * 2
            s += [np.sin(ang)] * 2
        return np.concatenate(c, 0).astype(f), np.concatenate(s, 0).astype(f)
    cg, sg = table([("row", 32), ("col", 32)] * 2)
    cm, sm = table([("row", 16), ("col", 16)])
    o, z = np.ones((64, SEQ), f), np.zeros((64, SEQ), f)
    pad = np.zeros((32, SEQ), f)
    A["rope"] = np.ascontiguousarray(np.stack([cg, sg, np.concatenate([o, cm, pad]), np.concatenate([z, sm, pad])], 1))

    i = np.arange(P)
    same = (i[:, None] // CH) == (i[None, :] // CH)
    scan = np.ones((P, NT), f)
    scan[:, ::CH] = 0
    A["scan"] = scan
    M = []
    for d in range(2):
        before = (i[:, None] < i[None, :]) if d == 0 else (i[:, None] > i[None, :])
        strict, incl = same & before, same & (before | (i[:, None] == i[None, :]))
        lv = []
        for m in (1, 2, 4, 8, 16, 32):
            blk = (i[:, None] // (2 * m)) == (i[None, :] // (2 * m))
            hi_, lo_ = (i // m) % 2 == 1, (i // m) % 2 == 0
            q = blk & (hi_[:, None] & lo_[None, :] if d == 0 else lo_[:, None] & hi_[None, :])
            lv.append(q)
        M.append(np.stack([strict, incl, strict, incl, -1.0 * lv[0], -1.0 * lv[0].T] + lv[1:]))
    A["masks"] = np.ascontiguousarray(np.stack(M).astype(f).transpose(2, 0, 1, 3))
    return A


def kernel(**inputs):
    import concourse.bacc as bacc
    from concourse.bass_utils import run_bass_kernel_spmd

    arrays = layout(**{k: np.asarray(v) for k, v in inputs.items()})
    nc = bacc.Bacc("TRN2", target_bir_lowering=False, num_devices=1)
    A = {n: nc.dram_tensor(n, a.shape, mybir.dt.from_np(a.dtype), kind="ExternalInput").ap()
         for n, a in arrays.items()}
    A["yT"] = nc.dram_tensor("yT", (P, KD, SEQ), F32, kind="ExternalOutput").ap()
    build_trunk(nc, A)
    r = run_bass_kernel_spmd(nc, [arrays], core_ids=[0])
    y = r.results[0]["yT"]
    return np.ascontiguousarray(y.transpose(2, 1, 0)).reshape(1, SEQ, D_MODEL)
```
